# Optimizing a Trainium2 kernel written in Bass

```python
import math
import jax, jax.numpy as jnp
from jax import lax
import numpy as np

D_MODEL = 1024
BATCH = 1
SEQ = 512
DEPTH = 2
DEC_BATCH = 8
DEC_SEQ = 1
PAST_LEN = 2048
PAGE_SIZE = 128

N_EVEN = (DEPTH + 1) // 2
N_ODD = DEPTH // 2
MIX_WIDTH = D_MODEL
CONV_CH = MIX_WIDTH // 2
CONV_WIDTH = 31
NSA_HEADS = 8
NSA_KV_HEADS = 2
NSA_GROUP = NSA_HEADS // NSA_KV_HEADS
NSA_HD = (MIX_WIDTH - CONV_CH) // NSA_HEADS
CMP_BLOCK = 32
SEL_BLOCK = 64
SEL_RATIO = SEL_BLOCK // CMP_BLOCK
TOP_N = 16
WINDOW = 512
Q_BLOCK = 128
FORCE_SCORE = 1.0e4
NUM_BUCKETS = 32
MAX_DISTANCE = 1024
MLSTM_HEADS = 4
MLSTM_DK = D_MODEL // MLSTM_HEADS
MLSTM_DV = D_MODEL // MLSTM_HEADS
MLSTM_CHUNK = 64
MEM_TOKENS = 256
X_HEADS = 4
X_HD = D_MODEL // X_HEADS
D_FF = 2816
N_EXPERTS = 8
TOP_K = 2
D_FF_EXPERT = D_FF // TOP_K
RMS_EPS = 1e-6
LN_EPS = 1e-5
NEG = -1e30
IN_EVEN = 2 * CONV_CH + NSA_HEADS * NSA_HD + 6 * NSA_KV_HEADS * NSA_HD + 3 * NSA_HEADS
IN_ODD = 2 * MLSTM_HEADS * MLSTM_DK + 2 * MLSTM_HEADS * MLSTM_DV + 2 * MLSTM_HEADS

kernel_name = "hybrid_conformer_nsa_mlstm_moe_decode_step"

def rms_norm(x, g):
    xf = x.astype(jnp.float32)
    y = xf * lax.rsqrt(jnp.mean(xf * xf, -1, keepdims=True) + RMS_EPS)
    return (y * g.astype(jnp.float32)).astype(x.dtype)

def rel_bucket(dist):
    n = jnp.maximum(dist, 0)
    max_exact = NUM_BUCKETS // 2
    nf = jnp.maximum(n, 1).astype(jnp.float32)
    large = max_exact + (jnp.log(nf / max_exact) / math.log(MAX_DISTANCE / max_exact)
                         * (NUM_BUCKETS - max_exact)).astype(jnp.int32)
    large = jnp.minimum(large, NUM_BUCKETS - 1)
    return jnp.where(n < max_exact, n, large)

def bias_qk(rel_bias, dist):
    b = rel_bias[rel_bucket(dist)].astype(jnp.float32)
    b = b.reshape(dist.shape + (NSA_KV_HEADS, NSA_GROUP))
    return jnp.transpose(b, (2, 3, 0, 1))

def masked_softmax(s, mask):
    s = jnp.where(mask, s, NEG)
    e = jnp.where(mask, jnp.exp(s - jnp.max(s, -1, keepdims=True)), 0.0)
    den = jnp.sum(e, -1, keepdims=True)
    return e / jnp.where(den > 0, den, 1.0)

def compress_kv(x, pe, w):
    B, T = x.shape[:2]
    nc = T // CMP_BLOCK
    blk = x[:, :nc * CMP_BLOCK].reshape(B, nc, CMP_BLOCK, NSA_KV_HEADS, NSA_HD) + pe[None, None, :, None, :]
    return jnp.einsum('bcjkd,jde->bcke', blk, w)

def nsa_attend(q, qpos, kc, vc, cend, ks_b, vs_b, kw, vw, kwpos, gates, rel_bias):
    f32 = jnp.float32
    B, Q = q.shape[:2]
    qg = q.reshape(B, Q, NSA_KV_HEADS, NSA_GROUP, NSA_HD)
    dist_c = qpos[:, None] - cend[None, :]
    s_c = jnp.einsum('bqkgd,bckd->bkgqc', qg, kc).astype(f32) + bias_qk(rel_bias, dist_c)
    p_c = masked_softmax(s_c, dist_c >= 0)
    o_c = jnp.einsum('bkgqc,bckd->bqkgd', p_c.astype(vc.dtype), vc)
    nsb = ks_b.shape[1]
    nc = kc.shape[1]
    n_sel = min(TOP_N, nsb)
    imp = jnp.sum(p_c, axis=2)
    imp = jnp.pad(imp, ((0, 0), (0, 0), (0, 0), (0, nsb * SEL_RATIO - nc)))
    imp = imp.reshape(B, NSA_KV_HEADS, Q, nsb, SEL_RATIO).sum(-1)
    blk = jnp.arange(nsb)[None, :]
    cur = (qpos // SEL_BLOCK)[:, None]
    forced = (blk == 0) | (blk == cur) | (blk == cur - 1)
    score = jnp.where(forced, FORCE_SCORE, jnp.where(blk <= cur, imp, -1.0))
    top_v, top_i = lax.top_k(score, n_sel)
    b_ix = jnp.arange(B)[:, None, None, None]
    h_ix = jnp.arange(NSA_KV_HEADS)[None, :, None, None]
    ks_t = jnp.transpose(ks_b, (0, 3, 1, 2, 4))
    vs_t = jnp.transpose(vs_b, (0, 3, 1, 2, 4))
    k_g = ks_t[b_ix, h_ix, top_i]
    v_g = vs_t[b_ix, h_ix, top_i]
    kpos = top_i[..., None] * SEL_BLOCK + jnp.arange(SEL_BLOCK)
    dist_s = qpos[None, None, :, None, None] - kpos
    mask_s = (dist_s >= 0) & (top_v >= 0)[..., None]
    tbl = jnp.transpose(rel_bias.reshape(NUM_BUCKETS, NSA_KV_HEADS, NSA_GROUP), (1, 0, 2))
    bias_s = tbl[jnp.arange(NSA_KV_HEADS)[None, :, None, None, None], rel_bucket(dist_s)]
    bias_s = jnp.moveaxis(bias_s, -1, 2).astype(f32)
    s_s = jnp.einsum('bqkgd,bkqnsd->bkgqns', qg, k_g).astype(f32) + bias_s
    m = n_sel * SEL_BLOCK
    p_s = masked_softmax(s_s.reshape(B, NSA_KV_HEADS, NSA_GROUP, Q, m),
                         mask_s.reshape(B, NSA_KV_HEADS, 1, Q, m))
    o_s = jnp.einsum('bkgqm,bkqmd->bqkgd', p_s.astype(v_g.dtype),
                     v_g.reshape(B, NSA_KV_HEADS, Q, m, NSA_HD))
    dist_w = qpos[:, None] - kwpos[None, :]
    mask_w = (dist_w >= 0) & (dist_w < WINDOW) & (kwpos >= 0)[None, :]
    s_w = jnp.einsum('bqkgd,bwkd->bkgqw', qg, kw).astype(f32) + bias_qk(rel_bias, dist_w)
    p_w = masked_softmax(s_w, mask_w)
    o_w = jnp.einsum('bkgqw,bwkd->bqkgd', p_w.astype(vw.dtype), vw)
    g = gates.reshape(B, Q, NSA_KV_HEADS, NSA_GROUP, 3)
    out = g[..., 0:1] * o_c + g[..., 1:2] * o_s + g[..., 2:3] * o_w
    return out.reshape(B, Q, NSA_HEADS * NSA_HD)

def nsa_prompt(q, kv, gates, pe, wcmp, rel_bias):
    B, S = q.shape[:2]
    kc = compress_kv(kv[:, :, 0], pe[0], wcmp[0])
    vc = compress_kv(kv[:, :, 1], pe[1], wcmp[1])
    cend = jnp.arange(kc.shape[1]) * CMP_BLOCK + (CMP_BLOCK - 1)
    nsb = S // SEL_BLOCK
    ks_b = kv[:, :, 2].reshape(B, nsb, SEL_BLOCK, NSA_KV_HEADS, NSA_HD)
    vs_b = kv[:, :, 3].reshape(B, nsb, SEL_BLOCK, NSA_KV_HEADS, NSA_HD)
    nq = S // Q_BLOCK
    wk = WINDOW + Q_BLOCK
    widx = jnp.arange(nq)[:, None] * Q_BLOCK + jnp.arange(wk)[None, :]
    wp = jnp.pad(kv[:, :, 4:6], ((0, 0), (WINDOW, 0), (0, 0), (0, 0), (0, 0)))
    wblk = jnp.moveaxis(wp[:, widx], 1, 0)
    kwpos = widx - WINDOW
    qb = jnp.moveaxis(q.reshape(B, nq, Q_BLOCK, NSA_HEADS, NSA_HD), 1, 0)
    gb = jnp.moveaxis(gates.reshape(B, nq, Q_BLOCK, NSA_HEADS, 3), 1, 0)
    qpos = jnp.arange(S).reshape(nq, Q_BLOCK)

    def one_block(args):
        qi, qp, wi, kp, gi = args
        return nsa_attend(qi, qp, kc, vc, cend, ks_b, vs_b, wi[:, :, 0], wi[:, :, 1], kp, gi, rel_bias)

    out = lax.map(one_block, (qb, qpos, wblk, kwpos, gb))
    return jnp.moveaxis(out, 0, 1).reshape(B, S, NSA_HEADS * NSA_HD)

def nsa_sample(q, kv, gates, past_rows, win_buf, pe, wcmp, rel_bias):
    Bd, Td = q.shape[:2]
    past = past_rows.shape[1]
    wb = win_buf.shape[1]
    rows = jnp.concatenate([past_rows.astype(kv.dtype), kv[:, :, :4]], 1)
    T = past + Td
    kc = compress_kv(rows[:, :, 0], pe[0], wcmp[0])
    vc = compress_kv(rows[:, :, 1], pe[1], wcmp[1])
    cend = jnp.arange(kc.shape[1]) * CMP_BLOCK + (CMP_BLOCK - 1)
    nsb = -(-T // SEL_BLOCK)
    sel = jnp.pad(rows[:, :, 2:4], ((0, 0), (0, nsb * SEL_BLOCK - T), (0, 0), (0, 0), (0, 0)))
    sel = sel.reshape(Bd, nsb, SEL_BLOCK, 2, NSA_KV_HEADS, NSA_HD)
    wall = jnp.concatenate([win_buf.astype(kv.dtype), kv[:, :, 4:6]], 1)
    kwpos = past - wb + jnp.arange(wb + Td)
    qpos = past + jnp.arange(Td)
    out = nsa_attend(q, qpos, kc, vc, cend, sel[:, :, :, 0], sel[:, :, :, 1],
                     wall[:, :, 0], wall[:, :, 1], kwpos, gates, rel_bias)
    return out, wall[:, -wb:]

def split_even(u):
    B, T = u.shape[:2]
    glu = u[..., :CONV_CH] * jax.nn.sigmoid(u[..., CONV_CH:2 * CONV_CH])
    o = 2 * CONV_CH
    q = u[..., o:o + NSA_HEADS * NSA_HD].reshape(B, T, NSA_HEADS, NSA_HD) * (NSA_HD ** -0.5)
    o += NSA_HEADS * NSA_HD
    kv = u[..., o:o + 6 * NSA_KV_HEADS * NSA_HD].reshape(B, T, 6, NSA_KV_HEADS, NSA_HD)
    o += 6 * NSA_KV_HEADS * NSA_HD
    gates = jax.nn.sigmoid(u[..., o:].reshape(B, T, NSA_HEADS, 3))
    return glu, q, kv, gates

def conformer_conv(xe, w, b, g, beta):
    y = lax.conv_general_dilated(xe, w[:, None, :].astype(xe.dtype), window_strides=(1,), padding='VALID',
                                 dimension_numbers=('NWC', 'WIO', 'NWC'), feature_group_count=CONV_CH) + b
    yf = y.astype(jnp.float32)
    mu = jnp.mean(yf, -1, keepdims=True)
    var = jnp.mean(jnp.square(yf - mu), -1, keepdims=True)
    yn = (yf - mu) * lax.rsqrt(var + LN_EPS) * g + beta
    return jax.nn.silu(yn).astype(xe.dtype)

def split_odd(u, b_i, b_f):
    f32 = jnp.float32
    B, T = u.shape[:2]
    hq = MLSTM_HEADS * MLSTM_DK
    hv = MLSTM_HEADS * MLSTM_DV

    def heads(a, d):
        return jnp.transpose(a.reshape(B, T, MLSTM_HEADS, d), (0, 2, 1, 3)).astype(f32)

    q = heads(u[..., :hq], MLSTM_DK)
    k = heads(u[..., hq:2 * hq], MLSTM_DK) * (MLSTM_DK ** -0.5)
    v = heads(u[..., 2 * hq:2 * hq + hv], MLSTM_DV)
    og = jax.nn.sigmoid(u[..., 2 * hq + hv:2 * hq + 2 * hv].astype(f32))
    gi = u[..., 2 * hq + 2 * hv:].astype(f32).reshape(B, T, 2, MLSTM_HEADS)
    ig = jnp.transpose(gi[:, :, 0] + b_i, (0, 2, 1))
    lf = jnp.transpose(jax.nn.log_sigmoid(gi[:, :, 1] + b_f), (0, 2, 1))
    return q, k, v, og, ig, lf

def mlstm_chunk(carry, inp):
    C, n, m = carry
    q, k, v, ig, lf = inp
    L = q.shape[2]
    b = jnp.cumsum(lf, axis=-1)
    causal = jnp.tril(jnp.ones((L, L), dtype=bool))
    dmat = jnp.where(causal, b[..., :, None] - b[..., None, :] + ig[..., None, :], NEG)
    inter = b + m[..., None]
    mt = jnp.maximum(inter, jnp.max(dmat, -1))
    wm = jnp.exp(dmat - mt[..., None])
    a = jnp.exp(inter - mt)
    wqk = wm * jnp.einsum('bhtd,bhsd->bhts', q, k)
    num = a[..., None] * jnp.einsum('bhvd,bhtd->bhtv', C, q) + jnp.einsum('bhts,bhsv->bhtv', wqk, v)
    den = a * jnp.einsum('bhd,bhtd->bht', n, q) + jnp.sum(wqk, -1)
    h = num / jnp.maximum(jnp.abs(den), jnp.exp(-mt))[..., None]
    m_new = mt[..., -1]
    a_end = jnp.exp(b[..., -1] + m - m_new)
    w_s = jnp.exp(b[..., -1:] - b + ig - m_new[..., None])
    C_new = a_end[..., None, None] * C + jnp.einsum('bhsv,bhsd->bhvd', v * w_s[..., None], k)
    n_new = a_end[..., None] * n + jnp.einsum('bhs,bhsd->bhd', w_s, k)
    return (C_new, n_new, m_new), h

def mlstm_prompt(q, k, v, ig, lf):
    B, H, S, _ = q.shape
    nch = S // MLSTM_CHUNK

    def to_chunks(a):
        return jnp.moveaxis(a.reshape(a.shape[:2] + (nch, MLSTM_CHUNK) + a.shape[3:]), 2, 0)

    init = (jnp.zeros((B, H, MLSTM_DV, MLSTM_DK), jnp.float32), jnp.zeros((B, H, MLSTM_DK), jnp.float32),
            jnp.full((B, H), NEG, jnp.float32))
    carry, h = lax.scan(mlstm_chunk, init, (to_chunks(q), to_chunks(k), to_chunks(v), to_chunks(ig), to_chunks(lf)))
    h = jnp.moveaxis(h, 0, 2).reshape(B, H, S, MLSTM_DV)
    return h, carry

def mlstm_out(h, og, gain, w_out, dtype):
    B, H, T, _ = h.shape
    hn = h * lax.rsqrt(jnp.mean(h * h, -1, keepdims=True) + RMS_EPS)
    hn = jnp.transpose(hn, (0, 2, 1, 3)).reshape(B, T, H * MLSTM_DV) * gain.astype(jnp.float32) * og
    return hn.astype(dtype) @ w_out

def cross_attn(h, kv, wq, wo):
    B, T = h.shape[:2]
    q = (h @ wq).reshape(B, T, X_HEADS, X_HD) * (X_HD ** -0.5)
    s = jnp.einsum('bqhd,bmhd->bhqm', q, kv[:, :, 0].astype(q.dtype)).astype(jnp.float32)
    p = jax.nn.softmax(s, axis=-1).astype(q.dtype)
    o = jnp.einsum('bhqm,bmhd->bqhd', p, kv[:, :, 1].astype(q.dtype)).reshape(B, T, X_HEADS * X_HD)
    return o @ wo

def swiglu(h, w_gu, w_dn):
    g, u = jnp.split(h @ w_gu, 2, axis=-1)
    return (jax.nn.silu(g) * u) @ w_dn

def moe_ffn(h, w_r, b_r, w_gu, w_dn):
    f32 = jnp.float32
    shp = h.shape
    hf = h.reshape(-1, shp[-1])
    logits = (hf @ w_r).astype(f32) + b_r.astype(f32)
    top_v, top_i = lax.top_k(logits, TOP_K)
    wts = jax.nn.softmax(top_v, axis=-1)
    comb = jnp.sum(jax.nn.one_hot(top_i, N_EXPERTS, dtype=f32) * wts[..., None], axis=1)
    y = jnp.zeros(hf.shape, f32)
    for ex in range(N_EXPERTS):
        g, u = jnp.split(hf @ w_gu[ex], 2, axis=-1)
        y = y + comb[:, ex:ex + 1] * ((jax.nn.silu(g) * u) @ w_dn[ex]).astype(f32)
    return y.astype(h.dtype).reshape(shp)

def setup_inputs(seed: int = 0) -> dict:
    key = jax.random.key(seed)
    ks = iter(jax.random.split(key, 64))

    def nrm(shape, scale):
        return scale * jax.random.normal(next(ks), shape, jnp.float32)

    def gain(shape):
        return 1.0 + nrm(shape, 0.01)

    n_pages = PAST_LEN // PAGE_SIZE
    n_used = DEC_BATCH * n_pages
    n_pool = n_used + (n_used + 3) // 4
    wb = min(WINDOW, PAST_LEN)
    D = D_MODEL
    inp = {}
    inp['x_prompt'] = nrm((BATCH, SEQ, D), 1.0)
    inp['x_sample'] = nrm((DEC_BATCH, DEC_SEQ, D), 1.0)
    inp['mem_prompt'] = nrm((BATCH, MEM_TOKENS, D), 1.0)
    inp['cache_conv'] = nrm((N_EVEN, DEC_BATCH, CONV_WIDTH - 1, CONV_CH), 0.5)
    inp['cache_nsa_pages'] = nrm((N_EVEN, n_pool, PAGE_SIZE, 4, NSA_KV_HEADS, NSA_HD), 1.0)
    inp['cache_nsa_window'] = nrm((N_EVEN, DEC_BATCH, wb, 2, NSA_KV_HEADS, NSA_HD), 1.0)
    inp['state_mlstm_c'] = nrm((N_ODD, DEC_BATCH, MLSTM_HEADS, MLSTM_DV, MLSTM_DK), 0.1)
    inp['state_mlstm_n'] = nrm((N_ODD, DEC_BATCH, MLSTM_HEADS, MLSTM_DK), 0.1)
    inp['state_mlstm_m'] = nrm((N_ODD, DEC_BATCH, MLSTM_HEADS), 1.0)
    inp['cache_mem_kv'] = nrm((DEPTH, DEC_BATCH, MEM_TOKENS, 2, X_HEADS, X_HD), 1.0)
    inp['page_table'] = jax.random.permutation(next(ks), n_pool)[:n_used].reshape(DEC_BATCH, n_pages).astype(jnp.int32)
    inp['rel_bias'] = nrm((NUM_BUCKETS, NSA_HEADS), 0.1)
    inp['norm_mix'] = gain((DEPTH, D))
    inp['norm_xattn'] = gain((DEPTH, D))
    inp['norm_mem'] = gain((DEPTH, D))
    inp['norm_ffn'] = gain((DEPTH, D))
    inp['norm_final'] = gain((D,))
    inp['w_in_even'] = nrm((N_EVEN, D, IN_EVEN), D ** -0.5)
    inp['w_out_even'] = nrm((N_EVEN, MIX_WIDTH, D), MIX_WIDTH ** -0.5)
    inp['conv_w'] = nrm((N_EVEN, CONV_WIDTH, CONV_CH), CONV_WIDTH ** -0.5)
    inp['conv_b'] = nrm((N_EVEN, CONV_CH), 0.01)
    inp['conv_ln_g'] = gain((N_EVEN, CONV_CH))
    inp['conv_ln_b'] = nrm((N_EVEN, CONV_CH), 0.01)
    inp['nsa_cmp_pe'] = nrm((N_EVEN, 2, CMP_BLOCK, NSA_HD), 0.1)
    inp['nsa_cmp_w'] = nrm((N_EVEN, 2, CMP_BLOCK, NSA_HD, NSA_HD), (CMP_BLOCK * NSA_HD) ** -0.5)
    inp['w_in_odd'] = nrm((N_ODD, D, IN_ODD), D ** -0.5)
    inp['mlstm_b_i'] = nrm((N_ODD, MLSTM_HEADS), 0.1)
    inp['mlstm_b_f'] = jnp.linspace(3.0, 6.0, MLSTM_HEADS)[None, :] + nrm((N_ODD, MLSTM_HEADS), 0.01)
    inp['mlstm_norm'] = gain((N_ODD, MLSTM_HEADS * MLSTM_DV))
    inp['w_out_odd'] = nrm((N_ODD, MLSTM_HEADS * MLSTM_DV, D), (MLSTM_HEADS * MLSTM_DV) ** -0.5)
    inp['xattn_wq'] = nrm((DEPTH, D, X_HEADS * X_HD), D ** -0.5)
    inp['xattn_wkv'] = nrm((DEPTH, D, 2 * X_HEADS * X_HD), D ** -0.5)
    inp['xattn_wo'] = nrm((DEPTH, X_HEADS * X_HD, D), (X_HEADS * X_HD) ** -0.5)
    inp['ffn_w_gu'] = nrm((N_EVEN, D, 2 * D_FF), D ** -0.5)
    inp['ffn_w_dn'] = nrm((N_EVEN, D_FF, D), D_FF ** -0.5)
    inp['router_w'] = nrm((N_ODD, D, N_EXPERTS), D ** -0.5)
    inp['router_b'] = nrm((N_ODD, N_EXPERTS), 0.01)
    inp['expert_w_gu'] = nrm((N_ODD, N_EXPERTS, D, 2 * D_FF_EXPERT), D ** -0.5)
    inp['expert_w_dn'] = nrm((N_ODD, N_EXPERTS, D_FF_EXPERT, D), D_FF_EXPERT ** -0.5)
    return inp

def reference(x_prompt, x_sample, mem_prompt, cache_conv, cache_nsa_pages, cache_nsa_window,
              state_mlstm_c, state_mlstm_n, state_mlstm_m, cache_mem_kv, page_table, rel_bias,
              norm_mix, norm_xattn, norm_mem, norm_ffn, norm_final, w_in_even, w_out_even,
              conv_w, conv_b, conv_ln_g, conv_ln_b, nsa_cmp_pe, nsa_cmp_w, w_in_odd, mlstm_b_i,
              mlstm_b_f, mlstm_norm, w_out_odd, xattn_wq, xattn_wkv, xattn_wo, ffn_w_gu, ffn_w_dn,
              router_w, router_b, expert_w_gu, expert_w_dn):
    B, S, _ = x_prompt.shape
    Bd = x_sample.shape[0]
    past = page_table.shape[1] * PAGE_SIZE
    wb = cache_nsa_window.shape[2]
    xp, xs = x_prompt, x_sample
    conv_p, conv_s, nsa_p, nsa_s, win_p, win_s = [], [], [], [], [], []
    mc_p, mc_s, mn_p, mn_s, mm_p, mm_s, memkv_p = [], [], [], [], [], [], []
    for l in range(DEPTH):
        li = l // 2
        if l % 2 == 0:
            glu, q, kv, gates = split_even(rms_norm(xp, norm_mix[l]) @ w_in_even[li])
            conv_ext = jnp.concatenate([jnp.zeros((B, CONV_WIDTH - 1, CONV_CH), glu.dtype), glu], 1)
            a_out = conformer_conv(conv_ext, conv_w[li], conv_b[li], conv_ln_g[li], conv_ln_b[li])
            b_out = nsa_prompt(q, kv, gates, nsa_cmp_pe[li], nsa_cmp_w[li], rel_bias)
            xp = xp + jnp.concatenate([a_out, b_out], -1) @ w_out_even[li]
            conv_p.append(conv_ext[:, -(CONV_WIDTH - 1):])
            nsa_p.append(kv[:, :, :4])
            win = kv[:, -min(wb, S):, 4:6]
            if win.shape[1] < wb:
                win = jnp.pad(win, ((0, 0), (wb - win.shape[1], 0), (0, 0), (0, 0), (0, 0)))
            win_p.append(win)
            glu, q, kv, gates = split_even(rms_norm(xs, norm_mix[l]) @ w_in_even[li])
            conv_ext = jnp.concatenate([cache_conv[li].astype(glu.dtype), glu], 1)
            a_out = conformer_conv(conv_ext, conv_w[li], conv_b[li], conv_ln_g[li], conv_ln_b[li])
            past_rows = cache_nsa_pages[li][page_table].reshape(Bd, past, 4, NSA_KV_HEADS, NSA_HD)
            b_out, win = nsa_sample(q, kv, gates, past_rows, cache_nsa_window[li], nsa_cmp_pe[li],
                                    nsa_cmp_w[li], rel_bias)
            xs = xs + jnp.concatenate([a_out, b_out], -1) @ w_out_even[li]
            conv_s.append(conv_ext[:, -(CONV_WIDTH - 1):])
            nsa_s.append(kv[:, :, :4])
            win_s.append(win)
        else:
            q, k, v, og, ig, lf = split_odd(rms_norm(xp, norm_mix[l]) @ w_in_odd[li], mlstm_b_i[li], mlstm_b_f[li])
            h, (c_new, n_new, m_new) = mlstm_prompt(q, k, v, ig, lf)
            xp = xp + mlstm_out(h, og, mlstm_norm[li], w_out_odd[li], xp.dtype)
            mc_p.append(c_new)
            mn_p.append(n_new)
            mm_p.append(m_new)
            q, k, v, og, ig, lf = split_odd(rms_norm(xs, norm_mix[l]) @ w_in_odd[li], mlstm_b_i[li], mlstm_b_f[li])
            init = (state_mlstm_c[li].astype(jnp.float32), state_mlstm_n[li].astype(jnp.float32),
                    state_mlstm_m[li].astype(jnp.float32))
            (c_new, n_new, m_new), h = mlstm_chunk(init, (q, k, v, ig, lf))
            xs = xs + mlstm_out(h, og, mlstm_norm[li], w_out_odd[li], xs.dtype)
            mc_s.append(c_new)
            mn_s.append(n_new)
            mm_s.append(m_new)
        mkv = (rms_norm(mem_prompt, norm_mem[l]) @ xattn_wkv[l]).reshape(B, MEM_TOKENS, 2, X_HEADS, X_HD)
        memkv_p.append(mkv)
        xp = xp + cross_attn(rms_norm(xp, norm_xattn[l]), mkv, xattn_wq[l], xattn_wo[l])
        xs = xs + cross_attn(rms_norm(xs, norm_xattn[l]), cache_mem_kv[l], xattn_wq[l], xattn_wo[l])
        if l % 2 == 0:
            xp = xp + swiglu(rms_norm(xp, norm_ffn[l]), ffn_w_gu[li], ffn_w_dn[li])
            xs = xs + swiglu(rms_norm(xs, norm_ffn[l]), ffn_w_gu[li], ffn_w_dn[li])
        else:
            xp = xp + moe_ffn(rms_norm(xp, norm_ffn[l]), router_w[li], router_b[li], expert_w_gu[li], expert_w_dn[li])
            xs = xs + moe_ffn(rms_norm(xs, norm_ffn[l]), router_w[li], router_b[li], expert_w_gu[li], expert_w_dn[li])
    y_prompt = rms_norm(xp, norm_final)
    y_sample = rms_norm(xs, norm_final)
    return (y_prompt, y_sample, jnp.stack(conv_p), jnp.stack(conv_s), jnp.stack(nsa_p), jnp.stack(nsa_s),
            jnp.stack(win_p), jnp.stack(win_s), jnp.stack(mc_p), jnp.stack(mc_s), jnp.stack(mn_p),
            jnp.stack(mn_s), jnp.stack(mm_p), jnp.stack(mm_s), jnp.stack(memkv_p))


_drawn_inputs = setup_inputs


def setup_inputs(seed=0):
    import zlib

    import numpy as np

    out = dict(_drawn_inputs(seed))
    spreads = {}
    factors = {'norm_mix': 2.756,
     'norm_xattn': 5.991,
     'norm_mem': 5.562,
     'norm_final': 32.575,
     'conv_ln_g': 3.81,
     'conv_ln_b': 3.294,
     'mlstm_norm': 13.629,
     'router_b': 22.489,
     'norm_ffn': 5.181,
     'mlstm_b_i': 2.739}
    for name, (base, spread) in spreads.items():
        noise = np.random.default_rng([zlib.crc32(name.encode()), seed]).standard_normal(out[name].shape)
        drawn = base * np.exp(spread * noise) if base else spread * noise
        out[name] = __import__('jax').numpy.asarray(drawn.astype(out[name].dtype))
    for name, factor in factors.items():
        out[name] = (out[name] * factor).astype(out[name].dtype)
    return out
```

```python
import math
from contextlib import ExitStack

import numpy as np
import concourse.bass as bass
from concourse import mybir

F32 = mybir.dt.float32
I32 = mybir.dt.int32
U32 = mybir.dt.uint32
ALU = mybir.AluOpType
ACT = mybir.ActivationFunctionType
AX = mybir.AxisListType.X

P = 128
D = 1024
DC = D // P
S = 512
NB = 8
T = S + NB
HT = T // 2
MEM = 256
QB = S // P
NEG = -1e30
PAST = 2048
PAGE = 128
PAGES = PAST // PAGE
CMP = 32
CONV_W = 31
CONV_C = 4
GLP = CONV_W - 1 + S
GLW = GLP + NB * CONV_W
DFF_C = 22
EXP_C = 11
NE = 8
NH = 4
SLOTS = 4
SLOT = 4096
UNITS = 2
TB = 104
TBN = T // TB

VEC = {}
_at = 0
for _n, _w in [("mix0", 8), ("mix1", 8), ("x0", 8), ("x1", 8), ("mem0", 8), ("mem1", 8), ("ffn0", 8),
               ("ffn1", 8), ("final", 8), ("conv_b", 4), ("ln_g", 4), ("ln_b", 4), ("mnorm", 8),
               ("conv_w", 4 * CONV_W)]:
    VEC[_n] = _at
    _at += _w
VECW = _at


def buckets(dist):
    n = np.maximum(dist, 0)
    nf = np.maximum(n, 1).astype(np.float32)
    large = 16 + (np.log(nf / np.float32(16)) / np.float32(math.log(1024 / 16)) * np.float32(16)).astype(np.int32)
    return np.where(n < 16, n, np.minimum(large, 31))


def one_hot(dist):
    out = np.zeros((33, len(dist)), np.float32)
    ok = dist >= 0
    out[buckets(dist)[ok], np.nonzero(ok)[0]] = 1.0
    out[32, ~ok] = NEG
    return out


def constants():
    rows = np.arange(64)
    same = (rows[:, None] // 4 == np.arange(16)[None, :]).astype(np.float32)
    pick = np.zeros((4, 4, P), np.float32)
    for h in range(4):
        pick[h, h] = 1.0
    past = one_hot(PAST - np.arange(PAST + 1))
    return {
        "c_ident": np.eye(P, dtype=np.float32),
        "c_toep": one_hot(S - 1 - np.arange(640)),
        "c_past": past,
        "c_group": same,
        "c_groupT": np.ascontiguousarray(same.T),
        "c_pick": pick.reshape(4, 4 * P),
        "c_own": (rows[:, None] // 8 == np.arange(8)[None, :]).astype(np.float32),
        "c_row": np.stack([np.arange(P) >= CMP - 1, np.arange(P) // 8 % 2 == 0, np.arange(P) // 8 % 2 == 1], 1).astype(np.float32),
        "c_tri": (np.arange(P)[None, :] >= np.arange(P)[:, None]).astype(np.float32),
        "c_expert": np.tile(np.arange(8, dtype=np.float32), (P, 1)),
    }


def program(nc, I, O):
    ctx = ExitStack()
    with ctx:
        body(nc, I, O, ctx)


def body(nc, I, O, ctx):
    def sb(name, shape, dt=F32):
        return ctx.enter_context(nc.sbuf_tensor(name, shape, dt))

    sems = {}

    def sem(name):
        if name not in sems:
            sems[name] = ctx.enter_context(nc.semaphore(name))
        return sems[name]

    X = sb("residual", [P, DC, T])
    H = sb("normed", [P, DC, T])
    ring = sb("stream_ring", [P, SLOTS, SLOT])
    ident = sb("ident", [P, P])
    ones = sb("ones", [P, P])
    vec = sb("vectors", [P, VECW])
    group = sb("group", [64, 16])
    groupT = sb("groupT", [16, 64])
    pick = sb("pick", [4, 4, P])
    own = sb("own", [64, 8])
    rowok = sb("rowok", [P, 3])
    tri = sb("tri", [P, P])
    experts_iota = sb("experts_iota", [P, 8])
    relx = sb("relx", [33, 64])
    rb = sb("router_b", [P, 8])
    gate_b = sb("gate_b", [4, 2])
    router = sb("router_w", [P, DC, NE])
    pages = sb("page_table", [1, NB * PAGES], I32)
    small = sb("small", [P, 256])
    eps = sb("eps", [P, 2])
    sq = sb("squares", [P, 2, T])
    inv = sb("inverse_norm", [P, T])
    arena_words = 25088
    arena = sb("arena", [P, arena_words])
    psum_v = [ctx.enter_context(nc.psum_tensor(f"vector_unit{i}", [P, 1024], F32)) for i in range(UNITS)]
    psum_s = [ctx.enter_context(nc.psum_tensor(f"scalar_unit{i}", [P, 1024], F32)) for i in range(UNITS)]
    toep_dram = nc.dram_tensor("toeplitz_rows", [8, P * 641 + 640], F32, kind="Internal").ap()
    gates_dram = nc.dram_tensor("sample_gates", [NB * 24], F32, kind="Internal").ap()

    def at(lo, *shape, rows=P):
        n = int(np.prod(shape))
        assert lo + n <= arena_words, (lo, n)
        v = arena[0:rows, lo:lo + n]
        if len(shape) == 2:
            v = v.rearrange("p (a b) -> p a b", a=shape[0])
        if len(shape) == 3:
            v = v.rearrange("p (a b c) -> p a b c", a=shape[0], b=shape[1])
        return v

    def slot_view(s, *shape, rows=P):
        n = int(np.prod(shape))
        v = ring[0:rows, s, 0:n]
        if len(shape) == 2:
            v = v.rearrange("p (a b) -> p a b", a=shape[0])
        if len(shape) == 3:
            v = v.rearrange("p (a b c) -> p a b c", a=shape[0], b=shape[1])
        return v

    GL = at(0, CONV_C, GLW)
    Q = at(3160, 4, T)
    KV = at(5240, 6, T)
    CW = at(8360, 2, CMP, P)
    KC = at(16552, 2, S + 16)
    GT = at(17608, T)
    E = at(18128, 8, S)
    CA = at(22224, CONV_C, T)
    PE_T = at(24304, 2, CMP)
    PEB = at(24368, 2)
    VTOK = at(14800, 2, QB, P)
    TOH = at(18128, 640, rows=33)
    OHP = at(18128, PAST + 1, rows=33)
    SC = at(8360, 2, S)
    PT = at(9384, QB, 2, P)
    CP = at(10408, 8, 16)
    CPT = at(10536, 8, P, rows=16)
    VC = at(11560, P, rows=16)
    GTOK = at(11688, QB, 24)
    QP = at(11784, NB, 64)
    SS = at(8360, PAST + 1, rows=64)
    SPT = at(10416, 16, 64)
    WPT = at(11440, 4, 64)
    SW = at(12296, S + 1, rows=64)
    SCM = at(12816, 2, 64, rows=64)
    VCS = at(12944, 4, P)
    CPT2 = at(13456, 64)
    NEWV = at(13520, 2, P, rows=8)
    NEWP = at(13776, 2, 8, rows=64)
    NEWT = at(13792, 2, 64, rows=8)
    SG = at(13920, 4, rows=64)
    SCORE = at(13930, 3, 40, rows=16)
    TOP = at(14050, 8, rows=16)
    SELN = at(14060, 40, rows=16)
    TSP = at(14100, 640)

    MX = at(0, DC, MEM)
    MK = at(2048, 16, MEM)
    MV = at(6144, 2, D)
    QX = at(8192, DC, T)
    XP = at(12352, 4, MEM)
    XPT = at(13376, 8, P)
    QXP = at(14400, 64, 32)
    XS = at(16448, MEM, rows=32)
    XST = at(16704, 2, 32)
    AO = at(16768, DC, T)
    MH = at(20928, DC, MEM)

    HID = at(0, DFF_C, T)
    COMB = at(11440, NE, T)
    LOG = at(15600, TBN, 8)
    TOP8 = at(15640, TBN, 8)
    IDX = at(15680, TBN, 8)
    IDXF = at(15720, TBN, 8)
    CMB = at(15760, TBN, 8)
    YT = at(15800, T)

    MIX = at(0, DC, T)
    HQ = at(4160, 2, T)
    HK = at(5200, 2, T)
    HV = at(6240, 2, T)
    HO = at(7280, 2, T)
    KTOK = at(8320, QB, 256)
    VTK = at(9344, QB, 256)
    ST = at(10368, QB, S)
    MB = at(12416, S)
    WRAW = at(12928, S)
    HH = at(13440, 2, T)
    FM = at(14480, 6, T, rows=4)
    GC = at(17600, QB, 4)
    CS = at(17616, 2 * NB, 256)
    SN = at(21712, NH, 2, NB)
    ML = at(21776, NB * NH)
    GS = at(21808, 4, NB)
    VW = at(21840, QB, 256)
    CO = at(22864, 2, 256)
    NP_ = at(23376, NH, 2)
    DEN = at(23384, T)
    SM = at(23904, 64)
    MM = at(23968, 8)
    PRD = at(23976, 2, NB)
    SMO = at(24000, NH * NB)
    MMP = at(24032, 8)

    def counter():
        counts = {}

        def add(name, n=1):
            counts[name] = counts.get(name, 0) + n
            return counts[name]

        return add

    def turns(units):
        at_ = [0]

        def next_unit():
            at_[0] += 1
            return units[(at_[0] - 1) % UNITS]

        return next_unit

    stream = []

    def weights(tag, src, chunks, kc, per):
        for c in range(0, chunks, per):
            n = min(per, chunks - c)
            stream.append((tag, [(lambda s, n=n: slot_view(s, n, kc * P),
                                  src[c:c + n].rearrange("c p n -> p c n"), None)]))

    def plan():
        weights("in_even", I["w_in_even"], 19, DC, 4)
        for b in range(NB):
            stream.append(("cmp", [(lambda s, g=g: slot_view(s, PAGES, 2 * P)[:, g, :], None, (b * PAGES + g, 0, 256))
                                   for g in range(PAGES)]))
        stream.append(("win", [(lambda s: slot_view(s, NB, S), I["win_k"].rearrange("b p n -> p b n"), None)]))
        for b in range(0, NB, 2):
            stream.append(("ksel", [(lambda s, b2=b2, g=g: slot_view(s, 2, PAGES, P)[:, b2, g, :], None,
                                     ((b + b2) * PAGES + g, 256, 128)) for b2 in range(2) for g in range(PAGES)]))
        stream.append(("win", [(lambda s: slot_view(s, NB * 4, P), I["win_v"].rearrange("b (g p) n -> p (b g) n", p=P), None)]))
        for b in range(0, NB, 2):
            stream.append(("vsel", [(lambda s, b2=b2, g=g: slot_view(s, 2, PAGES, P)[:, b2, g, :], None,
                                     ((b + b2) * PAGES + g, 384, 128)) for b2 in range(2) for g in range(PAGES)]))
        weights("out_even", I["w_out_even"], DC, DC, 4)
        for l in range(2):
            if l == 1:
                weights("in_odd_g", I["w_in_odd"][0:1], 1, DC, 1)
                for h in range(NH):
                    weights("in_odd", I["w_in_odd"][1 + 8 * h:9 + 8 * h], 8, DC, 4)
                weights("out_odd", I["w_out_odd"], DC, DC, 4)
            weights("wkv", I["xattn_wkv"][l], 16, DC, 4)
            weights("wq", I["xattn_wq"][l], DC, DC, 4)
            for kv in range(2):
                for b in range(0, NB, 2):
                    stream.append(("memkv", [(lambda s: slot_view(s, 2, 2048),
                                              I["mem_kv"][l, kv, b:b + 2].rearrange("b p n -> p b n"), None)]))
            weights("wo", I["xattn_wo"][l], DC, DC, 4)
            if l == 0:
                weights("gu", I["ffn_w_gu"], 2 * DFF_C, DC, 4)
                weights("dn", I["ffn_w_dn"], DC, DFF_C, 1)
            else:
                for e in range(NE):
                    weights("egu", I["expert_w_gu"][e], 2 * EXP_C, DC, 4)
                    weights("edn", I["expert_w_dn"][e], DC, EXP_C, 2)

    plan()
    landed, total = [], [0] * SLOTS
    for n, (_, moves) in enumerate(stream):
        total[n % SLOTS] += 16 * len(moves)
        landed.append(total[n % SLOTS])

    const_loads = [(ident, I["c_ident"]), (vec, I["vectors"]), (group, I["c_group"]), (groupT, I["c_groupT"]),
                   (own, I["c_own"]), (rowok, I["c_row"]), (tri, I["c_tri"]), (experts_iota, I["c_expert"]),
                   (relx, I["relx"]), (rb, I["router_b"]), (gate_b, I["gate_b"])]

    block = ctx.enter_context(nc.Block())

    def col(name, c=0, rows=P):
        return vec[0:rows, VEC[name] + c:VEC[name] + c + 1]

    def halves(unit):
        return unit[:, :].rearrange("p (a b) -> p a b", a=2)[:, :, 0:HT]

    def split(v):
        return v.rearrange("p (a b) -> p a b", a=2)

    @block.sync
    def _(sp):
        sp.dma_start(pages[:, :], I["page_table"]).then_inc(sem("pages_in"), 16)
        sp.wait_ge(sem("pages_in"), 16)
        for n, (tag, moves) in enumerate(stream):
            s = n % SLOTS
            if n >= SLOTS:
                sp.wait_ge(sem(f"slot_free{s}"), n // SLOTS)
            for dst, src, page in moves:
                if page is not None:
                    entry, lo, w = page
                    number = sp.value_load(pages[0:1, entry:entry + 1], min_val=0, max_val=I["pages"].shape[0] - 1)
                    src = I["pages"][bass.ds(number, 1), :, lo:lo + w].rearrange("a p n -> p (a n)")
                sp.dma_start(dst(s), src).then_inc(sem(f"slot_ready{s}"), 16)

    @block.gpsimd
    def _(pool):
        due = counter()
        stores = [0]

        def load(dst, src, name):
            pool.dma_start(dst, src).then_inc(sem(name), 16)

        def store(dst, src):
            stores[0] += 16
            pool.dma_start(dst, src).then_inc(sem("stored"), 16)

        def stored():
            pool.wait_ge(sem("stored"), stores[0])

        load(X[:, :, :], I["xT"], "x_in")
        for dst, src in const_loads:
            load(dst[:, :], src, "consts_in")
        load(pick[:, :, :], I["c_pick"].rearrange("p (a b) -> p a b", a=4), "consts_in")
        load(router[:, :, :], I["router_w"], "consts_in")
        load(CW, I["cmp_w"], "cmp_w_in")
        load(PE_T, I["cmp_pe"], "cmp_w_in")
        for c in range(CONV_C):
            load(GL[:, c, GLP:GLW].rearrange("p (b w) -> p b w", b=NB)[:, :, 0:CONV_W - 1], I["cache_conv"][:, c], "conv_in")
        load(TOH, I["c_toep"], "toep_in")
        pool.wait_ge(sem("glu_done"), due("glu_done", CONV_C))
        store(O["conv_p"], GL[:, :, S:GLP])
        for c in range(CONV_C):
            store(O["conv_s"][:, c], GL[:, c, GLP:GLW].rearrange("p (b w) -> p b w", b=NB)[:, :, 1:CONV_W])
        pool.wait_ge(sem("kv_done"), due("kv_done"))
        store(O["kv"], KV[:, :, :])
        store(O["win_k_s"][:, :, 0:S - 1], I["win_k"][:, :, 1:S])
        store(O["win_v_s"][:, 0:S - 1, :], I["win_v"][:, 1:S, :])
        with nc.allow_non_contiguous_dma(reason="one new column per sample"):
            store(O["win_k_s"][:, :, S - 1:S].rearrange("b p n -> p b n"), KV[:, 4, S:T].rearrange("p (b n) -> p b n", n=1))
            store(O["win_v_s"][:, S - 1:S, :].rearrange("b n p -> p b n"), KV[:, 5, S:T].rearrange("p (b n) -> p b n", n=1))
        for h in range(8):
            pool.wait_ge(sem("toep_row"), due("toep_row"))
            store(toep_dram[h, 0:P * 641].rearrange("(p n) -> p n", p=P)[:, 0:640], TSP)
            stored()
            pool.sem_inc(sem("toep_row_out"), 1)
        for h in range(8):
            load(E[:, h, :], toep_dram[h, 127:127 + P * 640].rearrange("(p n) -> p n", p=P)[:, 0:S], "toep_back")
        pool.wait_ge(sem("attention_over"), due("attention_over"))
        load(OHP, I["c_past"], "past_in")
        pool.wait_ge(sem("gates_tok"), due("gates_tok"))
        store(gates_dram.rearrange("(b n) -> b n", b=NB), small[0:NB, 0:24])
        stored()
        load(SG[:, 0:3], gates_dram.rearrange("(r n) -> r n", n=3), "gates_rows")
        for l in range(2):
            pool.wait_ge(sem("mixer_over"), due("mixer_over"))
            load(MX, I["memT"], "mem_in")
            pool.wait_ge(sem("mkv_done"), due("mkv_done"))
            store(O["mem_kv"][l], MK)
            stored()
            pool.sem_inc(sem("mkv_out"), 1)
            if l == 0:
                pool.wait_ge(sem("ffn_over"), due("ffn_over"))
                load(SN, I["state_n"], "state_in")
                load(ML[:, :], I["state_m"], "state_in")
                for h in range(NH):
                    if h:
                        pool.wait_ge(sem("c_sample_done"), due("c_sample_done"))
                        store(O["c_s"][h - 1], CS)
                        stored()
                    load(CS, I["state_c"][h], "c_in")
                    for vc in range(2):
                        pool.wait_ge(sem("c_prompt_done"), due("c_prompt_done"))
                        store(O["c_p"][h, vc], CO[:, vc, :])
                    stored()
                    pool.sem_inc(sem("c_prompt_out"), 1)
                pool.wait_ge(sem("c_sample_done"), due("c_sample_done"))
                store(O["c_s"][NH - 1], CS)
                store(O["n_p"], NP_)
                store(O["n_s"], SN)
                store(O["m_s"], SMO[0:1, :])
                store(O["m_p"], MMP[0:4, 0:1])
                stored()
                pool.sem_inc(sem("states_out"), 1)
        pool.wait_ge(sem("y_done"), due("y_done"))
        store(O["y"], H[:, :, :])
        stored()

    @block.tensor
    def _(pe):
        due = counter()
        take_unit = {"vector": turns(psum_v), "scalar": turns(psum_s)}
        taken = [0]
        mm = nc.tensor.matmul

        def next_slot(tag):
            n = taken[0]
            assert stream[n][0] == tag, (stream[n][0], tag)
            taken[0] += 1
            return n % SLOTS, landed[n]

        def over_features(rhs, kc, who, n=T):
            pe.wait_ge(sem(f"{who}_unit_free"), due(f"{who}_unit_free"))
            u = take_unit[who]()
            for a in range(2):
                lo, w = (a * HT, HT) if n == T else (a * n // 2, n // 2)
                for k in range(kc):
                    ins = mm(u[:, a * 512:a * 512 + w], ones[:, :], rhs[:, k, lo:lo + w], start=(k == 0), stop=(k == kc - 1))
            ins.then_inc(sem(f"{who}_unit_ready"), 1)

        def norm(n=T):
            pe.wait_ge(sem("vector_unit_free"), due("vector_unit_free"))
            u = take_unit["vector"]()
            w = n // 2
            for k in range(DC):
                pe.wait_ge(sem("square"), due("square"))
                for a in range(2):
                    ins = mm(u[:, a * 512:a * 512 + w], ones[:, :], sq[:, k % 2, a * w:a * w + w],
                             start=(k == 0), stop=(k == DC - 1))
                if k < DC - 1:
                    ins.then_inc(sem("square_used"), 1)
            ins.then_inc(sem("vector_unit_ready"), 1)

        def project(tag, src, chunks, kc, per, readers, n=T, cols=P):
            w = n // 2
            for c in range(chunks):
                if c % per == 0:
                    s, filled = next_slot(tag)
                    pe.wait_ge(sem(f"slot_ready{s}"), filled)
                wt = slot_view(s, per, kc, P)
                pe.wait_ge(sem(f"{readers[c]}_unit_free"), due(f"{readers[c]}_unit_free"))
                u = take_unit[readers[c]]()
                for a in range(2):
                    for k in range(kc):
                        ins = mm(u[0:cols, a * 512:a * 512 + w], wt[:, c % per, k, 0:cols], src[:, k, a * w:a * w + w],
                                 start=(k == 0), stop=(k == kc - 1))
                ins.then_inc(sem(f"{readers[c]}_unit_ready"), 1)
                if c % per == 0 and c:
                    pe.wait_ge(sem(f"{readers[c - 1]}_unit_ready"), before)
                    pe.sem_inc(sem(f"slot_free{last}"), 1)
                last, before = s, due(f"{readers[c]}_unit_free", 0)
            pe.wait_ge(sem(f"{readers[c]}_unit_ready"), before)
            pe.sem_inc(sem(f"slot_free{last}"), 1)

        pe.wait_ge(sem("consts_in"), 16 * (len(const_loads) + 2))
        pe.wait_ge(sem("ones_set"), due("ones_set"))
        norm()
        pe.wait_ge(sem("normed"), due("normed"))
        project("in_even", H, 19, DC, 4, ["scalar", "scalar"] * 4 + ["scalar"] * 4 + ["vector"] * 6 + ["scalar"])

        pe.wait_ge(sem("cmp_w_in"), 32)
        pe.wait_ge(sem("vector_unit_free"), due("vector_unit_free"))
        u = take_unit["vector"]()
        for v in range(2):
            for j in range(CMP):
                ins = mm(u[:, v:v + 1], CW[:, v, j, :], PE_T[:, v, j:j + 1], start=(j == 0), stop=(j == CMP - 1))
        ins.then_inc(sem("vector_unit_ready"), 1)
        pe.wait_ge(sem("kv_ready"), due("kv_ready"))
        pe.wait_ge(sem("vector_unit_free"), due("vector_unit_free"))
        u = take_unit["vector"]()
        for v in range(2):
            for j in range(CMP):
                ins = mm(u[:, v * 16:v * 16 + 16], CW[:, v, j, :], KV[:, v, j:S:CMP], start=(j == 0), stop=(j == CMP - 1))
        ins.then_inc(sem("vector_unit_ready"), 1)
        for b in range(NB):
            s, filled = next_slot("cmp")
            pe.wait_ge(sem(f"slot_ready{s}"), filled)
            pg = slot_view(s, PAGES, 2, P)
            pe.wait_ge(sem("vector_unit_free"), due("vector_unit_free"))
            u = take_unit["vector"]()
            for v in range(2):
                for j in range(CMP):
                    ins = mm(u[:, v * 64:v * 64 + 64], CW[:, v, j, :],
                             pg[:, :, v, :].rearrange("p g (c j) -> p g c j", j=CMP)[:, :, :, j],
                             start=(j == 0), stop=(j == CMP - 1))
            ins.then_inc(sem("vector_unit_ready"), 1)
            pe.wait_ge(sem("vector_unit_ready"), due("vector_unit_free", 0))
            pe.sem_inc(sem(f"slot_free{s}"), 1)
        pe.wait_ge(sem("toep_in"), 16)
        for h in range(8):
            pe.wait_ge(sem("scalar_unit_free"), due("scalar_unit_free"))
            u = take_unit["scalar"]()
            for a, (lo, w) in enumerate(((0, 512), (512, 128))):
                ins = mm(u[:, lo:lo + w], relx[:, h:h + 1].broadcast_to([33, P]), TOH[:, lo:lo + w],
                         start=True, stop=True)
            ins.then_inc(sem("scalar_unit_ready"), 1)
        pe.wait_ge(sem("scalar_unit_free"), due("scalar_unit_free"))
        u = take_unit["scalar"]()
        for v in range(2):
            for g in range(QB):
                ins = nc.tensor.transpose(u[:, (v * QB + g) * P:(v * QB + g + 1) * P], KV[:, 3 + 2 * v, g * P:(g + 1) * P], ident[:, :])
        ins.then_inc(sem("scalar_unit_ready"), 1)
        pe.wait_ge(sem("scalar_unit_free"), due("scalar_unit_free"))
        u = take_unit["scalar"]()
        for g in range(QB):
            nc.tensor.transpose(u[:, g * 24:g * 24 + 24], GT[0:24, g * P:(g + 1) * P], ident[0:24, 0:24])
        nc.tensor.transpose(u[0:NB, 96:120], GT[0:24, S:T], ident[0:24, 0:24])
        pe.wait_ge(sem("kc_ready"), due("kc_ready"))
        nc.tensor.transpose(u[0:16, 128:256], KC[:, 1, S:S + 16], ident[:, :])
        for v in range(2):
            nc.tensor.transpose(u[0:NB, 256 + v * P:384 + v * P], KV[:, 3 + 2 * v, S:T], ident[:, :])
        for g in range(4):
            ins = nc.tensor.transpose(u[:, 512 + g * P:512 + (g + 1) * P], KC[:, 1, g * P:(g + 1) * P], ident[:, :])
        ins.then_inc(sem("scalar_unit_ready"), 1)
        pe.wait_ge(sem("tok_ready"), due("tok_ready"))

        for qb in range(QB):
            wc = 4 * (qb + 1)
            pe.wait_ge(sem("vector_unit_free"), due("vector_unit_free"))
            u = take_unit["vector"]()
            for k in range(2):
                for g in range(4):
                    ins = mm(u[:, 512 * k + g * 16:512 * k + g * 16 + wc], Q[64 * k:64 * k + 64, g, qb * P:(qb + 1) * P],
                             KC[64 * k:64 * k + 64, 0, S:S + wc], start=True, stop=True)
            ins.then_inc(sem("vector_unit_ready"), 1)
            pe.wait_ge(sem("cmp_probs"), due("cmp_probs"))
            pe.wait_ge(sem("scalar_unit_free"), due("scalar_unit_free"))
            u = take_unit["scalar"]()
            for h in range(8):
                ins = nc.tensor.transpose(u[0:wc, h * P:(h + 1) * P], CP[:, h, 0:wc], ident[:, :])
            ins.then_inc(sem("scalar_unit_ready"), 1)
            pe.wait_ge(sem("cmp_probs_T"), due("cmp_probs_T"))
            for k in range(2):
                for gp in range(2):
                    pts = []
                    for br in range(2):
                        pe.wait_ge(sem("vector_unit_free"), due("vector_unit_free"))
                        u = take_unit["vector"]()
                        for g in range(2):
                            ins = mm(u[:, g * 512:g * 512 + (qb + 1) * P], Q[64 * k:64 * k + 64, 2 * gp + g, qb * P:(qb + 1) * P],
                                     KV[64 * k:64 * k + 64, 2 + 2 * br, 0:(qb + 1) * P], start=True, stop=True)
                        ins.then_inc(sem("vector_unit_ready"), 1)
                        pe.wait_ge(sem("probs"), due("probs"))
                        pe.wait_ge(sem("scalar_unit_free"), due("scalar_unit_free"))
                        u = take_unit["scalar"]()
                        for kb in range(qb + 1):
                            for g in range(2):
                                ins = nc.tensor.transpose(u[:, (kb * 2 + g) * P:(kb * 2 + g + 1) * P], SC[:, g, kb * P:(kb + 1) * P], ident[:, :])
                        ins.then_inc(sem("scalar_unit_ready"), 1)
                        pe.wait_ge(sem("probs_T"), due("probs_T"))
                        pe.wait_ge(sem("vector_unit_free"), due("vector_unit_free"))
                        u = take_unit["vector"]()
                        o = u
                        h = 4 * k + 2 * gp
                        if br == 0:
                            mm(o[:, 0:256], VC[0:wc, :], CPT[0:wc, h:h + 2, :].rearrange("p a b -> p (a b)"), start=True, stop=False)
                        for kb in range(qb + 1):
                            ins = mm(o[:, 0:256], VTOK[:, br, kb, :], PT[:, kb, :, :].rearrange("p a b -> p (a b)"),
                                     start=(br == 1 and kb == 0), stop=(kb == qb))
                        ins.then_inc(sem("vector_unit_ready"), 1)

        pe.wait_ge(sem("qp_ready"), due("qp_ready"))
        pe.wait_ge(sem("past_in"), 16)
        oh = OHP
        rel64 = relx[:, :]
        pe.wait_ge(sem("vector_unit_free"), due("vector_unit_free"))
        u = take_unit["vector"]()
        for b in range(NB):
            mm(u[0:64, 0:64], QP[:, b, :], KC[:, 0, b * 64:(b + 1) * 64], start=(b == 0), stop=False)
        ins = mm(u[0:64, 0:64], rel64, oh[:, CMP - 1:PAST:CMP], start=False, stop=True)
        ins.then_inc(sem("vector_unit_ready"), 1)
        pe.wait_ge(sem("cmp_s"), due("cmp_s"))
        pe.wait_ge(sem("vector_unit_free"), due("vector_unit_free"))
        u = take_unit["vector"]()
        ins = mm(u[0:16, 0:64], group[:, :], SCM[:, 1, :], start=True, stop=True)
        ins.then_inc(sem("vector_unit_ready"), 1)
        s, filled = next_slot("win")
        pe.wait_ge(sem(f"slot_ready{s}"), filled)
        wk = slot_view(s, NB, S)
        pe.wait_ge(sem("scalar_unit_free"), due("scalar_unit_free"))
        u = take_unit["scalar"]()
        swin = u
        for b in range(NB):
            mm(swin[0:64, 0:S], QP[:, b, :], wk[:, b, :], start=(b == 0), stop=False)
        mm(swin[0:64, 0:S], rel64, oh[:, PAST - S:PAST], start=False, stop=True)
        for v in range(2):
            for b in range(NB):
                mm(swin[0:64, S + v:S + v + 1], QP[:, b, :], KV[:, 2 + 2 * v, S + b:S + b + 1], start=(b == 0), stop=False)
            ins = mm(swin[0:64, S + v:S + v + 1], rel64, oh[:, PAST:PAST + 1], start=False, stop=True)
        ins.then_inc(sem("scalar_unit_ready"), 1)
        pe.wait_ge(sem("scalar_unit_ready"), due("scalar_unit_free", 0))
        pe.sem_inc(sem(f"slot_free{s}"), 1)
        pe.wait_ge(sem("vector_unit_free"), due("vector_unit_free"))
        u = take_unit["vector"]()
        us = [u]
        pe.wait_ge(sem("vector_unit_free"), due("vector_unit_free"))
        u = take_unit["vector"]()
        us += [u]
        banks = [us[i // 2][0:64, (i % 2) * 512:(i % 2) * 512 + 512] for i in range(4)]
        for b in range(NB):
            if b % 2 == 0:
                s, filled = next_slot("ksel")
                pe.wait_ge(sem(f"slot_ready{s}"), filled)
                ks = slot_view(s, 2, PAGES * P)
            for i in range(4):
                ins = mm(banks[i], QP[:, b, :], ks[:, b % 2, i * 512:(i + 1) * 512], start=(b == 0), stop=False)
            if b % 2:
                ins.then_inc(sem(f"slot_free{s}"), 1)
        pe.wait_ge(sem("sel_mask"), due("sel_mask"))
        for i in range(4):
            mm(banks[i], rel64, oh[:, i * 512:(i + 1) * 512], start=False, stop=False)
            ins = mm(banks[i], groupT[:, :], SELN[:, i * 8:i * 8 + 8].rearrange("p (a b) -> p a b", b=1).broadcast_to([16, 8, 64]),
                     start=False, stop=True)
            if i % 2:
                ins.then_inc(sem("vector_unit_ready"), 1)
        pe.wait_ge(sem("sel_probs"), due("sel_probs"))
        pe.wait_ge(sem("scalar_unit_free"), due("scalar_unit_free"))
        u = take_unit["scalar"]()
        for g in range(PAGES):
            ins = nc.tensor.transpose(u[:, g * 64:(g + 1) * 64], SS[:, g * P:(g + 1) * P], ident[0:64, 0:64])
        ins.then_inc(sem("scalar_unit_ready"), 1)
        pe.wait_ge(sem("win_probs"), due("win_probs"))
        pe.wait_ge(sem("scalar_unit_free"), due("scalar_unit_free"))
        u = take_unit["scalar"]()
        for g in range(4):
            nc.tensor.transpose(u[:, g * 64:(g + 1) * 64], SW[:, g * P:(g + 1) * P], ident[0:64, 0:64])
        nc.tensor.transpose(u[:, 256:320], SCM[:, :, :].rearrange("p a b -> p (a b)"), ident[0:64, 0:64])
        for v in range(2):
            ins = nc.tensor.transpose(u[0:8, 320 + 64 * v:384 + 64 * v], NEWP[:, v, :], ident[0:64, 0:64])
        ins.then_inc(sem("scalar_unit_ready"), 1)
        pe.wait_ge(sem("sample_T"), due("sample_T"))
        s, filled = next_slot("win")
        pe.wait_ge(sem(f"slot_ready{s}"), filled)
        wv = slot_view(s, NB, 4, P)
        pe.wait_ge(sem("vector_unit_free"), due("vector_unit_free"))
        u = take_unit["vector"]()
        o = u
        for b in range(NB):
            r = slice(8 * b, 8 * b + 8)
            for g in range(4):
                mm(o[:, r], wv[:, b, g, :], WPT[:, g, r], start=(g == 0), stop=False)
            for v in range(2):
                mm(o[:, r], NEWV[:, v, :], NEWT[:, v, r], start=False, stop=False)
            ins = mm(o[:, r], VCS[:, b // 2, :], CPT2[:, r], start=False, stop=True)
        ins.then_inc(sem(f"slot_free{s}"), 1)
        for b in range(NB):
            if b % 2 == 0:
                s, filled = next_slot("vsel")
                pe.wait_ge(sem(f"slot_ready{s}"), filled)
                vs = slot_view(s, 2, PAGES, P)
            for g in range(PAGES):
                ins = mm(o[:, 512 + 8 * b:520 + 8 * b], vs[:, b % 2, g, :], SPT[:, g, 8 * b:8 * b + 8], start=(g == 0), stop=(g == PAGES - 1))
            if b == NB - 1:
                ins.then_inc(sem("vector_unit_ready"), 1)
                pe.wait_ge(sem("vector_unit_ready"), due("vector_unit_free", 0))
                pe.sem_inc(sem(f"slot_free{s}"), 1)
            elif b % 2:
                ins.then_inc(sem(f"slot_free{s}"), 1)
        pe.wait_ge(sem("conv_done"), due("conv_done"))
        over_features(CA, CONV_C, "vector")
        pe.wait_ge(sem("centred"), due("centred"))
        over_features(GL, CONV_C, "vector")
        pe.wait_ge(sem("mix_ready"), due("mix_ready"))
        project("out_even", H, DC, DC, 4, ["vector"] * DC)

        def cross(l):
            norm(MEM)
            pe.wait_ge(sem("normed"), due("normed"))
            project("wkv", MH, 16, DC, 4, ["scalar"] * 16, n=MEM)
            norm()
            pe.wait_ge(sem("normed"), due("normed"))
            project("wq", H, DC, DC, 4, ["scalar"] * DC)
            pe.wait_ge(sem("mkv_ready"), due("mkv_ready"))
            for t in range(2):
                pe.wait_ge(sem("scalar_unit_free"), due("scalar_unit_free"))
                u = take_unit["scalar"]()
                for c in range(8):
                    ins = nc.tensor.transpose(u[:, c * P:(c + 1) * P], MK[:, 8 + c, t * P:(t + 1) * P], ident[:, :])
                ins.then_inc(sem("scalar_unit_ready"), 1)
            pe.wait_ge(sem("mv_ready"), due("mv_ready"))
            for qb in range(QB):
                pe.wait_ge(sem("vector_unit_free"), due("vector_unit_free"))
                u = take_unit["vector"]()
                for h in range(4):
                    for c in range(2):
                        ins = mm(u[:, h * MEM:(h + 1) * MEM], QX[:, 2 * h + c, qb * P:(qb + 1) * P], MK[:, 2 * h + c, :],
                                 start=(c == 0), stop=(c == 1))
                ins.then_inc(sem("vector_unit_ready"), 1)
                pe.wait_ge(sem("xprobs"), due("xprobs"))
                pe.wait_ge(sem("scalar_unit_free"), due("scalar_unit_free"))
                u = take_unit["scalar"]()
                for h in range(4):
                    for t in range(2):
                        ins = nc.tensor.transpose(u[:, (2 * h + t) * P:(2 * h + t + 1) * P], XP[:, h, t * P:(t + 1) * P], ident[:, :])
                ins.then_inc(sem("scalar_unit_ready"), 1)
                pe.wait_ge(sem("xprobs_T"), due("xprobs_T"))
                pe.wait_ge(sem("scalar_unit_free"), due("scalar_unit_free"))
                u = take_unit["scalar"]()
                for h in range(4):
                    for c in range(2):
                        for t in range(2):
                            ins = mm(u[:, (2 * h + c) * P:(2 * h + c + 1) * P], MV[:, t, (2 * h + c) * P:(2 * h + c + 1) * P],
                                     XPT[:, 2 * h + t, :], start=(t == 0), stop=(t == 1))
                ins.then_inc(sem("scalar_unit_ready"), 1)
            pe.wait_ge(sem("qxp_ready"), due("qxp_ready"))
            pe.wait_ge(sem("vector_unit_free"), due("vector_unit_free"))
            u = take_unit["vector"]()
            for b in range(NB):
                if b % 2 == 0:
                    s, filled = next_slot("memkv")
                    pe.wait_ge(sem(f"slot_ready{s}"), filled)
                    mk = slot_view(s, 2, DC, MEM)
                for c in range(DC):
                    ins = mm(u[0:32, 0:MEM], QXP[:, b * DC + c, :], mk[:, b % 2, c, :], start=(b == 0 and c == 0),
                             stop=(b == NB - 1 and c == DC - 1))
                if b == NB - 1:
                    ins.then_inc(sem("vector_unit_ready"), 1)
                    pe.wait_ge(sem("vector_unit_ready"), due("vector_unit_free", 0))
                    pe.sem_inc(sem(f"slot_free{s}"), 1)
                elif b % 2:
                    ins.then_inc(sem(f"slot_free{s}"), 1)
            pe.wait_ge(sem("xs_probs"), due("xs_probs"))
            pe.wait_ge(sem("vector_unit_free"), due("vector_unit_free"))
            u = take_unit["vector"]()
            for t in range(2):
                ins = nc.tensor.transpose(u[:, t * 32:(t + 1) * 32], XS[:, t * P:(t + 1) * P], ident[0:32, 0:32])
            ins.then_inc(sem("vector_unit_ready"), 1)
            pe.wait_ge(sem("xs_T"), due("xs_T"))
            pe.wait_ge(sem("vector_unit_free"), due("vector_unit_free"))
            u = take_unit["vector"]()
            for b in range(NB):
                if b % 2 == 0:
                    s, filled = next_slot("memkv")
                    pe.wait_ge(sem(f"slot_ready{s}"), filled)
                    mv = slot_view(s, 2, 2, D)
                for c in range(DC):
                    for t in range(2):
                        ins = mm(u[:, c * NB + b:c * NB + b + 1], mv[:, b % 2, t, c * P:(c + 1) * P],
                                 XST[:, t, 4 * b + c // 2:4 * b + c // 2 + 1], start=(t == 0), stop=(t == 1))
                if b == NB - 1:
                    ins.then_inc(sem("vector_unit_ready"), 1)
                    pe.wait_ge(sem("vector_unit_ready"), due("vector_unit_free", 0))
                    pe.sem_inc(sem(f"slot_free{s}"), 1)
                elif b % 2:
                    ins.then_inc(sem(f"slot_free{s}"), 1)
            pe.wait_ge(sem("ao_ready"), due("ao_ready"))
            project("wo", AO, DC, DC, 4, ["vector"] * DC)

        cross(0)
        norm()
        pe.wait_ge(sem("normed"), due("normed"))
        project("gu", H, 2 * DFF_C, DC, 4, ["scalar", "vector"] * DFF_C)
        pe.wait_ge(sem("hidden"), due("hidden"))
        project("dn", HID, DC, DFF_C, 1, ["vector"] * DC)

        norm()
        pe.wait_ge(sem("normed"), due("normed"))
        project("in_odd_g", H, 1, DC, 1, ["scalar"], cols=64)
        pe.wait_ge(sem("gate_rows"), due("gate_rows"))
        pe.wait_ge(sem("scalar_unit_free"), due("scalar_unit_free"))
        u = take_unit["scalar"]()
        for g in range(QB):
            ins = nc.tensor.transpose(u[:, g * 4:g * 4 + 4], FM[0:4, 2, g * P:(g + 1) * P], ident[0:4, 0:4])
        ins.then_inc(sem("scalar_unit_ready"), 1)
        for h in range(NH):
            project("in_odd", H, 8, DC, 4, ["scalar"] * 8)
            pe.wait_ge(sem("head_ready"), due("head_ready"))
            for src in (HK, HV):
                pe.wait_ge(sem("scalar_unit_free"), due("scalar_unit_free"))
                u = take_unit["scalar"]()
                for g in range(QB):
                    for c in range(2):
                        ins = nc.tensor.transpose(u[:, g * 256 + c * P:g * 256 + (c + 1) * P], src[:, c, g * P:(g + 1) * P], ident[:, :])
                ins.then_inc(sem("scalar_unit_ready"), 1)
            pe.wait_ge(sem("vector_unit_free"), due("vector_unit_free"))
            u = take_unit["vector"]()
            mm(u[:, 0:S], pick[:, h, :], FM[0:4, 3, 0:S], start=True, stop=True)
            mm(u[:, S:S + NB], pick[:, h, :], FM[0:4, 0, S:T], start=True, stop=True)
            ins = mm(u[:, S + NB:S + 2 * NB], pick[:, h, :], FM[0:4, 1, S:T], start=True, stop=True)
            ins.then_inc(sem("vector_unit_ready"), 1)
            for sb_ in range(QB):
                pe.wait_ge(sem("vector_unit_free"), due("vector_unit_free"))
                u = take_unit["vector"]()
                w = S - sb_ * P
                for c in range(2):
                    ins = mm(u[:, 0:w], HK[:, c, sb_ * P:(sb_ + 1) * P], HQ[:, c, sb_ * P:S], start=(c == 0), stop=(c == 1))
                ins.then_inc(sem("vector_unit_ready"), 1)
            pe.wait_ge(sem("st_ready"), due("st_ready"))
            for part in range(3):
                pe.wait_ge(sem("vector_unit_free"), due("vector_unit_free"))
                u = take_unit["vector"]()
                for sb_ in range(QB):
                    lhs = ones[:, :] if part == 2 else VTK[:, sb_, part * P:(part + 1) * P]
                    ins = mm(u[:, sb_ * P:S], lhs, ST[:, sb_, sb_ * P:S], start=(sb_ == 0), stop=(sb_ == QB - 1))
                ins.then_inc(sem("vector_unit_ready"), 1)
            pe.wait_ge(sem("vector_unit_free"), due("vector_unit_free"))
            u = take_unit["vector"]()
            ins = mm(u[:, 0:S], pick[:, h, :], FM[0:4, 5, 0:S], start=True, stop=True)
            ins.then_inc(sem("vector_unit_ready"), 1)
            pe.wait_ge(sem("vw_ready"), due("vw_ready"))
            pe.wait_ge(sem("scalar_unit_free"), due("scalar_unit_free"))
            u = take_unit["scalar"]()
            for vc in range(2):
                for g in range(QB):
                    mm(u[:, vc * 256:vc * 256 + 256], VW[:, g, vc * P:(vc + 1) * P], KTOK[:, g, :], start=(g == 0), stop=(g == QB - 1))
            for c in range(2):
                for g in range(QB):
                    ins = mm(u[:, 512 + c:513 + c], KTOK[:, g, c * P:(c + 1) * P], SM[:, g:g + 1], start=(g == 0), stop=(g == QB - 1))
            ins.then_inc(sem("scalar_unit_ready"), 1)
            for src in (HK, HQ):
                for half in range(2):
                    pe.wait_ge(sem("vector_unit_free"), due("vector_unit_free"))
                    u = take_unit["vector"]()
                    for b in range(4):
                        for c in range(2):
                            ins = mm(u[:, b * 256 + c * P:b * 256 + (c + 1) * P],
                                     src[:, c, S + half * 4 + b:S + half * 4 + b + 1].broadcast_to([P, P]), ident[:, :], start=True, stop=True)
                    ins.then_inc(sem("vector_unit_ready"), 1)
            pe.wait_ge(sem("nq_ready"), due("nq_ready"))
            pe.wait_ge(sem("vector_unit_free"), due("vector_unit_free"))
            u = take_unit["vector"]()
            for c in range(2):
                ins = mm(u[:, 0:NB], ones[:, :], PRD[:, c, :], start=(c == 0), stop=(c == 1))
            ins.then_inc(sem("vector_unit_ready"), 1)
            pe.wait_ge(sem("head_out"), due("head_out"))
            over_features(sq, 2, "vector")
        pe.wait_ge(sem("mix_ready"), due("mix_ready"))
        project("out_odd", MIX, DC, DC, 4, ["vector"] * DC)
        cross(1)

        norm()
        pe.wait_ge(sem("normed"), due("normed"))
        pe.wait_ge(sem("vector_unit_free"), due("vector_unit_free"))
        u = take_unit["vector"]()
        for t in range(TBN):
            for k in range(DC):
                ins = mm(u[0:TB, t * 8:t * 8 + 8], H[:, k, t * TB:(t + 1) * TB], router[:, k, :], start=(k == 0), stop=(k == DC - 1))
        ins.then_inc(sem("vector_unit_ready"), 1)
        pe.wait_ge(sem("comb_ready"), due("comb_ready"))
        for e in range(NE):
            pe.wait_ge(sem("scalar_unit_free"), due("scalar_unit_free"))
            u = take_unit["scalar"]()
            for t in range(TBN):
                lo = t * TB if t < 3 else 512 + (t - 3) * TB
                ins = mm(u[:, lo:lo + TB], CMB[0:TB, t, e:e + 1].broadcast_to([TB, P]), ident[0:TB, 0:TB], start=True, stop=True)
            ins.then_inc(sem("scalar_unit_ready"), 1)
        for e in range(NE):
            project("egu", H, 2 * EXP_C, DC, 4, ["scalar", "vector"] * EXP_C)
            pe.wait_ge(sem("hidden"), due("hidden"))
            project("edn", HID, DC, EXP_C, 2, ["vector"] * DC)
        norm()

    @block.scalar
    def _(act):
        due, sent = counter(), counter()
        next_unit = turns(psum_s)
        act.sem_inc(sem("scalar_unit_free"), UNITS)
        sent("scalar_unit_free", UNITS)
        A = nc.scalar.activation

        def squares(src, n=T):
            for k in range(DC):
                if k >= 2:
                    act.wait_ge(sem("square_used"), due("square_used"))
                A(sq[:, k % 2, 0:n], src[:, k, 0:n], ACT.Square).then_inc(sem("square"), 1)
                act.wait_ge(sem("square"), sent("square"))
            act.wait_ge(sem("square_used"), due("square_used"))

        def norm(src, n=T):
            squares(src, n)
            act.wait_ge(sem("mean_copied"), due("mean_copied"))
            A(inv[:, 0:n], inv[:, 0:n], ACT.Sqrt).then_inc(sem("root"), 1)
            act.wait_ge(sem("root"), sent("root"))

        act.wait_ge(sem("x_in"), 16)
        act.wait_ge(sem("consts_in"), 16 * (len(const_loads) + 2))
        norm(X)
        act.wait_ge(sem("conv_in"), 16 * CONV_C)
        for c in range(CONV_C):
            act.wait_ge(sem("scalar_unit_ready"), due("scalar_unit_ready"))
            u = next_unit()
            ev = halves(u)
            tmp = split(CA[:, c, :])
            A(tmp, ev, ACT.Copy).then_inc(sem("scalar_unit_free"), 1)
            act.wait_ge(sem("scalar_unit_free"), sent("scalar_unit_free"))
            act.wait_ge(sem("scalar_unit_ready"), due("scalar_unit_ready"))
            u = next_unit()
            A(split(sq[:, 0, :]), halves(u), ACT.Sigmoid).then_inc(sem("scalar_unit_free"), 1)
            act.wait_ge(sem("scalar_unit_free"), sent("scalar_unit_free"))
            act.sem_inc(sem("glu_parts"), 1)
            act.wait_ge(sem("glu_done"), due("glu_done"))
        for c in range(4):
            act.wait_ge(sem("scalar_unit_ready"), due("scalar_unit_ready"))
            u = next_unit()
            A(split(Q[:, c, :]), halves(u), ACT.Copy, scale=0.125).then_inc(sem("scalar_unit_free"), 1)
            act.wait_ge(sem("scalar_unit_free"), sent("scalar_unit_free"))
        act.wait_ge(sem("scalar_unit_ready"), due("scalar_unit_ready"))
        u = next_unit()
        A(split(GT)[0:24], halves(u)[0:24], ACT.Sigmoid).then_inc(sem("scalar_unit_free"), 1)
        act.wait_ge(sem("scalar_unit_free"), sent("scalar_unit_free"))
        for h in range(8):
            act.wait_ge(sem("scalar_unit_ready"), due("scalar_unit_ready"))
            u = next_unit()
            if h:
                act.wait_ge(sem("toep_row_out"), due("toep_row_out"))
            A(TSP[:, 0:320], u[:, 0:320], ACT.Copy).then_inc(sem("scalar_steps"), 1)
            act.wait_ge(sem("scalar_steps"), sent("scalar_steps"))
            A(TSP[:, 320:640], u[:, 320:640], ACT.Copy).then_inc(sem("scalar_unit_free"), 1)
            act.wait_ge(sem("scalar_unit_free"), sent("scalar_unit_free"))
            act.sem_inc(sem("toep_row"), 1)
        act.wait_ge(sem("scalar_unit_ready"), due("scalar_unit_ready"))
        u = next_unit()
        A(VTOK.rearrange("p a b c -> p (a b c)"), u[:, :], ACT.Copy).then_inc(sem("scalar_unit_free"), 1)
        act.wait_ge(sem("scalar_unit_free"), sent("scalar_unit_free"))
        act.wait_ge(sem("scalar_unit_ready"), due("scalar_unit_ready"))
        u = next_unit()
        A(small[0:NB, 0:24], u[0:NB, 96:120], ACT.Copy).then_inc(sem("scalar_steps"), 1)
        act.wait_ge(sem("scalar_steps"), sent("scalar_steps"))
        act.sem_inc(sem("gates_tok"), 1)
        A(GTOK.rearrange("p a b -> p (a b)"), u[:, 0:96], ACT.Copy).then_inc(sem("scalar_steps"), 1)
        act.wait_ge(sem("scalar_steps"), sent("scalar_steps"))
        A(VC, u[0:16, 128:256], ACT.Copy).then_inc(sem("scalar_steps"), 1)
        act.wait_ge(sem("scalar_steps"), sent("scalar_steps"))
        A(NEWV.rearrange("p a b -> p (a b)"), u[0:NB, 256:512], ACT.Copy).then_inc(sem("scalar_steps"), 1)
        act.wait_ge(sem("scalar_steps"), sent("scalar_steps"))
        A(VCS.rearrange("p a b -> p (a b)"), u[:, 512:1024], ACT.Copy).then_inc(sem("scalar_unit_free"), 1)
        act.wait_ge(sem("scalar_unit_free"), sent("scalar_unit_free"))
        act.sem_inc(sem("tok_ready"), 1)
        act.sem_inc(sem("tok_ready_v"), 1)
        for qb in range(QB):
            wc = 4 * (qb + 1)
            act.wait_ge(sem("cmp_shifted"), due("cmp_shifted"))
            A(CP[:, :, 0:wc], CP[:, :, 0:wc], ACT.Exp).then_inc(sem("cmp_exp"), 1)
            act.wait_ge(sem("cmp_exp"), sent("cmp_exp"))
            act.wait_ge(sem("scalar_unit_ready"), due("scalar_unit_ready"))
            u = next_unit()
            A(CPT[0:wc, :, :].rearrange("p a b -> p (a b)"), u[0:wc, :], ACT.Copy).then_inc(sem("scalar_unit_free"), 1)
            act.wait_ge(sem("scalar_unit_free"), sent("scalar_unit_free"))
            act.sem_inc(sem("cmp_probs_T"), 1)
            for _k in range(8):
                w = (qb + 1) * P
                act.wait_ge(sem("shifted"), due("shifted"))
                for g in range(2):
                    ins = A(SC[:, g, 0:w], SC[:, g, 0:w], ACT.Exp, bias=small[:, 64 + g:65 + g], accum_out=small[:, 68 + g:69 + g])
                    if g == 0:
                        ins.then_inc(sem("scalar_steps"), 1)
                        act.wait_ge(sem("scalar_steps"), sent("scalar_steps"))
                ins.then_inc(sem("exped"), 1)
                act.wait_ge(sem("exped"), sent("exped"))
                act.wait_ge(sem("scalar_unit_ready"), due("scalar_unit_ready"))
                u = next_unit()
                A(PT[:, 0:qb + 1, :, :].rearrange("p a b c -> p (a b c)"), u[:, 0:2 * w], ACT.Copy).then_inc(sem("scalar_unit_free"), 1)
                act.wait_ge(sem("scalar_unit_free"), sent("scalar_unit_free"))
                act.sem_inc(sem("probs_T"), 1)
        act.wait_ge(sem("cmp_s_shifted"), due("cmp_s_shifted"))
        A(SCM[:, 0, :], SCM[:, 0, :], ACT.Exp, accum_out=small[0:64, 80:81]).then_inc(sem("cmp_s_exp"), 1)
        act.wait_ge(sem("cmp_s_exp"), sent("cmp_s_exp"))
        act.wait_ge(sem("scalar_unit_ready"), due("scalar_unit_ready"))
        u = next_unit()
        A(SW[:, 0:S], u[0:64, 0:S], ACT.Copy).then_inc(sem("scalar_steps"), 1)
        act.wait_ge(sem("scalar_steps"), sent("scalar_steps"))
        A(SW[:, S:S + 1], u[0:64, S + 1:S + 2], ACT.Copy).then_inc(sem("scalar_steps"), 1)
        act.wait_ge(sem("scalar_steps"), sent("scalar_steps"))
        A(SS[:, PAST:PAST + 1], u[0:64, S:S + 1], ACT.Copy).then_inc(sem("scalar_unit_free"), 1)
        act.wait_ge(sem("scalar_unit_free"), sent("scalar_unit_free"))
        act.sem_inc(sem("win_scores"), 1)
        act.wait_ge(sem("win_shift"), due("win_shift"))
        A(SW[:, :], SW[:, :], ACT.Exp, bias=small[0:64, 82:83], accum_out=small[0:64, 83:84]).then_inc(sem("win_exp"), 1)
        act.wait_ge(sem("win_exp"), sent("win_exp"))
        act.wait_ge(sem("sel_shift"), due("sel_shift"))
        A(SS[:, :], SS[:, :], ACT.Exp, bias=small[0:64, 84:85], accum_out=small[0:64, 85:86]).then_inc(sem("sel_exp"), 1)
        act.wait_ge(sem("sel_exp"), sent("sel_exp"))
        act.wait_ge(sem("scalar_unit_ready"), due("scalar_unit_ready"))
        u = next_unit()
        A(SPT.rearrange("p a b -> p (a b)"), u[:, :], ACT.Copy).then_inc(sem("scalar_unit_free"), 1)
        act.wait_ge(sem("scalar_unit_free"), sent("scalar_unit_free"))
        act.wait_ge(sem("scalar_unit_ready"), due("scalar_unit_ready"))
        u = next_unit()
        A(WPT.rearrange("p a b -> p (a b)"), u[:, 0:256], ACT.Copy).then_inc(sem("scalar_steps"), 1)
        act.wait_ge(sem("scalar_steps"), sent("scalar_steps"))
        A(CPT2, u[:, 256:320], ACT.Copy).then_inc(sem("scalar_steps"), 1)
        act.wait_ge(sem("scalar_steps"), sent("scalar_steps"))
        A(NEWT.rearrange("p a b -> p (a b)"), u[0:8, 320:448], ACT.Copy).then_inc(sem("scalar_unit_free"), 1)
        act.wait_ge(sem("scalar_unit_free"), sent("scalar_unit_free"))
        act.sem_inc(sem("sample_T"), 1)
        act.wait_ge(sem("centred_v"), due("centred_v"))
        for c in range(CONV_C):
            ins = A(GL[:, c, 0:T], CA[:, c, :], ACT.Square)
            if c < CONV_C - 1:
                ins.then_inc(sem("scalar_steps"), 1)
                act.wait_ge(sem("scalar_steps"), sent("scalar_steps"))
        ins.then_inc(sem("centred"), 1)
        act.wait_ge(sem("centred"), sent("centred"))
        act.wait_ge(sem("variance"), due("variance"))
        A(inv[:, :], inv[:, :], ACT.Sqrt).then_inc(sem("root"), 1)
        act.wait_ge(sem("root"), sent("root"))
        for c in range(CONV_C):
            act.wait_ge(sem("conv_normed"), due("conv_normed"))
            A(GL[:, c, 0:T], H[:, c, :], ACT.Sigmoid).then_inc(sem("conv_gate"), 1)
            act.wait_ge(sem("conv_gate"), sent("conv_gate"))

        def cross(l):
            act.wait_ge(sem("mem_in"), 16 * (l + 1))
            norm(MX, MEM)
            for c in range(16):
                act.wait_ge(sem("scalar_unit_ready"), due("scalar_unit_ready"))
                u = next_unit()
                A(MK[:, c, :].rearrange("p (a b) -> p a b", a=2), u[:, :].rearrange("p (a b) -> p a b", a=2)[:, :, 0:128], ACT.Copy).then_inc(sem("scalar_unit_free"), 1)
                act.wait_ge(sem("scalar_unit_free"), sent("scalar_unit_free"))
            act.sem_inc(sem("mkv_done"), 1)
            act.sem_inc(sem("mkv_ready"), 1)
            norm(X)
            for c in range(DC):
                act.wait_ge(sem("scalar_unit_ready"), due("scalar_unit_ready"))
                u = next_unit()
                A(split(QX[:, c, :]), halves(u), ACT.Copy, scale=0.0625).then_inc(sem("scalar_unit_free"), 1)
                act.wait_ge(sem("scalar_unit_free"), sent("scalar_unit_free"))
            act.sem_inc(sem("qx_ready"), 1)
            for t in range(2):
                act.wait_ge(sem("scalar_unit_ready"), due("scalar_unit_ready"))
                u = next_unit()
                A(MV[:, t, :], u[:, :], ACT.Copy).then_inc(sem("scalar_unit_free"), 1)
                act.wait_ge(sem("scalar_unit_free"), sent("scalar_unit_free"))
            act.sem_inc(sem("mv_ready"), 1)
            for qb in range(QB):
                act.wait_ge(sem("xmax"), due("xmax"))
                for h in range(4):
                    ins = A(XP[:, h, :], XP[:, h, :], ACT.Exp, bias=small[:, 96 + h:97 + h], accum_out=small[:, 100 + h:101 + h])
                    if h < 3:
                        ins.then_inc(sem("scalar_steps"), 1)
                        act.wait_ge(sem("scalar_steps"), sent("scalar_steps"))
                ins.then_inc(sem("xexp"), 1)
                act.wait_ge(sem("xexp"), sent("xexp"))
                act.wait_ge(sem("scalar_unit_ready"), due("scalar_unit_ready"))
                u = next_unit()
                A(XPT.rearrange("p a b -> p (a b)"), u[:, :], ACT.Copy).then_inc(sem("scalar_unit_free"), 1)
                act.wait_ge(sem("scalar_unit_free"), sent("scalar_unit_free"))
                act.sem_inc(sem("xprobs_T"), 1)
                act.wait_ge(sem("scalar_unit_ready"), due("scalar_unit_ready"))
                u = next_unit()
                A(AO[:, :, qb * P:(qb + 1) * P], u[:, :].rearrange("p (a b) -> p a b", a=8), ACT.Copy).then_inc(sem("scalar_unit_free"), 1)
                act.wait_ge(sem("scalar_unit_free"), sent("scalar_unit_free"))
            act.wait_ge(sem("xs_max"), due("xs_max"))
            A(XS, XS, ACT.Exp, bias=small[0:32, 104:105], accum_out=small[0:32, 105:106]).then_inc(sem("xs_exp"), 1)
            act.wait_ge(sem("xs_exp"), sent("xs_exp"))
            act.wait_ge(sem("residual"), due("residual"))
            norm(X)

        def gate(chunks):
            for c in range(chunks):
                act.wait_ge(sem("scalar_unit_ready"), due("scalar_unit_ready"))
                u = next_unit()
                A(split(HID[:, c, :]), halves(u), ACT.Silu).then_inc(sem("scalar_unit_free"), 1)
                act.wait_ge(sem("scalar_unit_free"), sent("scalar_unit_free"))
                act.sem_inc(sem("gate_parts"), 1)

        act.wait_ge(sem("residual"), due("residual"))
        cross(0)
        gate(DFF_C)
        act.wait_ge(sem("residual"), due("residual"))
        norm(X)
        act.wait_ge(sem("scalar_unit_ready"), due("scalar_unit_ready"))
        u = next_unit()
        A(split(FM[0:4, 0, :]), halves(u)[0:4], ACT.Identity, bias=gate_b[:, 0:1]).then_inc(sem("scalar_steps"), 1)
        act.wait_ge(sem("scalar_steps"), sent("scalar_steps"))
        A(split(FM[0:4, 1, :]), halves(u)[32:36], ACT.Identity, bias=gate_b[:, 1:2]).then_inc(sem("scalar_unit_free"), 1)
        act.wait_ge(sem("scalar_unit_free"), sent("scalar_unit_free"))
        act.sem_inc(sem("gates_raw"), 1)
        act.wait_ge(sem("gate_abs"), due("gate_abs"))
        A(FM[0:4, 2, :], FM[0:4, 2, :], ACT.Exp, scale=-1.0).then_inc(sem("gate_exp"), 1)
        act.wait_ge(sem("gate_exp"), sent("gate_exp"))
        act.wait_ge(sem("gate_one"), due("gate_one"))
        A(FM[0:4, 4, :], FM[0:4, 3, :], ACT.Ln).then_inc(sem("gate_ln"), 1)
        act.wait_ge(sem("gate_ln"), sent("gate_ln"))
        act.wait_ge(sem("gate_m"), due("gate_m"))
        A(FM[0:4, 5, 0:S], FM[0:4, 4, 0:S], ACT.Exp, scale=-1.0).then_inc(sem("gate_rows_exp"), 1)
        act.wait_ge(sem("gate_rows_exp"), sent("gate_rows_exp"))
        act.wait_ge(sem("scalar_unit_ready"), due("scalar_unit_ready"))
        u = next_unit()
        A(GC.rearrange("p a b -> p (a b)"), u[:, 0:16], ACT.Copy).then_inc(sem("scalar_unit_free"), 1)
        act.wait_ge(sem("scalar_unit_free"), sent("scalar_unit_free"))
        act.sem_inc(sem("gc_ready"), 1)
        for h in range(NH):
            if h:
                act.wait_ge(sem("head_over"), due("head_over"))
            for i, dst in enumerate((HQ, HK, HV, HO)):
                for c in range(2):
                    act.wait_ge(sem("scalar_unit_ready"), due("scalar_unit_ready"))
                    u = next_unit()
                    fn, sc_ = (ACT.Sigmoid, 1.0) if i == 3 else (ACT.Copy, 0.0625 if i == 1 else 1.0)
                    A(split(dst[:, c, :]), halves(u), fn, scale=sc_).then_inc(sem("scalar_unit_free"), 1)
                    act.wait_ge(sem("scalar_unit_free"), sent("scalar_unit_free"))
            act.sem_inc(sem("head_ready"), 1)
            act.sem_inc(sem("head_ready_v"), 1)
            for dst in (KTOK, VTK):
                act.wait_ge(sem("scalar_unit_ready"), due("scalar_unit_ready"))
                u = next_unit()
                A(dst.rearrange("p a b -> p (a b)"), u[:, :], ACT.Copy).then_inc(sem("scalar_unit_free"), 1)
                act.wait_ge(sem("scalar_unit_free"), sent("scalar_unit_free"))
            act.sem_inc(sem("tok_head"), 1)
            for sb_ in range(QB):
                w = S - sb_ * P
                act.wait_ge(sem("w_arg"), due("w_arg"))
                A(WRAW[:, 0:w], WRAW[:, 0:w], ACT.Exp).then_inc(sem("w_exp"), 1)
                act.wait_ge(sem("w_exp"), sent("w_exp"))
            act.wait_ge(sem("sm_arg"), due("sm_arg"))
            A(SM[:, 0:4], SM[:, 0:4], ACT.Exp).then_inc(sem("sm_exp"), 1)
            act.wait_ge(sem("sm_exp"), sent("sm_exp"))
            act.wait_ge(sem("gs_arg"), due("gs_arg"))
            A(SM[:, 8:32], SM[:, 8:32], ACT.Exp).then_inc(sem("gs_exp"), 1)
            act.wait_ge(sem("gs_exp"), sent("gs_exp"))
            act.wait_ge(sem("scalar_unit_ready"), due("scalar_unit_ready"))
            u = next_unit()
            if h:
                act.wait_ge(sem("c_prompt_out"), due("c_prompt_out"))
            A(NP_[:, h, :], u[:, 512:514], ACT.Copy).then_inc(sem("scalar_steps"), 1)
            act.wait_ge(sem("scalar_steps"), sent("scalar_steps"))
            for vc in range(2):
                ins = A(CO[:, vc, :], u[:, vc * 256:(vc + 1) * 256], ACT.Copy)
                if vc:
                    ins.then_inc(sem("scalar_unit_free"), 1)
                    act.wait_ge(sem("scalar_unit_free"), sent("scalar_unit_free"))
                else:
                    ins.then_inc(sem("scalar_steps"), 1)
                    act.wait_ge(sem("scalar_steps"), sent("scalar_steps"))
                act.sem_inc(sem("c_prompt_done"), 1)
            act.wait_ge(sem("head_h"), due("head_h"))
            A(sq[:, 0, :], HH[:, 0, :], ACT.Square).then_inc(sem("scalar_steps"), 1)
            act.wait_ge(sem("scalar_steps"), sent("scalar_steps"))
            A(sq[:, 1, :], HH[:, 1, :], ACT.Square).then_inc(sem("head_out"), 1)
            act.wait_ge(sem("head_out"), sent("head_out"))
            act.wait_ge(sem("mean_copied"), due("mean_copied"))
            A(inv[:, :], inv[:, :], ACT.Sqrt).then_inc(sem("root"), 1)
            act.wait_ge(sem("root"), sent("root"))
        act.wait_ge(sem("residual"), due("residual"))
        cross(1)
        act.wait_ge(sem("router_max"), due("router_max"))
        A(LOG[0:TB, :, :], LOG[0:TB, :, :], ACT.Exp).then_inc(sem("router_exp"), 1)
        act.wait_ge(sem("router_exp"), sent("router_exp"))
        for e in range(NE):
            act.wait_ge(sem("scalar_unit_ready"), due("scalar_unit_ready"))
            u = next_unit()
            A(COMB[:, e, 0:3 * TB], u[:, 0:3 * TB], ACT.Copy).then_inc(sem("scalar_steps"), 1)
            act.wait_ge(sem("scalar_steps"), sent("scalar_steps"))
            A(COMB[:, e, 3 * TB:T], u[:, 512:512 + 2 * TB], ACT.Copy).then_inc(sem("scalar_unit_free"), 1)
            act.wait_ge(sem("scalar_unit_free"), sent("scalar_unit_free"))
        act.sem_inc(sem("comb_bcast"), 1)
        for e in range(NE):
            gate(EXP_C)
        act.wait_ge(sem("residual"), due("residual"))
        norm(X)

    @block.vector
    def _(dve):
        due, sent = counter(), counter()
        next_unit = turns(psum_v)
        dve.sem_inc(sem("vector_unit_free"), UNITS)
        sent("vector_unit_free", UNITS)
        V = nc.vector

        def post(name):
            dve.sem_inc(sem(name), 1)

        def norm(src, dst, gain, n=T, bias=1e-6):
            dve.wait_ge(sem("vector_unit_ready"), due("vector_unit_ready"))
            u = next_unit()
            w = n // 2
            V.tensor_scalar(inv[:, 0:n].rearrange("p (a b) -> p a b", a=2),
                                    u[:, :].rearrange("p (a b) -> p a b", a=2)[:, :, 0:w], 1.0 / D, bias, ALU.mult, ALU.add).then_inc(sem("vector_unit_free"), 1)
            dve.wait_ge(sem("vector_unit_free"), sent("vector_unit_free"))
            dve.sem_inc(sem("mean_copied"), 1)
            dve.wait_ge(sem("root"), due("root"))
            V.reciprocal(inv[:, 0:n], inv[:, 0:n]).then_inc(sem("vector_steps"), 1)
            dve.wait_ge(sem("vector_steps"), sent("vector_steps"))
            for k in range(DC):
                V.scalar_tensor_tensor(dst[:, k, 0:n], src[:, k, 0:n], col(gain, k), inv[:, 0:n], ALU.mult, ALU.mult).then_inc(sem("vector_steps"), 1)
                dve.wait_ge(sem("vector_steps"), sent("vector_steps"))
            dve.sem_inc(sem("normed"), 1)

        def add_residual():
            for c in range(DC):
                dve.wait_ge(sem("vector_unit_ready"), due("vector_unit_ready"))
                u = next_unit()
                V.tensor_tensor(split(X[:, c, :]), split(X[:, c, :]), halves(u), ALU.add).then_inc(sem("vector_unit_free"), 1)
                dve.wait_ge(sem("vector_unit_free"), sent("vector_unit_free"))
            dve.sem_inc(sem("residual"), 1)

        def convolve(c, first, end):
            ext = GL[:, c, GLP:GLW].rearrange("p (b w) -> p b w", b=NB)
            for j in range(first, end):
                wj = col("conv_w", c * CONV_W + j)
                for dst, src in ((CA[:, c, 0:S], GL[:, c, j:j + S]), (CA[:, c, S:T], ext[:, :, j])):
                    if j == 0:
                        V.tensor_scalar(dst, src, wj, col("conv_b", c), ALU.mult, ALU.add).then_inc(sem("vector_steps"), 1)
                        dve.wait_ge(sem("vector_steps"), sent("vector_steps"))
                    else:
                        V.scalar_tensor_tensor(dst, src, wj, dst, ALU.mult, ALU.add).then_inc(sem("vector_steps"), 1)
                        dve.wait_ge(sem("vector_steps"), sent("vector_steps"))

        V.memset(ones[:, :], 1.0).then_inc(sem("vector_steps"), 1)
        dve.wait_ge(sem("vector_steps"), sent("vector_steps"))
        dve.sem_inc(sem("ones_set"), 1)
        dve.wait_ge(sem("x_in"), 16)
        dve.wait_ge(sem("consts_in"), 16 * (len(const_loads) + 2))
        norm(X, H, "mix0")
        dve.wait_ge(sem("conv_in"), 16 * CONV_C)
        V.memset(GL[:, :, 0:CONV_W - 1], 0.0).then_inc(sem("vector_steps"), 1)
        dve.wait_ge(sem("vector_steps"), sent("vector_steps"))
        for c in range(CONV_C):
            dve.wait_ge(sem("glu_parts"), due("glu_parts"))
            V.tensor_tensor(GL[:, c, CONV_W - 1:GLP], CA[:, c, 0:S], sq[:, 0, 0:S], ALU.mult).then_inc(sem("vector_steps"), 1)
            dve.wait_ge(sem("vector_steps"), sent("vector_steps"))
            ext = GL[:, c, GLP:GLW].rearrange("p (b w) -> p b w", b=NB)
            V.tensor_tensor(ext[:, :, CONV_W - 1], CA[:, c, S:T], sq[:, 0, S:T], ALU.mult).then_inc(sem("glu_done"), 1)
            dve.wait_ge(sem("glu_done"), sent("glu_done"))
        for c in range(6):
            dve.wait_ge(sem("vector_unit_ready"), due("vector_unit_ready"))
            u = next_unit()
            V.tensor_copy(split(KV[:, c, :]), halves(u)).then_inc(sem("vector_unit_free"), 1)
            dve.wait_ge(sem("vector_unit_free"), sent("vector_unit_free"))
        dve.sem_inc(sem("kv_done"), 1)
        dve.sem_inc(sem("kv_ready"), 1)
        dve.wait_ge(sem("vector_unit_ready"), due("vector_unit_ready"))
        u = next_unit()
        V.tensor_copy(PEB, u[:, 0:2]).then_inc(sem("vector_unit_free"), 1)
        dve.wait_ge(sem("vector_unit_free"), sent("vector_unit_free"))
        dve.wait_ge(sem("vector_unit_ready"), due("vector_unit_ready"))
        u = next_unit()
        for v in range(2):
            ins = V.tensor_scalar(KC[:, v, S:S + 16], u[:, v * 16:v * 16 + 16], PEB[:, v:v + 1], None, ALU.add)
            if v == 0:
                ins.then_inc(sem("vector_steps"), 1)
                dve.wait_ge(sem("vector_steps"), sent("vector_steps"))
            else:
                ins.then_inc(sem("vector_unit_free"), 1)
                dve.wait_ge(sem("vector_unit_free"), sent("vector_unit_free"))
        for b in range(NB):
            convolve(b // 2, (b % 2) * 16, CONV_W if b % 2 else 16)
            dve.wait_ge(sem("vector_unit_ready"), due("vector_unit_ready"))
            u = next_unit()
            for v in range(2):
                ins = V.tensor_scalar(KC[:, v, b * 64:(b + 1) * 64], u[:, v * 64:v * 64 + 64], PEB[:, v:v + 1], None, ALU.add)
                if v == 0:
                    ins.then_inc(sem("vector_steps"), 1)
                    dve.wait_ge(sem("vector_steps"), sent("vector_steps"))
                else:
                    ins.then_inc(sem("vector_unit_free"), 1)
                    dve.wait_ge(sem("vector_unit_free"), sent("vector_unit_free"))
        dve.sem_inc(sem("kc_ready"), 1)
        dve.sem_inc(sem("conv_done"), 1)
        dve.wait_ge(sem("toep_back"), 16 * 8)
        dve.wait_ge(sem("tok_ready_v"), due("tok_ready_v"))
        for qb in range(QB):
            off, wc, w = 384 - P * qb, 4 * (qb + 1), P * (qb + 1)
            dve.wait_ge(sem("vector_unit_ready"), due("vector_unit_ready"))
            u = next_unit()
            for k in range(2):
                got = u[:, 512 * k:512 * k + 64].rearrange("p (a b) -> p a b", a=4)[:, :, 0:wc]
                ins = V.tensor_tensor(CP[:, 4 * k:4 * k + 4, 0:wc], got, E[:, 4 * k:4 * k + 4, off + CMP - 1:off + CMP * wc:CMP], ALU.add)
                if k == 0:
                    ins.then_inc(sem("vector_steps"), 1)
                    dve.wait_ge(sem("vector_steps"), sent("vector_steps"))
                else:
                    ins.then_inc(sem("vector_unit_free"), 1)
                    dve.wait_ge(sem("vector_unit_free"), sent("vector_unit_free"))
            V.tensor_reduce(small[:, 32:40], CP[:, :, 0:wc], AX, ALU.max).then_inc(sem("vector_steps"), 1)
            dve.wait_ge(sem("vector_steps"), sent("vector_steps"))
            V.tensor_tensor(CP[:, :, 0:wc], CP[:, :, 0:wc], small[:, 32:40].rearrange("p (a b) -> p a b", b=1).broadcast_to([P, 8, wc]), ALU.subtract).then_inc(sem("cmp_shifted"), 1)
            dve.wait_ge(sem("cmp_shifted"), sent("cmp_shifted"))
            dve.wait_ge(sem("cmp_exp"), due("cmp_exp"))
            V.tensor_reduce(small[:, 40:48], CP[:, :, 0:wc], AX, ALU.add).then_inc(sem("vector_steps"), 1)
            dve.wait_ge(sem("vector_steps"), sent("vector_steps"))
            V.reciprocal(small[:, 40:48], small[:, 40:48]).then_inc(sem("vector_steps"), 1)
            dve.wait_ge(sem("vector_steps"), sent("vector_steps"))
            if qb == 0:
                V.tensor_scalar(small[:, 40:48], small[:, 40:48], rowok[:, 0:1], None, ALU.mult).then_inc(sem("vector_steps"), 1)
                dve.wait_ge(sem("vector_steps"), sent("vector_steps"))
            gates = GTOK[:, qb, :].rearrange("p (h c) -> p h c", c=3)
            V.tensor_tensor(small[:, 40:48], small[:, 40:48], gates[:, :, 0], ALU.mult).then_inc(sem("vector_steps"), 1)
            dve.wait_ge(sem("vector_steps"), sent("vector_steps"))
            V.tensor_tensor(CP[:, :, 0:wc], CP[:, :, 0:wc], small[:, 40:48].rearrange("p (a b) -> p a b", b=1).broadcast_to([P, 8, wc]), ALU.mult).then_inc(sem("vector_steps"), 1)
            dve.wait_ge(sem("vector_steps"), sent("vector_steps"))
            dve.sem_inc(sem("cmp_probs"), 1)
            for k in range(2):
                for gp in range(2):
                    for br in range(2):
                        h = 4 * k + 2 * gp
                        dve.wait_ge(sem("vector_unit_ready"), due("vector_unit_ready"))
                        u = next_unit()
                        s3 = u[:, :].rearrange("p (a b) -> p a b", a=2)[:, :, 0:w]
                        V.tensor_tensor(SC[:, :, 0:w], s3, E[:, h:h + 2, off:off + w], ALU.add).then_inc(sem("vector_unit_free"), 1)
                        dve.wait_ge(sem("vector_unit_free"), sent("vector_unit_free"))
                        V.tensor_reduce(small[:, 64:66], SC[:, :, 0:w], AX, ALU.max, negate=True).then_inc(sem("vector_steps"), 1)
                        dve.wait_ge(sem("vector_steps"), sent("vector_steps"))
                        dve.sem_inc(sem("shifted"), 1)
                        dve.wait_ge(sem("exped"), due("exped"))
                        V.reciprocal(small[:, 70:72], small[:, 68:70]).then_inc(sem("vector_steps"), 1)
                        dve.wait_ge(sem("vector_steps"), sent("vector_steps"))
                        V.tensor_tensor(small[:, 70:72], small[:, 70:72], gates[:, h:h + 2, 1 + br], ALU.mult).then_inc(sem("vector_steps"), 1)
                        dve.wait_ge(sem("vector_steps"), sent("vector_steps"))
                        for g in range(2):
                            V.tensor_scalar(SC[:, g, 0:w], SC[:, g, 0:w], small[:, 70 + g:71 + g], None, ALU.mult).then_inc(sem("vector_steps"), 1)
                            dve.wait_ge(sem("vector_steps"), sent("vector_steps"))
                        dve.sem_inc(sem("probs"), 1)
                        dve.wait_ge(sem("vector_unit_ready"), due("vector_unit_ready"))
                        u = next_unit()
                        dst = H[64 * k:64 * k + 64, 4 + 2 * gp:6 + 2 * gp, qb * P:(qb + 1) * P]
                        got = u[64 * k:64 * k + 64, 0:256].rearrange("p (a b) -> p a b", a=2)
                        if br == 0:
                            V.tensor_copy(dst, got).then_inc(sem("vector_unit_free"), 1)
                            dve.wait_ge(sem("vector_unit_free"), sent("vector_unit_free"))
                        else:
                            V.tensor_tensor(dst, dst, got, ALU.add).then_inc(sem("vector_unit_free"), 1)
                            dve.wait_ge(sem("vector_unit_free"), sent("vector_unit_free"))
        V.memset(QP[:, :, :], 0.0).then_inc(sem("vector_steps"), 1)
        dve.wait_ge(sem("vector_steps"), sent("vector_steps"))
        for k in range(2):
            for b in range(NB):
                V.tensor_copy(QP[64 * k:64 * k + 64, b, b * 8 + 4 * k:b * 8 + 4 * k + 4], Q[64 * k:64 * k + 64, :, S + b]).then_inc(sem("vector_steps"), 1)
                dve.wait_ge(sem("vector_steps"), sent("vector_steps"))
        dve.sem_inc(sem("qp_ready"), 1)
        dve.sem_inc(sem("attention_over"), 1)
        dve.wait_ge(sem("vector_unit_ready"), due("vector_unit_ready"))
        u = next_unit()
        V.tensor_reduce(small[0:64, 78:79], u[0:64, 0:64], AX, ALU.max).then_inc(sem("vector_steps"), 1)
        dve.wait_ge(sem("vector_steps"), sent("vector_steps"))
        V.tensor_scalar(SCM[:, 0, :], u[0:64, 0:64], small[0:64, 78:79], None, ALU.subtract).then_inc(sem("vector_unit_free"), 1)
        dve.wait_ge(sem("vector_unit_free"), sent("vector_unit_free"))
        dve.sem_inc(sem("cmp_s_shifted"), 1)
        dve.wait_ge(sem("cmp_s_exp"), due("cmp_s_exp"))
        dve.wait_ge(sem("gates_rows"), 16)
        V.reciprocal(small[0:64, 81:82], small[0:64, 80:81]).then_inc(sem("vector_steps"), 1)
        dve.wait_ge(sem("vector_steps"), sent("vector_steps"))
        V.tensor_scalar(SCM[:, 1, :], SCM[:, 0, :], small[0:64, 81:82], None, ALU.mult).then_inc(sem("vector_steps"), 1)
        dve.wait_ge(sem("vector_steps"), sent("vector_steps"))
        dve.sem_inc(sem("cmp_s"), 1)
        dve.wait_ge(sem("vector_unit_ready"), due("vector_unit_ready"))
        u = next_unit()
        V.memset(SCORE, 0.0).then_inc(sem("vector_steps"), 1)
        dve.wait_ge(sem("vector_steps"), sent("vector_steps"))
        V.tensor_copy(SCORE[:, 2, 0:32], u[0:16, 0:64:2]).then_inc(sem("vector_steps"), 1)
        dve.wait_ge(sem("vector_steps"), sent("vector_steps"))
        V.tensor_tensor(SCORE[:, 0, 0:32], SCORE[:, 2, 0:32], u[0:16, 1:64:2], ALU.add).then_inc(sem("vector_unit_free"), 1)
        dve.wait_ge(sem("vector_unit_free"), sent("vector_unit_free"))
        V.memset(SCORE[:, 0, 0:1], 1e4).then_inc(sem("vector_steps"), 1)
        dve.wait_ge(sem("vector_steps"), sent("vector_steps"))
        V.memset(SCORE[:, 0, 31:33], 1e4).then_inc(sem("vector_steps"), 1)
        dve.wait_ge(sem("vector_steps"), sent("vector_steps"))
        for r in range(2):
            V.max(TOP, SCORE[:, r, 0:33]).then_inc(sem("vector_steps"), 1)
            dve.wait_ge(sem("vector_steps"), sent("vector_steps"))
            V.match_replace(SCORE[:, r + 1, 0:33], TOP, SCORE[:, r, 0:33], -2.0).then_inc(sem("vector_steps"), 1)
            dve.wait_ge(sem("vector_steps"), sent("vector_steps"))
        V.tensor_scalar(SELN[:, 0:33], SCORE[:, 2, 0:33], -1.5, NEG, ALU.is_gt, ALU.mult).then_inc(sem("vector_steps"), 1)
        dve.wait_ge(sem("vector_steps"), sent("vector_steps"))
        dve.sem_inc(sem("sel_mask"), 1)
        for i in range(2):
            V.tensor_scalar(SCM[:, i, :], SCM[:, 1, :], SG[:, 0:1], rowok[0:64, 1 + i:2 + i], ALU.mult, ALU.mult).then_inc(sem("vector_steps"), 1)
            dve.wait_ge(sem("vector_steps"), sent("vector_steps"))
        dve.wait_ge(sem("win_scores"), due("win_scores"))
        V.memset(SW[:, 0:1], NEG).then_inc(sem("vector_steps"), 1)
        dve.wait_ge(sem("vector_steps"), sent("vector_steps"))
        V.tensor_reduce(small[0:64, 82:83], SW, AX, ALU.max, negate=True).then_inc(sem("vector_steps"), 1)
        dve.wait_ge(sem("vector_steps"), sent("vector_steps"))
        dve.sem_inc(sem("win_shift"), 1)
        dve.wait_ge(sem("win_exp"), due("win_exp"))
        V.reciprocal(small[0:64, 86:87], small[0:64, 83:84]).then_inc(sem("vector_steps"), 1)
        dve.wait_ge(sem("vector_steps"), sent("vector_steps"))
        V.tensor_scalar(SW, SW, small[0:64, 86:87], SG[:, 2:3], ALU.mult, ALU.mult).then_inc(sem("vector_steps"), 1)
        dve.wait_ge(sem("vector_steps"), sent("vector_steps"))
        V.tensor_scalar(NEWP[:, 1, :], own[:, :], SW[:, S:S + 1], None, ALU.mult).then_inc(sem("vector_steps"), 1)
        dve.wait_ge(sem("vector_steps"), sent("vector_steps"))
        for i in range(2):
            dve.wait_ge(sem("vector_unit_ready"), due("vector_unit_ready"))
            u = next_unit()
            V.tensor_copy(SS[:, i * 1024:(i + 1) * 1024], u[0:64, :]).then_inc(sem("vector_unit_free"), 1)
            dve.wait_ge(sem("vector_unit_free"), sent("vector_unit_free"))
        V.tensor_reduce(small[0:64, 84:85], SS, AX, ALU.max, negate=True).then_inc(sem("vector_steps"), 1)
        dve.wait_ge(sem("vector_steps"), sent("vector_steps"))
        dve.sem_inc(sem("sel_shift"), 1)
        dve.wait_ge(sem("sel_exp"), due("sel_exp"))
        V.reciprocal(small[0:64, 87:88], small[0:64, 85:86]).then_inc(sem("vector_steps"), 1)
        dve.wait_ge(sem("vector_steps"), sent("vector_steps"))
        V.tensor_scalar(SS, SS, small[0:64, 87:88], SG[:, 1:2], ALU.mult, ALU.mult).then_inc(sem("vector_steps"), 1)
        dve.wait_ge(sem("vector_steps"), sent("vector_steps"))
        V.tensor_scalar(NEWP[:, 0, :], own[:, :], SS[:, PAST:PAST + 1], None, ALU.mult).then_inc(sem("vector_steps"), 1)
        dve.wait_ge(sem("vector_steps"), sent("vector_steps"))
        dve.sem_inc(sem("sel_probs"), 1)
        dve.sem_inc(sem("win_probs"), 1)
        dve.wait_ge(sem("vector_unit_ready"), due("vector_unit_ready"))
        u = next_unit()
        for k in range(2):
            dst = H[64 * k:64 * k + 64, 4:8, S:T].rearrange("p g b -> p b g")
            got = [u[64 * k:64 * k + 64, lo:lo + 64].rearrange("p (b k g) -> p b k g", k=2, g=4)[:, :, k, :] for lo in (0, 512)]
            V.tensor_copy(dst, got[0]).then_inc(sem("vector_steps"), 1)
            dve.wait_ge(sem("vector_steps"), sent("vector_steps"))
            ins = V.tensor_tensor(dst, dst, got[1], ALU.add)
            if k == 0:
                ins.then_inc(sem("vector_steps"), 1)
                dve.wait_ge(sem("vector_steps"), sent("vector_steps"))
            else:
                ins.then_inc(sem("vector_unit_free"), 1)
                dve.wait_ge(sem("vector_unit_free"), sent("vector_unit_free"))
        dve.wait_ge(sem("vector_unit_ready"), due("vector_unit_ready"))
        u = next_unit()
        V.tensor_scalar(split(inv[:, :]), halves(u), 1.0 / 512, None, ALU.mult).then_inc(sem("vector_unit_free"), 1)
        dve.wait_ge(sem("vector_unit_free"), sent("vector_unit_free"))
        for c in range(CONV_C):
            V.tensor_tensor(CA[:, c, :], CA[:, c, :], inv[:, :], ALU.subtract).then_inc(sem("vector_steps"), 1)
            dve.wait_ge(sem("vector_steps"), sent("vector_steps"))
        dve.sem_inc(sem("centred_v"), 1)
        dve.wait_ge(sem("vector_unit_ready"), due("vector_unit_ready"))
        u = next_unit()
        V.tensor_scalar(split(inv[:, :]), halves(u), 1.0 / 512, 1e-5, ALU.mult, ALU.add).then_inc(sem("vector_unit_free"), 1)
        dve.wait_ge(sem("vector_unit_free"), sent("vector_unit_free"))
        dve.sem_inc(sem("variance"), 1)
        dve.wait_ge(sem("root"), due("root"))
        V.reciprocal(inv[:, :], inv[:, :]).then_inc(sem("vector_steps"), 1)
        dve.wait_ge(sem("vector_steps"), sent("vector_steps"))
        for c in range(CONV_C):
            V.scalar_tensor_tensor(H[:, c, :], CA[:, c, :], col("ln_g", c), inv[:, :], ALU.mult, ALU.mult).then_inc(sem("vector_steps"), 1)
            dve.wait_ge(sem("vector_steps"), sent("vector_steps"))
            V.tensor_scalar(H[:, c, :], H[:, c, :], col("ln_b", c), None, ALU.add).then_inc(sem("vector_steps"), 1)
            dve.wait_ge(sem("vector_steps"), sent("vector_steps"))
            dve.sem_inc(sem("conv_normed"), 1)
        for c in range(CONV_C):
            dve.wait_ge(sem("conv_gate"), due("conv_gate"))
            V.tensor_tensor(H[:, c, :], H[:, c, :], GL[:, c, 0:T], ALU.mult).then_inc(sem("vector_steps"), 1)
            dve.wait_ge(sem("vector_steps"), sent("vector_steps"))
        dve.sem_inc(sem("mix_ready"), 1)
        add_residual()
        dve.sem_inc(sem("mixer_over"), 1)

        def cross(l):
            dve.wait_ge(sem("mem_in"), 16 * (l + 1))
            norm(MX, MH, f"mem{l}", MEM)
            norm(X, H, f"x{l}")
            for qb in range(QB):
                dve.wait_ge(sem("vector_unit_ready"), due("vector_unit_ready"))
                u = next_unit()
                V.tensor_copy(XP.rearrange("p a b -> p (a b)"), u[:, :]).then_inc(sem("vector_unit_free"), 1)
                dve.wait_ge(sem("vector_unit_free"), sent("vector_unit_free"))
                V.tensor_reduce(small[:, 96:100], XP, AX, ALU.max, negate=True).then_inc(sem("vector_steps"), 1)
                dve.wait_ge(sem("vector_steps"), sent("vector_steps"))
                dve.sem_inc(sem("xmax"), 1)
                dve.wait_ge(sem("xexp"), due("xexp"))
                V.reciprocal(small[:, 100:104], small[:, 100:104]).then_inc(sem("vector_steps"), 1)
                dve.wait_ge(sem("vector_steps"), sent("vector_steps"))
                for h in range(4):
                    V.tensor_scalar(XP[:, h, :], XP[:, h, :], small[:, 100 + h:101 + h], None, ALU.mult).then_inc(sem("vector_steps"), 1)
                    dve.wait_ge(sem("vector_steps"), sent("vector_steps"))
                dve.sem_inc(sem("xprobs"), 1)
            V.memset(QXP[:, :, :], 0.0).then_inc(sem("vector_steps"), 1)
            dve.wait_ge(sem("vector_steps"), sent("vector_steps"))
            dve.wait_ge(sem("qx_ready"), due("qx_ready"))
            for b in range(NB):
                for h in range(4):
                    ins = V.tensor_copy(QXP[:, b * DC + 2 * h:b * DC + 2 * h + 2, 4 * b + h], QX[:, 2 * h:2 * h + 2, S + b])
                    ins.then_inc(sem("vector_steps"), 1)
                    dve.wait_ge(sem("vector_steps"), sent("vector_steps"))
            dve.sem_inc(sem("qxp_ready"), 1)
            dve.wait_ge(sem("vector_unit_ready"), due("vector_unit_ready"))
            u = next_unit()
            V.tensor_copy(XS, u[0:32, 0:MEM]).then_inc(sem("vector_unit_free"), 1)
            dve.wait_ge(sem("vector_unit_free"), sent("vector_unit_free"))
            V.tensor_reduce(small[0:32, 104:105], XS, AX, ALU.max, negate=True).then_inc(sem("vector_steps"), 1)
            dve.wait_ge(sem("vector_steps"), sent("vector_steps"))
            dve.sem_inc(sem("xs_max"), 1)
            dve.wait_ge(sem("xs_exp"), due("xs_exp"))
            V.reciprocal(small[0:32, 105:106], small[0:32, 105:106]).then_inc(sem("vector_steps"), 1)
            dve.wait_ge(sem("vector_steps"), sent("vector_steps"))
            V.tensor_scalar(XS, XS, small[0:32, 105:106], None, ALU.mult).then_inc(sem("vector_steps"), 1)
            dve.wait_ge(sem("vector_steps"), sent("vector_steps"))
            dve.sem_inc(sem("xs_probs"), 1)
            dve.wait_ge(sem("vector_unit_ready"), due("vector_unit_ready"))
            u = next_unit()
            V.tensor_copy(XST.rearrange("p a b -> p (a b)"), u[:, 0:64]).then_inc(sem("vector_unit_free"), 1)
            dve.wait_ge(sem("vector_unit_free"), sent("vector_unit_free"))
            dve.sem_inc(sem("xs_T"), 1)
            dve.wait_ge(sem("vector_unit_ready"), due("vector_unit_ready"))
            u = next_unit()
            V.tensor_copy(AO[:, :, S:T], u[:, 0:64].rearrange("p (a b) -> p a b", a=8)).then_inc(sem("vector_unit_free"), 1)
            dve.wait_ge(sem("vector_unit_free"), sent("vector_unit_free"))
            dve.wait_ge(sem("mkv_out"), due("mkv_out"))
            dve.sem_inc(sem("ao_ready"), 1)
            add_residual()
            norm(X, H, f"ffn{l}")

        def up(chunks):
            for c in range(chunks):
                dve.wait_ge(sem("gate_parts"), due("gate_parts"))
                dve.wait_ge(sem("vector_unit_ready"), due("vector_unit_ready"))
                u = next_unit()
                V.tensor_tensor(split(HID[:, c, :]), split(HID[:, c, :]), halves(u), ALU.mult).then_inc(sem("vector_unit_free"), 1)
                dve.wait_ge(sem("vector_unit_free"), sent("vector_unit_free"))
            dve.sem_inc(sem("hidden"), 1)

        cross(0)
        up(DFF_C)
        add_residual()
        dve.sem_inc(sem("ffn_over"), 1)

        norm(X, H, "mix1")
        dve.wait_ge(sem("gates_raw"), due("gates_raw"))
        ig, lf, e_, u_, l_, x_ = (FM[0:4, i, :] for i in range(6))
        V.tensor_scalar(u_, lf, -1.0, None, ALU.mult).then_inc(sem("vector_steps"), 1)
        dve.wait_ge(sem("vector_steps"), sent("vector_steps"))
        V.tensor_tensor(e_, lf, u_, ALU.max).then_inc(sem("vector_steps"), 1)
        dve.wait_ge(sem("vector_steps"), sent("vector_steps"))
        dve.sem_inc(sem("gate_abs"), 1)
        dve.wait_ge(sem("gate_exp"), due("gate_exp"))
        V.tensor_scalar(u_, e_, 1.0, None, ALU.add).then_inc(sem("vector_steps"), 1)
        dve.wait_ge(sem("vector_steps"), sent("vector_steps"))
        dve.sem_inc(sem("gate_one"), 1)
        V.tensor_scalar(x_, u_, -1.0, None, ALU.add).then_inc(sem("vector_steps"), 1)
        dve.wait_ge(sem("vector_steps"), sent("vector_steps"))
        V.tensor_tensor(e_, e_, x_, ALU.subtract).then_inc(sem("vector_steps"), 1)
        dve.wait_ge(sem("vector_steps"), sent("vector_steps"))
        dve.wait_ge(sem("gate_ln"), due("gate_ln"))
        V.reciprocal(x_, u_).then_inc(sem("vector_steps"), 1)
        dve.wait_ge(sem("vector_steps"), sent("vector_steps"))
        V.tensor_tensor(e_, e_, x_, ALU.mult).then_inc(sem("vector_steps"), 1)
        dve.wait_ge(sem("vector_steps"), sent("vector_steps"))
        V.tensor_tensor(l_, l_, e_, ALU.add).then_inc(sem("vector_steps"), 1)
        dve.wait_ge(sem("vector_steps"), sent("vector_steps"))
        V.tensor_scalar(lf, lf, 0.0, None, ALU.min).then_inc(sem("vector_steps"), 1)
        dve.wait_ge(sem("vector_steps"), sent("vector_steps"))
        V.tensor_tensor(lf, lf, l_, ALU.subtract).then_inc(sem("vector_steps"), 1)
        dve.wait_ge(sem("vector_steps"), sent("vector_steps"))
        V.memset(x_[:, 0:S], 0.0).then_inc(sem("vector_steps"), 1)
        dve.wait_ge(sem("vector_steps"), sent("vector_steps"))
        V.tensor_tensor_scan(l_[:, 0:S], lf[:, 0:S], x_[:, 0:S], 0.0, ALU.add, ALU.add).then_inc(sem("vector_steps"), 1)
        dve.wait_ge(sem("vector_steps"), sent("vector_steps"))
        V.tensor_tensor(e_[:, 0:S], ig[:, 0:S], l_[:, 0:S], ALU.subtract).then_inc(sem("vector_steps"), 1)
        dve.wait_ge(sem("vector_steps"), sent("vector_steps"))
        V.tensor_tensor_scan(u_[:, 0:S], e_[:, 0:S], x_[:, 0:S], NEG, ALU.max, ALU.add).then_inc(sem("vector_steps"), 1)
        dve.wait_ge(sem("vector_steps"), sent("vector_steps"))
        V.tensor_tensor(l_[:, 0:S], l_[:, 0:S], u_[:, 0:S], ALU.add).then_inc(sem("vector_steps"), 1)
        dve.wait_ge(sem("vector_steps"), sent("vector_steps"))
        V.tensor_copy(MMP[0:4, 0:1], l_[:, S - 1:S]).then_inc(sem("vector_steps"), 1)
        dve.wait_ge(sem("vector_steps"), sent("vector_steps"))
        dve.sem_inc(sem("gate_m"), 1)
        dve.wait_ge(sem("gate_rows_exp"), due("gate_rows_exp"))
        dve.wait_ge(sem("state_in"), 32)
        dve.sem_inc(sem("gate_rows"), 1)
        dve.wait_ge(sem("gc_ready"), due("gc_ready"))
        for h in range(NH):
            dve.wait_ge(sem("head_ready_v"), due("head_ready_v"))
            dve.wait_ge(sem("tok_head"), due("tok_head"))
            dve.wait_ge(sem("vector_unit_ready"), due("vector_unit_ready"))
            u = next_unit()
            V.tensor_copy(MB, u[:, 0:S]).then_inc(sem("vector_steps"), 1)
            dve.wait_ge(sem("vector_steps"), sent("vector_steps"))
            V.tensor_copy(GS[:, 0:2, :].rearrange("p a b -> p (a b)"), u[:, S:S + 16]).then_inc(sem("vector_unit_free"), 1)
            dve.wait_ge(sem("vector_unit_free"), sent("vector_unit_free"))
            for sb_ in range(QB):
                w = S - sb_ * P
                V.tensor_scalar(WRAW[:, 0:w], MB[:, sb_ * P:S], GC[:, sb_, h:h + 1], -1.0, ALU.subtract, ALU.mult).then_inc(sem("vector_steps"), 1)
                dve.wait_ge(sem("vector_steps"), sent("vector_steps"))
                V.tensor_scalar(WRAW[:, 0:w], WRAW[:, 0:w], 0.0, None, ALU.min).then_inc(sem("vector_steps"), 1)
                dve.wait_ge(sem("vector_steps"), sent("vector_steps"))
                dve.sem_inc(sem("w_arg"), 1)
                dve.wait_ge(sem("w_exp"), due("w_exp"))
                V.tensor_tensor(WRAW[:, 0:P], WRAW[:, 0:P], tri[:, :], ALU.mult).then_inc(sem("vector_steps"), 1)
                dve.wait_ge(sem("vector_steps"), sent("vector_steps"))
                dve.wait_ge(sem("vector_unit_ready"), due("vector_unit_ready"))
                u = next_unit()
                V.tensor_tensor(ST[:, sb_, sb_ * P:S], WRAW[:, 0:w], u[:, 0:w], ALU.mult).then_inc(sem("vector_unit_free"), 1)
                dve.wait_ge(sem("vector_unit_free"), sent("vector_unit_free"))
            dve.sem_inc(sem("st_ready"), 1)
            V.tensor_scalar(SM[:, 0:4], GC[:, :, h], MB[:, S - 1:S], None, ALU.subtract).then_inc(sem("vector_steps"), 1)
            dve.wait_ge(sem("vector_steps"), sent("vector_steps"))
            dve.sem_inc(sem("sm_arg"), 1)
            dve.wait_ge(sem("sm_exp"), due("sm_exp"))
            for g in range(QB):
                V.tensor_scalar(VW[:, g, :], VTK[:, g, :], SM[:, g:g + 1], None, ALU.mult).then_inc(sem("vector_steps"), 1)
                dve.wait_ge(sem("vector_steps"), sent("vector_steps"))
            dve.sem_inc(sem("vw_ready"), 1)
            gi, gf, inter, mt = (GS[:, i, :] for i in range(4))
            V.tensor_tensor(inter, gf, ML[:, :].rearrange("p (b h) -> p b h", h=NH)[:, :, h], ALU.add).then_inc(sem("vector_steps"), 1)
            dve.wait_ge(sem("vector_steps"), sent("vector_steps"))
            V.tensor_tensor(mt, inter, gi, ALU.max).then_inc(sem("vector_steps"), 1)
            dve.wait_ge(sem("vector_steps"), sent("vector_steps"))
            V.tensor_copy(SMO[:, h * NB:(h + 1) * NB], mt).then_inc(sem("vector_steps"), 1)
            dve.wait_ge(sem("vector_steps"), sent("vector_steps"))
            V.tensor_tensor(SM[:, 8:16], inter, mt, ALU.subtract).then_inc(sem("vector_steps"), 1)
            dve.wait_ge(sem("vector_steps"), sent("vector_steps"))
            V.tensor_tensor(SM[:, 16:24], gi, mt, ALU.subtract).then_inc(sem("vector_steps"), 1)
            dve.wait_ge(sem("vector_steps"), sent("vector_steps"))
            V.tensor_scalar(SM[:, 24:32], mt, -1.0, None, ALU.mult).then_inc(sem("vector_steps"), 1)
            dve.wait_ge(sem("vector_steps"), sent("vector_steps"))
            dve.sem_inc(sem("gs_arg"), 1)
            dve.wait_ge(sem("gs_exp"), due("gs_exp"))
            for part in range(2):
                dve.wait_ge(sem("vector_unit_ready"), due("vector_unit_ready"))
                u = next_unit()
                V.tensor_copy(HH[:, part, 0:S], u[:, 0:S]).then_inc(sem("vector_unit_free"), 1)
                dve.wait_ge(sem("vector_unit_free"), sent("vector_unit_free"))
            dve.wait_ge(sem("vector_unit_ready"), due("vector_unit_ready"))
            u = next_unit()
            V.tensor_scalar(DEN[:, 0:S], u[:, 0:S], -1.0, None, ALU.mult).then_inc(sem("vector_steps"), 1)
            dve.wait_ge(sem("vector_steps"), sent("vector_steps"))
            V.tensor_tensor(DEN[:, 0:S], DEN[:, 0:S], u[:, 0:S], ALU.max).then_inc(sem("vector_unit_free"), 1)
            dve.wait_ge(sem("vector_unit_free"), sent("vector_unit_free"))
            dve.wait_ge(sem("vector_unit_ready"), due("vector_unit_ready"))
            u = next_unit()
            V.tensor_tensor(DEN[:, 0:S], DEN[:, 0:S], u[:, 0:S], ALU.max).then_inc(sem("vector_unit_free"), 1)
            dve.wait_ge(sem("vector_unit_free"), sent("vector_unit_free"))
            V.reciprocal(DEN[:, 0:S], DEN[:, 0:S]).then_inc(sem("vector_steps"), 1)
            dve.wait_ge(sem("vector_steps"), sent("vector_steps"))
            dve.wait_ge(sem("c_in"), 16 * (h + 1))
            decay, inp = SM[:, 8:16], SM[:, 16:24]
            for c in range(2):
                V.tensor_tensor(SN[:, h, c, :], SN[:, h, c, :], decay, ALU.mult).then_inc(sem("vector_steps"), 1)
                dve.wait_ge(sem("vector_steps"), sent("vector_steps"))
                V.tensor_tensor(PRD[:, c, :], HK[:, c, S:T], inp, ALU.mult).then_inc(sem("vector_steps"), 1)
                dve.wait_ge(sem("vector_steps"), sent("vector_steps"))
                V.tensor_tensor(SN[:, h, c, :], SN[:, h, c, :], PRD[:, c, :], ALU.add).then_inc(sem("vector_steps"), 1)
                dve.wait_ge(sem("vector_steps"), sent("vector_steps"))
                V.tensor_tensor(HH[:, c, S:T], HV[:, c, S:T], inp, ALU.mult).then_inc(sem("vector_steps"), 1)
                dve.wait_ge(sem("vector_steps"), sent("vector_steps"))
            for half in range(2):
                dve.wait_ge(sem("vector_unit_ready"), due("vector_unit_ready"))
                u = next_unit()
                for b in range(4):
                    for vc in range(2):
                        bb = half * 4 + b
                        cs = CS[:, vc * NB + bb, :]
                        V.tensor_scalar(cs, cs, SM[:, 8 + bb:9 + bb], None, ALU.mult).then_inc(sem("vector_steps"), 1)
                        dve.wait_ge(sem("vector_steps"), sent("vector_steps"))
                        ins = V.scalar_tensor_tensor(cs, u[:, b * 256:(b + 1) * 256], HH[:, vc, S + bb:S + bb + 1], cs, ALU.mult, ALU.add)
                        if (b, vc) != (3, 1):
                            ins.then_inc(sem("vector_steps"), 1)
                            dve.wait_ge(sem("vector_steps"), sent("vector_steps"))
                        else:
                            ins.then_inc(sem("vector_unit_free"), 1)
                            dve.wait_ge(sem("vector_unit_free"), sent("vector_unit_free"))
            for half in range(2):
                dve.wait_ge(sem("vector_unit_ready"), due("vector_unit_ready"))
                u = next_unit()
                for b in range(4):
                    for vc in range(2):
                        bb = half * 4 + b
                        V.tensor_tensor(WRAW[:, 0:256], CS[:, vc * NB + bb, :], u[:, b * 256:(b + 1) * 256], ALU.mult).then_inc(sem("vector_steps"), 1)
                        dve.wait_ge(sem("vector_steps"), sent("vector_steps"))
                        ins = V.tensor_reduce(HH[:, vc, S + bb:S + bb + 1], WRAW[:, 0:256], AX, ALU.add)
                        if (b, vc) != (3, 1):
                            ins.then_inc(sem("vector_steps"), 1)
                            dve.wait_ge(sem("vector_steps"), sent("vector_steps"))
                        else:
                            ins.then_inc(sem("vector_unit_free"), 1)
                            dve.wait_ge(sem("vector_unit_free"), sent("vector_unit_free"))
            dve.sem_inc(sem("c_sample_done"), 1)
            for c in range(2):
                V.tensor_tensor(PRD[:, c, :], SN[:, h, c, :], HQ[:, c, S:T], ALU.mult).then_inc(sem("vector_steps"), 1)
                dve.wait_ge(sem("vector_steps"), sent("vector_steps"))
            dve.sem_inc(sem("nq_ready"), 1)
            dve.wait_ge(sem("vector_unit_ready"), due("vector_unit_ready"))
            u = next_unit()
            V.tensor_scalar(DEN[:, S:T], u[:, 0:NB], -1.0, None, ALU.mult).then_inc(sem("vector_steps"), 1)
            dve.wait_ge(sem("vector_steps"), sent("vector_steps"))
            V.tensor_tensor(DEN[:, S:T], DEN[:, S:T], u[:, 0:NB], ALU.max).then_inc(sem("vector_unit_free"), 1)
            dve.wait_ge(sem("vector_unit_free"), sent("vector_unit_free"))
            V.tensor_tensor(DEN[:, S:T], DEN[:, S:T], SM[:, 24:32], ALU.max).then_inc(sem("vector_steps"), 1)
            dve.wait_ge(sem("vector_steps"), sent("vector_steps"))
            V.reciprocal(DEN[:, S:T], DEN[:, S:T]).then_inc(sem("vector_steps"), 1)
            dve.wait_ge(sem("vector_steps"), sent("vector_steps"))
            for c in range(2):
                V.tensor_tensor(HH[:, c, :], HH[:, c, :], DEN[:, :], ALU.mult).then_inc(sem("vector_steps"), 1)
                dve.wait_ge(sem("vector_steps"), sent("vector_steps"))
            dve.sem_inc(sem("head_h"), 1)
            dve.wait_ge(sem("vector_unit_ready"), due("vector_unit_ready"))
            u = next_unit()
            V.tensor_scalar(split(inv[:, :]), halves(u), 1.0 / 256, 1e-6, ALU.mult, ALU.add).then_inc(sem("vector_unit_free"), 1)
            dve.wait_ge(sem("vector_unit_free"), sent("vector_unit_free"))
            dve.sem_inc(sem("mean_copied"), 1)
            dve.wait_ge(sem("root"), due("root"))
            V.reciprocal(inv[:, :], inv[:, :]).then_inc(sem("vector_steps"), 1)
            dve.wait_ge(sem("vector_steps"), sent("vector_steps"))
            for c in range(2):
                V.scalar_tensor_tensor(HH[:, c, :], HH[:, c, :], col("mnorm", 2 * h + c), inv[:, :], ALU.mult, ALU.mult).then_inc(sem("vector_steps"), 1)
                dve.wait_ge(sem("vector_steps"), sent("vector_steps"))
                V.tensor_tensor(MIX[:, 2 * h + c, :], HH[:, c, :], HO[:, c, :], ALU.mult).then_inc(sem("vector_steps"), 1)
                dve.wait_ge(sem("vector_steps"), sent("vector_steps"))
            dve.sem_inc(sem("head_over"), 1)
        dve.sem_inc(sem("mix_ready"), 1)
        add_residual()
        dve.wait_ge(sem("states_out"), due("states_out"))
        dve.sem_inc(sem("mixer_over"), 1)
        cross(1)

        dve.wait_ge(sem("vector_unit_ready"), due("vector_unit_ready"))
        u = next_unit()
        for t in range(TBN):
            ins = V.tensor_tensor(LOG[0:TB, t, :], u[0:TB, t * 8:t * 8 + 8], rb[0:TB, :], ALU.add)
            if t < TBN - 1:
                ins.then_inc(sem("vector_steps"), 1)
                dve.wait_ge(sem("vector_steps"), sent("vector_steps"))
            else:
                ins.then_inc(sem("vector_unit_free"), 1)
                dve.wait_ge(sem("vector_unit_free"), sent("vector_unit_free"))
        for t in range(TBN):
            V.max(TOP8[0:TB, t, :], LOG[0:TB, t, :]).then_inc(sem("vector_steps"), 1)
            dve.wait_ge(sem("vector_steps"), sent("vector_steps"))
            V.max_index(IDX[0:TB, t, :].bitcast(U32), TOP8[0:TB, t, :], LOG[0:TB, t, :]).then_inc(sem("vector_steps"), 1)
            dve.wait_ge(sem("vector_steps"), sent("vector_steps"))
        V.tensor_copy(IDXF[0:TB, :, :], IDX[0:TB, :, :].bitcast(U32)).then_inc(sem("vector_steps"), 1)
        dve.wait_ge(sem("vector_steps"), sent("vector_steps"))
        V.tensor_tensor(LOG[0:TB, :, 0], TOP8[0:TB, :, 1], TOP8[0:TB, :, 0], ALU.subtract).then_inc(sem("vector_steps"), 1)
        dve.wait_ge(sem("vector_steps"), sent("vector_steps"))
        dve.sem_inc(sem("router_max"), 1)
        dve.wait_ge(sem("router_exp"), due("router_exp"))
        V.tensor_scalar(LOG[0:TB, :, 1], LOG[0:TB, :, 0], 1.0, None, ALU.add).then_inc(sem("vector_steps"), 1)
        dve.wait_ge(sem("vector_steps"), sent("vector_steps"))
        V.reciprocal(LOG[0:TB, :, 1], LOG[0:TB, :, 1]).then_inc(sem("vector_steps"), 1)
        dve.wait_ge(sem("vector_steps"), sent("vector_steps"))
        V.tensor_tensor(LOG[0:TB, :, 2], LOG[0:TB, :, 0], LOG[0:TB, :, 1], ALU.mult).then_inc(sem("vector_steps"), 1)
        dve.wait_ge(sem("vector_steps"), sent("vector_steps"))
        for t in range(TBN):
            for i in range(2):
                dst = CMB[0:TB, t, :] if i == 0 else TOP8[0:TB, t, :]
                V.tensor_scalar(dst, experts_iota[0:TB, :], IDXF[0:TB, t, i:i + 1], LOG[0:TB, t, 1 + i:2 + i], ALU.is_equal, ALU.mult).then_inc(sem("vector_steps"), 1)
                dve.wait_ge(sem("vector_steps"), sent("vector_steps"))
            V.tensor_tensor(CMB[0:TB, t, :], CMB[0:TB, t, :], TOP8[0:TB, t, :], ALU.add).then_inc(sem("vector_steps"), 1)
            dve.wait_ge(sem("vector_steps"), sent("vector_steps"))
        dve.sem_inc(sem("comb_ready"), 1)
        dve.wait_ge(sem("comb_bcast"), due("comb_bcast"))
        for e in range(NE):
            up(EXP_C)
            for c in range(DC):
                dve.wait_ge(sem("vector_unit_ready"), due("vector_unit_ready"))
                u = next_unit()
                V.tensor_tensor(split(YT), split(COMB[:, e, :]), halves(u), ALU.mult).then_inc(sem("vector_unit_free"), 1)
                dve.wait_ge(sem("vector_unit_free"), sent("vector_unit_free"))
                V.tensor_tensor(X[:, c, :], X[:, c, :], YT, ALU.add).then_inc(sem("vector_steps"), 1)
                dve.wait_ge(sem("vector_steps"), sent("vector_steps"))
        dve.sem_inc(sem("residual"), 1)
        norm(X, H, "final")
        dve.sem_inc(sem("y_done"), 1)


OUTS = {
    "y": (P, DC, T), "conv_p": (P, CONV_C, CONV_W - 1), "conv_s": (P, CONV_C, NB, CONV_W - 1), "kv": (P, 6, T),
    "win_k_s": (NB, P, S), "win_v_s": (NB, S, P), "c_p": (NH, 2, P, 256), "c_s": (NH, P, 2 * NB, 256),
    "n_p": (P, NH, 2), "n_s": (P, NH, 2, NB), "m_p": (4, 1), "m_s": (1, NH * NB), "mem_kv": (2, P, 16, MEM),
}


def kernel(**inputs):
    import concourse.bacc as _bacc
    from concourse.bass_utils import run_bass_kernel_spmd as _run

    a = {n: np.asarray(v) for n, v in inputs.items()}
    A = np.ascontiguousarray

    def feats(v):
        return A(v.T.reshape(-1, P, v.shape[0]).transpose(1, 0, 2))

    def cols(v):
        return v.reshape(-1, P).T

    def tiles(w):
        k, n = w.shape
        return A(w.reshape(k // P, P, n // P, P).transpose(2, 1, 0, 3).reshape(n // P, P, k))

    g = {}
    g["xT"] = feats(np.concatenate([a["x_prompt"][0], a["x_sample"][:, 0]], 0))
    g["memT"] = feats(a["mem_prompt"][0])
    vec = np.zeros((P, VECW), np.float32)
    for name, v in [("mix0", a["norm_mix"][0]), ("mix1", a["norm_mix"][1]), ("x0", a["norm_xattn"][0]),
                    ("x1", a["norm_xattn"][1]), ("mem0", a["norm_mem"][0]), ("mem1", a["norm_mem"][1]),
                    ("ffn0", a["norm_ffn"][0]), ("ffn1", a["norm_ffn"][1]), ("final", a["norm_final"]),
                    ("conv_b", a["conv_b"][0]), ("ln_g", a["conv_ln_g"][0]), ("ln_b", a["conv_ln_b"][0]),
                    ("mnorm", a["mlstm_norm"][0])]:
        c = cols(v)
        vec[:, VEC[name]:VEC[name] + c.shape[1]] = c
    vec[:, VEC["conv_w"]:] = a["conv_w"][0].reshape(CONV_W, CONV_C, P).transpose(2, 1, 0).reshape(P, -1)
    g["vectors"] = vec
    w = a["w_in_even"][0]
    order = []
    for c in range(4):
        order += list(range(c * P, (c + 1) * P)) + list(range(512 + c * P, 512 + (c + 1) * P))
    for c in range(4):
        order += list(range(1024 + c * 64, 1088 + c * 64)) + list(range(1280 + c * 64, 1344 + c * 64))
    order += list(range(1536, 1536 + 768))
    w2 = np.zeros((D, 19 * P), np.float32)
    w2[:, :18 * P] = w[:, order]
    w2[:, 18 * P:18 * P + 24] = w[:, 2304:2328]
    g["w_in_even"] = tiles(w2)
    w = a["w_out_even"][0]
    b = w[512:].reshape(2, 4, 64, D).transpose(1, 0, 2, 3).reshape(512, D)
    g["w_out_even"] = tiles(np.concatenate([w[:512], b], 0))
    w = a["w_in_odd"][0]
    order = []
    for h in range(4):
        for part in range(4):
            order += list(range(part * D + h * 256, part * D + (h + 1) * 256))
    gt = np.zeros((D, P), np.float32)
    gt[:, 0:4] = w[:, 4096:4100]
    gt[:, 32:36] = w[:, 4100:4104]
    g["w_in_odd"] = tiles(np.concatenate([gt, w[:, order]], 1))
    g["w_out_odd"] = tiles(a["w_out_odd"][0])
    for n in ("xattn_wkv", "xattn_wq", "xattn_wo"):
        g[n] = np.stack([tiles(v) for v in a[n]])

    def pairs(w):
        f = w.shape[1] // 2
        v = w.reshape(w.shape[0], 2, f // P, P).transpose(0, 2, 1, 3).reshape(w.shape[0], 2 * f)
        return tiles(v)

    g["ffn_w_gu"] = pairs(a["ffn_w_gu"][0])
    g["ffn_w_dn"] = tiles(a["ffn_w_dn"][0])
    g["expert_w_gu"] = np.stack([pairs(v) for v in a["expert_w_gu"][0]])
    g["expert_w_dn"] = np.stack([tiles(v) for v in a["expert_w_dn"][0]])
    g["router_w"] = A(a["router_w"][0].reshape(DC, P, NE).transpose(1, 0, 2))
    g["router_b"] = A(np.broadcast_to(a["router_b"][0], (P, NE)))
    g["gate_b"] = A(np.stack([a["mlstm_b_i"][0], a["mlstm_b_f"][0]], 1))
    g["relx"] = np.tile(np.concatenate([a["rel_bias"], np.ones((1, 8), np.float32)], 0), (1, NB))
    pg = a["cache_nsa_pages"][0].reshape(-1, PAGE, 4, P)
    g["pages"] = A(np.concatenate([pg[:, :, 0].transpose(0, 2, 1), pg[:, :, 1].transpose(0, 2, 1),
                                   pg[:, :, 2].transpose(0, 2, 1), pg[:, :, 3]], 2))
    g["page_table"] = A(a["page_table"].reshape(1, -1)).astype(np.int32)
    wn = a["cache_nsa_window"][0].reshape(NB, S, 2, P)
    g["win_k"] = A(wn[:, :, 0].transpose(0, 2, 1))
    g["win_v"] = A(wn[:, :, 1])
    cw = np.zeros((P, 2, CMP, P), np.float32)
    for k in range(2):
        cw[64 * k:64 * k + 64, :, :, 64 * k:64 * k + 64] = a["nsa_cmp_w"][0].transpose(2, 0, 1, 3)
    g["cmp_w"] = cw
    pe = a["nsa_cmp_pe"][0].transpose(2, 0, 1)
    g["cmp_pe"] = A(np.concatenate([pe, pe], 0))
    g["cache_conv"] = A(a["cache_conv"][0].reshape(NB, CONV_W - 1, CONV_C, P).transpose(3, 2, 0, 1))
    g["state_c"] = A(a["state_mlstm_c"][0].reshape(NB, NH, 2, P, 256).transpose(1, 3, 2, 0, 4).reshape(NH, P, 2 * NB, 256))
    g["state_n"] = A(a["state_mlstm_n"][0].reshape(NB, NH, 2, P).transpose(3, 1, 2, 0))
    g["state_m"] = A(np.broadcast_to(a["state_mlstm_m"][0].reshape(1, -1), (P, NB * NH)))
    mk = a["cache_mem_kv"]
    kk = mk[:, :, :, 0].reshape(2, NB, MEM, 4, 2, P).transpose(0, 1, 5, 3, 4, 2).reshape(2, NB, P, 2048)
    vv = mk[:, :, :, 1].reshape(2, NB, 2, P, D).transpose(0, 1, 3, 2, 4).reshape(2, NB, P, 2048)
    g["mem_kv"] = np.stack([kk, vv], 1)
    g.update(constants())

    nc = _bacc.Bacc("TRN2", target_bir_lowering=False, num_devices=1)
    arrays, ins, outs = {}, {}, {}
    for name, v in g.items():
        arrays["in_" + name] = v
        ins[name] = nc.dram_tensor("in_" + name, v.shape, mybir.dt.from_np(v.dtype), kind="ExternalInput").ap()
    for name, shape in OUTS.items():
        outs[name] = nc.dram_tensor("out_" + name, shape, F32, kind="ExternalOutput").ap()
    program(nc, ins, outs)
    r = _run(nc, [arrays], core_ids=[0]).results[0]
    o = {name: np.asarray(r["out_" + name]) for name in OUTS}

    y = o["y"].transpose(2, 1, 0).reshape(T, D)
    kv = o["kv"].transpose(2, 1, 0)
    conv_p = o["conv_p"].transpose(2, 1, 0).reshape(1, 1, CONV_W - 1, 512)
    conv_s = o["conv_s"].transpose(2, 3, 1, 0).reshape(1, NB, CONV_W - 1, 512)
    nsa_p = kv[:S, :4].reshape(1, 1, S, 4, 2, 64)
    nsa_s = kv[S:, :4].reshape(1, NB, 1, 4, 2, 64)
    win_p = kv[:S, 4:].reshape(1, 1, S, 2, 2, 64)
    win_s = np.stack([o["win_k_s"].transpose(0, 2, 1), o["win_v_s"]], 2).reshape(1, NB, S, 2, 2, 64)
    c_p = o["c_p"].reshape(1, 1, NH, 256, 256)
    c_s = o["c_s"].reshape(NH, P, 2, NB, 256).transpose(3, 0, 2, 1, 4).reshape(1, NB, NH, 256, 256)
    n_p = o["n_p"].transpose(1, 2, 0).reshape(1, 1, NH, 256)
    n_s = o["n_s"].transpose(3, 1, 2, 0).reshape(1, NB, NH, 256)
    m_p = o["m_p"].reshape(1, 1, NH)
    m_s = o["m_s"].reshape(NH, NB).T.reshape(1, NB, NH)
    mkv = o["mem_kv"].transpose(0, 3, 2, 1).reshape(2, 1, MEM, 2, 4, 256)
    return tuple(A(v) for v in (y[:S].reshape(1, S, D), y[S:].reshape(NB, 1, D), conv_p, conv_s, nsa_p, nsa_s,
                                win_p, win_s, c_p, c_s, n_p, n_s, m_p, m_s, mkv))
```

```python
import math
from contextlib import ExitStack

import numpy as np
import concourse.bass as bass
from concourse import mybir

F32 = mybir.dt.float32
BF16 = mybir.dt.bfloat16
F16 = mybir.dt.float16
I32 = mybir.dt.int32
U32 = mybir.dt.uint32
ALU = mybir.AluOpType
ACT = mybir.ActivationFunctionType
AX = mybir.AxisListType.X

P = 128
D = 1024
DC = D // P
S = 512
NB = 8
T = S + NB
HT = T // 2
MEM = 256
QB = S // P
NEG = -1e30
PAST = 2048
PAGE = 128
PAGES = PAST // PAGE
CMP = 32
CONV_W = 31
CONV_C = 4
GLP = CONV_W - 1 + S
GLW = GLP + NB * CONV_W
DFF_C = 22
EXP_C = 11
NE = 8
NH = 4
SLOTS = 2
SLOT = 4096
UNITS = 2
TB = 104
TBN = T // TB

VEC = {}
_at = 0
for _n, _w in [("mix0", 8), ("mix1", 8), ("x0", 8), ("x1", 8), ("mem0", 8), ("mem1", 8), ("ffn0", 8),
               ("ffn1", 8), ("final", 8), ("conv_b", 4), ("ln_g", 4), ("ln_b", 4), ("mnorm", 8),
               ("conv_w", 4 * CONV_W)]:
    VEC[_n] = _at
    _at += _w
VECW = _at


def buckets(dist):
    n = np.maximum(dist, 0)
    nf = np.maximum(n, 1).astype(np.float32)
    large = 16 + (np.log(nf / np.float32(16)) / np.float32(math.log(1024 / 16)) * np.float32(16)).astype(np.int32)
    return np.where(n < 16, n, np.minimum(large, 31))


def one_hot(dist):
    out = np.zeros((33, len(dist)), np.float32)
    ok = dist >= 0
    out[buckets(dist)[ok], np.nonzero(ok)[0]] = 1.0
    out[32, ~ok] = NEG
    return out


def constants():
    rows = np.arange(64)
    same = (rows[:, None] // 4 == np.arange(16)[None, :]).astype(np.float32)
    pick = np.zeros((4, 4, P), np.float32)
    for h in range(4):
        pick[h, h] = 1.0
    past = one_hot(PAST - np.arange(PAST + 1))
    return {
        "c_ident": np.eye(P, dtype=np.float32),
        "c_toep": one_hot(S - 1 - np.arange(640)),
        "c_past": past,
        "c_group": same,
        "c_groupT": np.ascontiguousarray(same.T),
        "c_pick": pick.reshape(4, 4 * P),
        "c_own": (rows[:, None] // 8 == np.arange(8)[None, :]).astype(np.float32),
        "c_row": np.stack([np.arange(P) >= CMP - 1, np.arange(P) // 8 % 2 == 0, np.arange(P) // 8 % 2 == 1], 1).astype(np.float32),
        "c_tri": (np.arange(P)[None, :] >= np.arange(P)[:, None]).astype(np.float32),
        "c_expert": np.tile(np.arange(8, dtype=np.float32), (P, 1)),
    }


def program(nc, I, O):
    ctx = ExitStack()
    with ctx:
        body(nc, I, O, ctx)


def body(nc, I, O, ctx):
    def sb(name, shape, dt=F32):
        return ctx.enter_context(nc.sbuf_tensor(name, shape, dt))

    sems = {}

    def sem(name):
        if name not in sems:
            sems[name] = ctx.enter_context(nc.semaphore(name))
        return sems[name]

    X = sb("residual", [P, DC, T])
    H = sb("normed", [P, 2, DC, T], BF16)
    ring = sb("stream_ring", [P, SLOTS, SLOT])
    parts = sb("weight_parts", [P, 2, 2, SLOT], BF16)
    ident = sb("ident", [P, P])
    ones = sb("ones", [P, P])
    vec = sb("vectors", [P, VECW])
    group = sb("group", [64, 16])
    groupT = sb("groupT", [16, 64])
    pick = sb("pick", [4, 4, P])
    own = sb("own", [64, 8])
    rowok = sb("rowok", [P, 3])
    tri = sb("tri", [P, P])
    experts_iota = sb("experts_iota", [P, 8])
    relx = sb("relx", [33, 64])
    rb = sb("router_b", [P, 8])
    gate_b = sb("gate_b", [4, 2])
    router = sb("router_w", [P, DC, NE])
    pages = sb("page_table", [1, NB * PAGES], I32)
    small = sb("small", [P, 256])
    eps = sb("eps", [P, 2])
    sq = sb("squares", [P, 2, T])
    inv = sb("inverse_norm", [P, T])
    arena_words = 25088
    arena = sb("arena", [P, arena_words])
    psum_v = [ctx.enter_context(nc.psum_tensor(f"vector_unit{i}", [P, 1024], F32)) for i in range(UNITS)]
    psum_s = [ctx.enter_context(nc.psum_tensor(f"scalar_unit{i}", [P, 1024], F32)) for i in range(UNITS)]
    toep_dram = nc.dram_tensor("toeplitz_rows", [8, P * 641 + 640], F32, kind="Internal").ap()
    gates_dram = nc.dram_tensor("sample_gates", [NB * 24], F32, kind="Internal").ap()

    def at(lo, *shape, rows=P):
        n = int(np.prod(shape))
        assert lo + n <= arena_words, (lo, n)
        v = arena[0:rows, lo:lo + n]
        if len(shape) == 2:
            v = v.rearrange("p (a b) -> p a b", a=shape[0])
        if len(shape) == 3:
            v = v.rearrange("p (a b c) -> p a b c", a=shape[0], b=shape[1])
        return v

    def parts_at(lo, kc, n=T):
        return at(lo, kc * n).bitcast(BF16).rearrange("p (t k n) -> p t k n", t=2, k=kc)

    def slot_view(s, *shape, rows=P):
        n = int(np.prod(shape))
        v = ring[0:rows, s, 0:n]
        if len(shape) == 2:
            v = v.rearrange("p (a b) -> p a b", a=shape[0])
        if len(shape) == 3:
            v = v.rearrange("p (a b c) -> p a b c", a=shape[0], b=shape[1])
        return v

    GL = at(0, CONV_C, GLW)
    Q = at(3160, 4, T)
    KV = at(5240, 6, T)
    CW = at(8360, 2 * CMP * P).bitcast(BF16).rearrange("p (v t j m) -> p v t j m", v=2, t=2, j=CMP)
    KC = at(16552, 2, S + 16)
    GT = at(17608, T)
    E = at(18128, 8, S)
    CA = at(22224, CONV_C, T)
    PE_T = at(24304, 2, CMP)
    PEB = at(24368, 2)
    VTOK = at(14800, 2, QB, P)
    TOH = at(18128, 640, rows=33)
    OHP = at(18128, PAST + 1, rows=33)
    KVP = at(20000, 2 * S).bitcast(BF16).rearrange("p (t v n) -> p t v n", t=2, v=2)
    PEP = at(21100, 2 * CMP).bitcast(BF16).rearrange("p (t v j) -> p t v j", t=2, v=2)
    SC = at(0, 3, 2, S)
    PT = at(9384, QB, 2, P)
    CP = at(10408, 8, 16)
    CPT = at(10536, 8, P, rows=16)
    VC = at(11560, P, rows=16)
    GTOK = at(11688, QB, 24)
    QP = at(11784, NB, 64)
    SS = at(8360, PAST + 1, rows=64)
    SPT = at(10416, 16, 64)
    WPT = at(11440, 4, 64)
    SW = at(12296, S + 1, rows=64)
    SCM = at(12816, 2, 64, rows=64)
    VCS = at(12944, 4, P)
    CPT2 = at(13456, 64)
    NEWV = at(13520, 2, P, rows=8)
    NEWP = at(13776, 2, 8, rows=64)
    NEWT = at(13792, 2, 64, rows=8)
    SG = at(13920, 4, rows=64)
    SCORE = at(13930, 3, 40, rows=16)
    TOP = at(14050, 8, rows=16)
    SELN = at(14060, 40, rows=16)
    TSP = at(14100, 640)

    MX = at(0, DC, MEM)
    MK = at(2048, 16, MEM)
    MV = at(6144, 2, D)
    QX = at(8192, DC, T)
    XPT = at(13376, 8, P)
    QXP = at(14400, 64, 32)
    XS = at(16448, MEM, rows=32)
    XST = at(14400, 2 * NB, 32)
    XO = at(13376, D, rows=32)
    AO = parts_at(16768, DC)
    MH = parts_at(20928, DC, MEM)
    XP = at(20928, 2, 4, MEM)

    HID = parts_at(0, DFF_C)
    HIDE = parts_at(0, EXP_C)
    HF = at(20000, DC, T)
    COMB = at(11440, NE, T)
    LOG = at(15600, TBN, 8)
    TOP8 = at(15640, TBN, 8)
    IDX = at(15680, TBN, 8)
    IDXF = at(15720, TBN, 8)
    CMB = at(15760, TBN, 8)
    YT = at(15800, T)

    MIX = parts_at(0, DC)
    HQ = at(4160, 2, T)
    HK = at(5200, 2, T)
    HV = at(6240, 2, T)
    HO = at(7280, 2, T)
    KTOK = at(8320, QB, 256)
    VTK = at(9344, QB, 256)
    ST = at(10368, QB, S)
    MB = at(12416, S)
    WRAW = at(12928, S)
    HH = at(13440, 2, T)
    FM = at(14480, 6, T, rows=4)
    GC = at(17600, QB, 4)
    CS = at(17616, 2 * NB, 256)
    SN = at(21712, NH, 2, NB)
    ML = at(21776, NB * NH)
    GS = at(21808, 4, NB)
    VW = at(21840, QB, 256)
    CO = at(22864, 2, 256)
    NP_ = at(23376, NH, 2)
    DEN = at(23384, T)
    SM = at(23904, 64)
    MM = at(23968, 8)
    PRD = at(23976, 2, NB)
    SMO = at(24000, NH * NB)
    MMP = at(24032, 8)

    def counter():
        counts = {}

        def add(name, n=1):
            counts[name] = counts.get(name, 0) + n
            return counts[name]

        return add

    def turns(units):
        at_ = [0]

        def next_unit():
            at_[0] += 1
            return units[(at_[0] - 1) % UNITS]

        return next_unit

    stream, parted = [], []

    def weights(tag, src, chunks, kc, per):
        for c in range(0, chunks, per):
            n = min(per, chunks - c)
            parted.append(len(stream))
            stream.append((tag, [(lambda s, n=n: slot_view(s, n, kc * P),
                                  src[c:c + n].rearrange("c p n -> p c n"), None)]))

    def plan():
        weights("in_even", I["w_in_even"][0:12], 12, DC, 4)
        for v in range(2):
            stream.append(("cmp_w", [(lambda s: slot_view(s, CMP, P), I["cmp_w"][:, v], None)]))
        weights("in_even", I["w_in_even"][12:19], 7, DC, 4)
        for b in range(NB):
            parted.append(len(stream))
            stream.append(("cmp", [(lambda s, g=g: slot_view(s, PAGES, 2 * P)[:, g, :], None, (b * PAGES + g, 0, 256))
                                   for g in range(PAGES)]))
        stream.append(("win", [(lambda s: slot_view(s, NB, S), I["win_k"].rearrange("b p n -> p b n"), None)]))
        for b in range(0, NB, 2):
            stream.append(("ksel", [(lambda s, b2=b2, g=g: slot_view(s, 2, PAGES, P)[:, b2, g, :], None,
                                     ((b + b2) * PAGES + g, 256, 128)) for b2 in range(2) for g in range(PAGES)]))
        for b in range(0, NB, 2):
            stream.append(("vsel", [(lambda s, b2=b2, g=g: slot_view(s, 2, PAGES, P)[:, b2, g, :], None,
                                     ((b + b2) * PAGES + g, 384, 128)) for b2 in range(2) for g in range(PAGES)]))
        stream.append(("win", [(lambda s: slot_view(s, NB * 4, P), I["win_v"].rearrange("b (g p) n -> p (b g) n", p=P), None)]))
        weights("out_even", I["w_out_even"], DC, DC, 4)
        for l in range(2):
            if l == 1:
                weights("in_odd_g", I["w_in_odd"][0:1], 1, DC, 1)
                for h in range(NH):
                    weights("in_odd", I["w_in_odd"][1 + 8 * h:9 + 8 * h], 8, DC, 4)
                weights("out_odd", I["w_out_odd"], DC, DC, 4)
            weights("wkv", I["xattn_wkv"][l], 16, DC, 4)
            weights("wq", I["xattn_wq"][l], DC, DC, 4)
            for kv in range(2):
                for b in range(0, NB, 2):
                    stream.append(("memkv", [(lambda s: slot_view(s, 2, 2048),
                                              I["mem_kv"][l, kv, b:b + 2].rearrange("b p n -> p b n"), None)]))
            weights("wo", I["xattn_wo"][l], DC, DC, 4)
            if l == 0:
                weights("gu", I["ffn_w_gu"], 2 * DFF_C, DC, 4)
                weights("dn", I["ffn_w_dn"], DC, DFF_C, 1)
            else:
                for e in range(NE):
                    weights("egu", I["expert_w_gu"][e], 2 * EXP_C, DC, 4)
                    weights("edn", I["expert_w_dn"][e], DC, EXP_C, 2)

    plan()
    order, ahead = [], set()
    for n in range(len(stream)):
        if n not in ahead:
            order.append(n)
        if n in parted and n + 1 < len(stream) and n + 1 not in parted:
            later = [m for m in parted if m > n]
            order += later[:1]
            ahead.update(later[:1])
    weight_tags = {stream[n][0] for n in parted}
    stream = [stream[n] for n in order]
    parted = [n for n, item in enumerate(stream) if item[0] in weight_tags]
    direct = [n for n, item in enumerate(stream) if item[0] not in weight_tags]
    cached = [n for n in direct if stream[n][0] != "cmp_w"]
    queues = [1] * len(stream)
    for n, (tag, _) in enumerate(stream):
        if tag in ("cmp", "ksel", "vsel"):
            queues[n] = 2 if tag == "cmp" else 3
    queues[cached[1]] = 1
    queues[[n for n in range(len(stream)) if stream[n][0] == "cmp"][0]] = 1
    shared_scalar = [n for n in range(len(stream)) if queues[n] > 1]
    shared_pool = [n for n in range(len(stream)) if queues[n] > 2]
    POOL_SHARE = 16 * len(stream[shared_pool[0]][1][2::3])
    words = []
    for n in parted:
        src = stream[n][1][0][1]
        words.append(PAGES * 2 * P if src is None else src.shape[1] * src.shape[2])
    landed, total = [], [0] * SLOTS
    for n, (_, moves) in enumerate(stream):
        total[n % SLOTS] += 16 * (len(moves) - len(moves[2::queues[n]] if queues[n] > 2 else ()))
        landed.append(total[n % SLOTS])

    const_loads = [(ident, I["c_ident"]), (vec, I["vectors"]), (group, I["c_group"]), (groupT, I["c_groupT"]),
                   (own, I["c_own"]), (rowok, I["c_row"]), (tri, I["c_tri"]), (experts_iota, I["c_expert"]),
                   (relx, I["relx"]), (rb, I["router_b"]), (gate_b, I["gate_b"])]

    STEPS = QB * 8

    def step(i):
        return i // 8, i // 4 % 2, i // 2 % 2, i % 2

    block = ctx.enter_context(nc.Block())

    def col(name, c=0, rows=P):
        return vec[0:rows, VEC[name] + c:VEC[name] + c + 1]

    def halves(unit):
        return unit[:, :].rearrange("p (a b) -> p a b", a=2)[:, :, 0:HT]

    def split(v):
        return v.rearrange("p (a b) -> p a b", a=2)

    @block.sync
    def _(sp):
        sp.dma_start(pages[:, :], I["page_table"]).then_inc(sem("pages_in"), 16)
        sp.wait_ge(sem("pages_in"), 16)
        for n, (tag, moves) in enumerate(stream):
            s = n % SLOTS
            if n >= SLOTS:
                sp.wait_ge(sem(f"slot_free{s}"), n // SLOTS)
            for dst, src, page in moves[::queues[n]]:
                if page is not None:
                    entry, lo, w = page
                    number = sp.value_load(pages[0:1, entry:entry + 1], min_val=0, max_val=I["pages"].shape[0] - 1)
                    src = I["pages"][bass.ds(number, 1), :, lo:lo + w].rearrange("a p n -> p (a n)")
                sp.dma_start(dst(s), src).then_inc(sem(f"slot_ready{s}"), 16)

    @block.gpsimd
    def _(pool):
        due = counter()
        stores = [0]

        def load(dst, src, name):
            pool.dma_start(dst, src).then_inc(sem(name), 16)

        def store(dst, src):
            stores[0] += 16
            pool.dma_start(dst, src).then_inc(sem("stored"), 16)

        def stored():
            pool.wait_ge(sem("stored"), stores[0])

        load(X[:, :, :], I["xT"], "x_in")
        for dst, src in const_loads:
            load(dst[:, :], src, "consts_in")
        load(pick[:, :, :], I["c_pick"].rearrange("p (a b) -> p a b", a=4), "consts_in")
        load(router[:, :, :], I["router_w"], "consts_in")
        load(PE_T, I["cmp_pe"], "cmp_pe_in")
        for c in range(CONV_C):
            load(GL[:, c, GLP:GLW].rearrange("p (b w) -> p b w", b=NB)[:, :, 0:CONV_W - 1], I["cache_conv"][:, c], "conv_in")
        load(TOH, I["c_toep"], "toep_in")
        pool.wait_ge(sem("glu_done"), due("glu_done", CONV_C))
        store(O["conv_p"], GL[:, :, S:GLP])
        for c in range(CONV_C):
            store(O["conv_s"][:, c], GL[:, c, GLP:GLW].rearrange("p (b w) -> p b w", b=NB)[:, :, 1:CONV_W])
        pool.wait_ge(sem("kv_done"), due("kv_done"))
        store(O["kv"], KV[:, :, :])
        store(O["win_k_s"][:, :, 0:S - 1], I["win_k"][:, :, 1:S])
        store(O["win_v_s"][:, 0:S - 1, :], I["win_v"][:, 1:S, :])
        with nc.allow_non_contiguous_dma(reason="one new column per sample"):
            store(O["win_k_s"][:, :, S - 1:S].rearrange("b p n -> p b n"), KV[:, 4, S:T].rearrange("p (b n) -> p b n", n=1))
            store(O["win_v_s"][:, S - 1:S, :].rearrange("b n p -> p b n"), KV[:, 5, S:T].rearrange("p (b n) -> p b n", n=1))
        for h in range(8):
            pool.wait_ge(sem("toep_row"), due("toep_row"))
            store(toep_dram[h, 0:P * 641].rearrange("(p n) -> p n", p=P)[:, 0:640], TSP)
            stored()
            pool.sem_inc(sem("toep_row_out"), 1)
        for h in range(8):
            load(E[:, h, :], toep_dram[h, 127:127 + P * 640].rearrange("(p n) -> p n", p=P)[:, 0:S], "toep_back")
        pool.wait_ge(sem("attention_over"), due("attention_over"))
        load(OHP, I["c_past"], "past_in")
        pool.wait_ge(sem("gates_tok"), due("gates_tok"))
        store(gates_dram.rearrange("(b n) -> b n", b=NB), small[0:NB, 0:24])
        stored()
        load(SG[:, 0:3], gates_dram.rearrange("(r n) -> r n", n=3), "gates_rows")
        pool.wait_ge(sem("pages_in"), 16)
        for n in shared_pool:
            s = n % SLOTS
            pool.wait_ge(sem(f"slot_free{s}"), n // SLOTS)
            for dst, _, (entry, lo, w) in stream[n][1][2::queues[n]]:
                number = pool.value_load(pages[0:1, entry:entry + 1], min_val=0, max_val=I["pages"].shape[0] - 1)
                pool.dma_start(dst(s), I["pages"][bass.ds(number, 1), :, lo:lo + w].rearrange("a p n -> p (a n)")).then_inc(sem(f"pages_pool{s}"), 16)
        for l in range(2):
            pool.wait_ge(sem("mixer_over"), due("mixer_over"))
            load(MX, I["memT"], "mem_in")
            pool.wait_ge(sem("mkv_done"), due("mkv_done"))
            store(O["mem_kv"][l], MK)
            stored()
            pool.sem_inc(sem("mkv_out"), 1)
            if l == 0:
                pool.wait_ge(sem("ffn_over"), due("ffn_over"))
                load(SN, I["state_n"], "state_in")
                load(ML[:, :], I["state_m"], "state_in")
                for h in range(NH):
                    if h:
                        pool.wait_ge(sem("c_sample_done"), due("c_sample_done"))
                        store(O["c_s"][h - 1], CS)
                        stored()
                    load(CS, I["state_c"][h], "c_in")
                    for vc in range(2):
                        pool.wait_ge(sem("c_prompt_done"), due("c_prompt_done"))
                        store(O["c_p"][h, vc], CO[:, vc, :])
                    stored()
                    pool.sem_inc(sem("c_prompt_out"), 1)
                pool.wait_ge(sem("c_sample_done"), due("c_sample_done"))
                store(O["c_s"][NH - 1], CS)
                store(O["n_p"], NP_)
                store(O["n_s"], SN)
                store(O["m_s"], SMO[0:1, :])
                store(O["m_p"], MMP[0:4, 0:1])
                stored()
                pool.sem_inc(sem("states_out"), 1)
        pool.wait_ge(sem("y_done"), due("y_done"))
        store(O["y"], X[:, :, :])
        stored()

    @block.tensor
    def _(pe):
        due = counter()
        take_unit = {"vector": turns(psum_v), "scalar": turns(psum_s)}
        taken, parts_used = [0], [0]
        mm = nc.tensor.matmul

        def next_slot(tag):
            n = cached[taken[0]]
            assert stream[n][0] == tag, (stream[n][0], tag)
            taken[0] += 1
            return n % SLOTS, landed[n]

        def over_features(rhs, kc, who, n=T):
            pe.wait_ge(sem(f"{who}_unit_free"), due(f"{who}_unit_free"))
            u = take_unit[who]()
            for a in range(2):
                lo, w = (a * HT, HT) if n == T else (a * n // 2, n // 2)
                for k in range(kc):
                    ins = mm(u[:, a * 512:a * 512 + w], ones[:, :], rhs[:, k, lo:lo + w], start=(k == 0), stop=(k == kc - 1))
            ins.then_inc(sem(f"{who}_unit_ready"), 1)

        def norm(n=T, kc=DC):
            pe.wait_ge(sem("vector_unit_free"), due("vector_unit_free"))
            u = take_unit["vector"]()
            w = n // 2
            for k in range(kc):
                pe.wait_ge(sem("square"), due("square"))
                for a in range(2):
                    ins = mm(u[:, a * 512:a * 512 + w], ones[:, :], sq[:, k % 2, a * w:a * w + w],
                             start=(k == 0), stop=(k == kc - 1))
                if k < kc - 1:
                    ins.then_inc(sem("square_used"), 1)
            ins.then_inc(sem("vector_unit_ready"), 1)

        def project(src, chunks, kc, per, readers, n=T, cols=P, wait_chunks=None):
            w = n // 2 if n == T else n
            for c in range(chunks):
                if c % per == 0:
                    pe.wait_ge(sem("parts_ready"), due("parts_ready"))
                    wt = parts[:, parts_used[0] % 2, :, 0:per * kc * P].rearrange("p t (c k m) -> p t c k m", c=per, k=kc)
                    parts_used[0] += 1
                pe.wait_ge(sem(f"{readers[c]}_unit_free"), due(f"{readers[c]}_unit_free"))
                u = take_unit[readers[c]]()
                for a in range(n // w):
                    for k in range(kc):
                        if wait_chunks and c == 0 and a == 0:
                            pe.wait_ge(sem(wait_chunks), due(wait_chunks))
                        for i, j in ((0, 0), (0, 1), (1, 0)):
                            weight, x = wt[:, i, c % per, k, 0:cols], src[:, j, k, a * w:a * w + w]
                            ins = mm(u[0:cols, a * 512:a * 512 + w], weight if i else weight.bitcast(F16), x.bitcast(F16) if j else x,
                                     start=(k == 0 and i + j == 0), stop=(k == kc - 1 and i == 1))
                    if a == 0 and c % per == 0 and c:
                        pe.wait_ge(sem(f"{readers[c - 1]}_unit_ready"), before)
                        pe.sem_inc(sem("parts_free"), 1)
                ins.then_inc(sem(f"{readers[c]}_unit_ready"), 1)
                before = due(f"{readers[c]}_unit_free", 0)
            pe.wait_ge(sem(f"{readers[c]}_unit_ready"), before)
            pe.sem_inc(sem("parts_free"), 1)

        pe.wait_ge(sem("consts_in"), 16 * (len(const_loads) + 2))
        pe.wait_ge(sem("ones_set"), due("ones_set"))
        norm()
        project(H, 19, DC, 4, ["scalar", "scalar"] * 4 + ["scalar"] * 4 + ["vector"] * 6 + ["scalar"], wait_chunks="normed")

        def compress(u, columns, values):
            for v in range(2):
                for j in range(CMP):
                    for i, x in ((0, 0), (0, 1), (1, 0)):
                        weight, value = CW[:, v, i, j, :], values(x, v, j)
                        ins = mm(u[:, columns(v)], weight if i else weight.bitcast(F16), value if x else value.bitcast(F16),
                                 start=(j == 0 and i + x == 0), stop=(j == CMP - 1 and i == 1))
            return ins

        pe.wait_ge(sem("cmp_w_ready"), due("cmp_w_ready"))
        pe.wait_ge(sem("vector_unit_free"), due("vector_unit_free"))
        u = take_unit["vector"]()
        compress(u, lambda v: slice(v, v + 1), lambda x, v, j: PEP[:, x, v, j:j + 1]).then_inc(sem("vector_unit_ready"), 1)
        pe.wait_ge(sem("kv_ready"), due("kv_ready"))
        pe.wait_ge(sem("vector_unit_free"), due("vector_unit_free"))
        u = take_unit["vector"]()
        compress(u, lambda v: slice(v * 16, v * 16 + 16), lambda x, v, j: KVP[:, x, v, j:S:CMP]).then_inc(sem("vector_unit_ready"), 1)
        for b in range(NB):
            pe.wait_ge(sem("parts_ready"), due("parts_ready"))
            pg = parts[:, parts_used[0] % 2, :, :].rearrange("p t (g v c j) -> p t g v c j", g=PAGES, v=2, j=CMP)
            parts_used[0] += 1
            pe.wait_ge(sem("vector_unit_free"), due("vector_unit_free"))
            u = take_unit["vector"]()
            compress(u, lambda v: slice(v * 64, v * 64 + 64), lambda x, v, j: pg[:, x, :, v, :, j]).then_inc(sem("vector_unit_ready"), 1)
            pe.wait_ge(sem("vector_unit_ready"), due("vector_unit_free", 0))
            pe.sem_inc(sem("parts_free"), 1)
        pe.wait_ge(sem("toep_in"), 16)
        for h in range(8):
            pe.wait_ge(sem("scalar_unit_free"), due("scalar_unit_free"))
            u = take_unit["scalar"]()
            for a, (lo, w) in enumerate(((0, 512), (512, 128))):
                ins = mm(u[:, lo:lo + w], relx[:, h:h + 1].broadcast_to([33, P]), TOH[:, lo:lo + w],
                         start=True, stop=True)
            ins.then_inc(sem("scalar_unit_ready"), 1)
        pe.wait_ge(sem("scalar_unit_free"), due("scalar_unit_free"))
        u = take_unit["scalar"]()
        for v in range(2):
            for g in range(QB):
                ins = nc.tensor.transpose(u[:, (v * QB + g) * P:(v * QB + g + 1) * P], KV[:, 3 + 2 * v, g * P:(g + 1) * P], ident[:, :])
        ins.then_inc(sem("scalar_unit_ready"), 1)
        pe.wait_ge(sem("scalar_unit_free"), due("scalar_unit_free"))
        u = take_unit["scalar"]()
        for g in range(QB):
            nc.tensor.transpose(u[:, g * 24:g * 24 + 24], GT[0:24, g * P:(g + 1) * P], ident[0:24, 0:24])
        nc.tensor.transpose(u[0:NB, 96:120], GT[0:24, S:T], ident[0:24, 0:24])
        pe.wait_ge(sem("kc_ready"), due("kc_ready"))
        nc.tensor.transpose(u[0:16, 128:256], KC[:, 1, S:S + 16], ident[:, :])
        for v in range(2):
            nc.tensor.transpose(u[0:NB, 256 + v * P:384 + v * P], KV[:, 3 + 2 * v, S:T], ident[:, :])
        for g in range(4):
            ins = nc.tensor.transpose(u[:, 512 + g * P:512 + (g + 1) * P], KC[:, 1, g * P:(g + 1) * P], ident[:, :])
        ins.then_inc(sem("scalar_unit_ready"), 1)
        pe.wait_ge(sem("conv_done"), due("conv_done"))
        pe.wait_ge(sem("vector_unit_free"), due("vector_unit_free"))
        u = take_unit["vector"]()
        for a in range(2):
            for c in range(CONV_C):
                ins = mm(u[:, a * 512:a * 512 + HT], ones[:, :], CA[:, c, a * HT:a * HT + HT], start=(c == 0), stop=(c == CONV_C - 1))
        ins.then_inc(sem("vector_unit_ready"), 1)
        norm(kc=CONV_C)
        pe.wait_ge(sem("tok_ready"), due("tok_ready"))
        def compressed_scores(qb):
            wc = 4 * (qb + 1)
            pe.wait_ge(sem("vector_unit_free"), due("vector_unit_free"))
            u = take_unit["vector"]()
            for k in range(2):
                for g in range(4):
                    ins = mm(u[:, 512 * k + g * 16:512 * k + g * 16 + wc], Q[64 * k:64 * k + 64, g, qb * P:(qb + 1) * P],
                             KC[64 * k:64 * k + 64, 0, S:S + wc], start=True, stop=True)
            ins.then_inc(sem("vector_unit_ready"), 1)

        def turn_compressed(qb):
            wc = 4 * (qb + 1)
            pe.wait_ge(sem("cmp_probs"), due("cmp_probs"))
            pe.wait_ge(sem("scalar_unit_free"), due("scalar_unit_free"))
            u = take_unit["scalar"]()
            for h in range(8):
                ins = nc.tensor.transpose(u[0:wc, h * P:(h + 1) * P], CP[:, h, 0:wc], ident[:, :])
            ins.then_inc(sem("scalar_unit_ready"), 1)

        def scores(i):
            qb, k, gp, br = step(i)
            pe.wait_ge(sem("vector_unit_free"), due("vector_unit_free"))
            u = take_unit["vector"]()
            for g in range(2):
                ins = mm(u[:, g * 512:g * 512 + (qb + 1) * P], Q[64 * k:64 * k + 64, 2 * gp + g, qb * P:(qb + 1) * P],
                         KV[64 * k:64 * k + 64, 2 + 2 * br, 0:(qb + 1) * P], start=True, stop=True)
            ins.then_inc(sem("vector_unit_ready"), 1)

        compressed_scores(0)
        scores(0)
        scores(1)
        turn_compressed(0)
        for i in range(STEPS):
            qb, k, gp, br = step(i)
            wc = 4 * (qb + 1)
            pe.wait_ge(sem("probs"), due("probs"))
            pe.wait_ge(sem("scalar_unit_free"), due("scalar_unit_free"))
            u = take_unit["scalar"]()
            for kb in range(qb + 1):
                for g in range(2):
                    ins = nc.tensor.transpose(u[:, (kb * 2 + g) * P:(kb * 2 + g + 1) * P], SC[:, i % 3, g, kb * P:(kb + 1) * P], ident[:, :])
            ins.then_inc(sem("scalar_unit_ready"), 1)
            if i + 2 < STEPS:
                if (i + 2) % 8 == 0:
                    compressed_scores(qb + 1)
                scores(i + 2)
            if i % 8 == 0:
                pe.wait_ge(sem("cmp_probs_T"), due("cmp_probs_T"))
            pe.wait_ge(sem("probs_T"), due("probs_T"))
            pe.wait_ge(sem("vector_unit_free"), due("vector_unit_free"))
            o = take_unit["vector"]()
            h = 4 * k + 2 * gp
            if br == 0:
                mm(o[:, 0:256], VC[0:wc, :], CPT[0:wc, h:h + 2, :].rearrange("p a b -> p (a b)"), start=True, stop=False)
            for kb in range(qb + 1):
                ins = mm(o[:, 0:256], VTOK[:, br, kb, :], PT[:, kb, :, :].rearrange("p a b -> p (a b)"),
                         start=(br == 1 and kb == 0), stop=(kb == qb))
            ins.then_inc(sem("vector_unit_ready"), 1)
            if i % 8 == 7 and qb + 1 < QB:
                turn_compressed(qb + 1)

        pe.wait_ge(sem("qp_ready"), due("qp_ready"))
        pe.wait_ge(sem("past_in"), 16)
        oh = OHP
        rel64 = relx[:, :]
        pe.wait_ge(sem("vector_unit_free"), due("vector_unit_free"))
        u = take_unit["vector"]()
        for b in range(NB):
            mm(u[0:64, 0:64], QP[:, b, :], KC[:, 0, b * 64:(b + 1) * 64], start=(b == 0), stop=False)
        ins = mm(u[0:64, 0:64], rel64, oh[:, CMP - 1:PAST:CMP], start=False, stop=True)
        ins.then_inc(sem("vector_unit_ready"), 1)
        pe.wait_ge(sem("cmp_s"), due("cmp_s"))
        pe.wait_ge(sem("vector_unit_free"), due("vector_unit_free"))
        u = take_unit["vector"]()
        ins = mm(u[0:16, 0:64], group[:, :], SCM[:, 1, :], start=True, stop=True)
        ins.then_inc(sem("vector_unit_ready"), 1)
        s, filled = next_slot("win")
        pe.wait_ge(sem(f"slot_ready{s}"), filled)
        wk = slot_view(s, NB, S)
        pe.wait_ge(sem("scalar_unit_free"), due("scalar_unit_free"))
        u = take_unit["scalar"]()
        swin = u
        for b in range(NB):
            mm(swin[0:64, 0:S], QP[:, b, :], wk[:, b, :], start=(b == 0), stop=False)
        mm(swin[0:64, 0:S], rel64, oh[:, PAST - S:PAST], start=False, stop=True)
        for v in range(2):
            for b in range(NB):
                mm(swin[0:64, S + v:S + v + 1], QP[:, b, :], KV[:, 2 + 2 * v, S + b:S + b + 1], start=(b == 0), stop=False)
            ins = mm(swin[0:64, S + v:S + v + 1], rel64, oh[:, PAST:PAST + 1], start=False, stop=True)
        ins.then_inc(sem("scalar_unit_ready"), 1)
        pe.wait_ge(sem("scalar_unit_ready"), due("scalar_unit_free", 0))
        pe.sem_inc(sem(f"slot_free{s}"), 1)
        pe.wait_ge(sem("vector_unit_free"), due("vector_unit_free"))
        u = take_unit["vector"]()
        us = [u]
        pe.wait_ge(sem("vector_unit_free"), due("vector_unit_free"))
        u = take_unit["vector"]()
        us += [u]
        banks = [us[i // 2][0:64, (i % 2) * 512:(i % 2) * 512 + 512] for i in range(4)]
        for b in range(NB):
            if b % 2 == 0:
                s, filled = next_slot("ksel")
                pe.wait_ge(sem(f"slot_ready{s}"), filled)
                if b:
                    pe.wait_ge(sem(f"pages_pool{s}"), due(f"pages_pool{s}", POOL_SHARE))
                ks = slot_view(s, 2, PAGES * P)
            for i in range(4):
                ins = mm(banks[i], QP[:, b, :], ks[:, b % 2, i * 512:(i + 1) * 512], start=(b == 0), stop=False)
            if b % 2:
                ins.then_inc(sem(f"slot_free{s}"), 1)
        pe.wait_ge(sem("sel_mask"), due("sel_mask"))
        for i in range(4):
            mm(banks[i], rel64, oh[:, i * 512:(i + 1) * 512], start=False, stop=False)
            ins = mm(banks[i], groupT[:, :], SELN[:, i * 8:i * 8 + 8].rearrange("p (a b) -> p a b", b=1).broadcast_to([16, 8, 64]),
                     start=False, stop=True)
            if i % 2:
                ins.then_inc(sem("vector_unit_ready"), 1)
        pe.wait_ge(sem("sel_probs"), due("sel_probs"))
        pe.wait_ge(sem("scalar_unit_free"), due("scalar_unit_free"))
        u = take_unit["scalar"]()
        for g in range(PAGES):
            ins = nc.tensor.transpose(u[:, g * 64:(g + 1) * 64], SS[:, g * P:(g + 1) * P], ident[0:64, 0:64])
        ins.then_inc(sem("scalar_unit_ready"), 1)
        pe.wait_ge(sem("win_probs"), due("win_probs"))
        pe.wait_ge(sem("scalar_unit_free"), due("scalar_unit_free"))
        u = take_unit["scalar"]()
        for g in range(4):
            nc.tensor.transpose(u[:, g * 64:(g + 1) * 64], SW[:, g * P:(g + 1) * P], ident[0:64, 0:64])
        nc.tensor.transpose(u[:, 256:320], SCM[:, :, :].rearrange("p a b -> p (a b)"), ident[0:64, 0:64])
        for v in range(2):
            ins = nc.tensor.transpose(u[0:8, 320 + 64 * v:384 + 64 * v], NEWP[:, v, :], ident[0:64, 0:64])
        ins.then_inc(sem("scalar_unit_ready"), 1)
        pe.wait_ge(sem("sample_T"), due("sample_T"))
        pe.wait_ge(sem("vector_unit_free"), due("vector_unit_free"))
        u = take_unit["vector"]()
        o = u
        for b in range(NB):
            if b % 2 == 0:
                s, filled = next_slot("vsel")
                pe.wait_ge(sem(f"slot_ready{s}"), filled)
                pe.wait_ge(sem(f"pages_pool{s}"), due(f"pages_pool{s}", POOL_SHARE))
                vs = slot_view(s, 2, PAGES, P)
            for g in range(PAGES):
                ins = mm(o[:, 512 + 8 * b:520 + 8 * b], vs[:, b % 2, g, :], SPT[:, g, 8 * b:8 * b + 8], start=(g == 0), stop=(g == PAGES - 1))
            if b % 2:
                ins.then_inc(sem(f"slot_free{s}"), 1)
        s, filled = next_slot("win")
        pe.wait_ge(sem(f"slot_ready{s}"), filled)
        wv = slot_view(s, NB, 4, P)
        for b in range(NB):
            r = slice(8 * b, 8 * b + 8)
            for g in range(4):
                mm(o[:, r], wv[:, b, g, :], WPT[:, g, r], start=(g == 0), stop=False)
            for v in range(2):
                mm(o[:, r], NEWV[:, v, :], NEWT[:, v, r], start=False, stop=False)
            ins = mm(o[:, r], VCS[:, b // 2, :], CPT2[:, r], start=False, stop=True)
        ins.then_inc(sem("vector_unit_ready"), 1)
        pe.wait_ge(sem("vector_unit_ready"), due("vector_unit_free", 0))
        pe.sem_inc(sem(f"slot_free{s}"), 1)
        pe.wait_ge(sem("mix_ready"), due("mix_ready"))
        project(H, DC, DC, 4, ["vector"] * DC)

        def cross(l):
            norm(MEM)
            project(MH, 16, DC, 4, ["scalar"] * 16, n=MEM, wait_chunks="normed")
            norm()
            project(H, DC, DC, 4, ["scalar"] * DC, wait_chunks="normed")
            pe.wait_ge(sem("mkv_ready"), due("mkv_ready"))
            for t in range(2):
                pe.wait_ge(sem("scalar_unit_free"), due("scalar_unit_free"))
                u = take_unit["scalar"]()
                for c in range(8):
                    ins = nc.tensor.transpose(u[:, c * P:(c + 1) * P], MK[:, 8 + c, t * P:(t + 1) * P], ident[:, :])
                ins.then_inc(sem("scalar_unit_ready"), 1)
            pe.wait_ge(sem("mv_ready"), due("mv_ready"))
            def scores(qb):
                pe.wait_ge(sem("vector_unit_free"), due("vector_unit_free"))
                u = take_unit["vector"]()
                for h in range(4):
                    for c in range(2):
                        ins = mm(u[:, h * MEM:(h + 1) * MEM], QX[:, 2 * h + c, qb * P:(qb + 1) * P], MK[:, 2 * h + c, :],
                                 start=(c == 0), stop=(c == 1))
                ins.then_inc(sem("vector_unit_ready"), 1)

            scores(0)
            for qb in range(QB):
                if qb + 1 < QB:
                    scores(qb + 1)
                pe.wait_ge(sem("xprobs"), due("xprobs"))
                pe.wait_ge(sem("scalar_unit_free"), due("scalar_unit_free"))
                u = take_unit["scalar"]()
                for h in range(4):
                    for t in range(2):
                        ins = nc.tensor.transpose(u[:, (2 * h + t) * P:(2 * h + t + 1) * P], XP[:, qb % 2, h, t * P:(t + 1) * P], ident[:, :])
                ins.then_inc(sem("scalar_unit_ready"), 1)
                pe.wait_ge(sem("xprobs_T"), due("xprobs_T"))
                pe.wait_ge(sem("vector_unit_free"), due("vector_unit_free"))
                u = take_unit["vector"]()
                for h in range(4):
                    for c in range(2):
                        for t in range(2):
                            ins = mm(u[:, (2 * h + c) * P:(2 * h + c + 1) * P], MV[:, t, (2 * h + c) * P:(2 * h + c + 1) * P],
                                     XPT[:, 2 * h + t, :], start=(t == 0), stop=(t == 1))
                ins.then_inc(sem("vector_unit_ready"), 1)
            pe.wait_ge(sem("qxp_ready"), due("qxp_ready"))
            pe.wait_ge(sem("vector_unit_free"), due("vector_unit_free"))
            u = take_unit["vector"]()
            for b in range(NB):
                if b % 2 == 0:
                    s, filled = next_slot("memkv")
                    pe.wait_ge(sem(f"slot_ready{s}"), filled)
                    mk = slot_view(s, 2, DC, MEM)
                for c in range(DC):
                    ins = mm(u[0:32, 0:MEM], QXP[:, b * DC + c, :], mk[:, b % 2, c, :], start=(b == 0 and c == 0),
                             stop=(b == NB - 1 and c == DC - 1))
                if b == NB - 1:
                    ins.then_inc(sem("vector_unit_ready"), 1)
                    pe.wait_ge(sem("vector_unit_ready"), due("vector_unit_free", 0))
                    pe.sem_inc(sem(f"slot_free{s}"), 1)
                elif b % 2:
                    ins.then_inc(sem(f"slot_free{s}"), 1)
            pe.wait_ge(sem("xs_probs"), due("xs_probs"))
            pe.wait_ge(sem("vector_unit_free"), due("vector_unit_free"))
            u = take_unit["vector"]()
            for t in range(2):
                ins = nc.tensor.transpose(u[:, t * 32:(t + 1) * 32], XS[:, t * P:(t + 1) * P], ident[0:32, 0:32])
            ins.then_inc(sem("vector_unit_ready"), 1)
            pe.wait_ge(sem("xs_T"), due("xs_T"))
            pe.wait_ge(sem("vector_unit_free"), due("vector_unit_free"))
            u = take_unit["vector"]()
            for b in range(NB):
                if b % 2 == 0:
                    s, filled = next_slot("memkv")
                    pe.wait_ge(sem(f"slot_ready{s}"), filled)
                    mv = slot_view(s, 2, 2, D)
                for t in range(2):
                    for lo in (0, 512):
                        ins = mm(u[0:32, lo:lo + 512], XST[:, 2 * b + t, :], mv[:, b % 2, t, lo:lo + 512],
                                 start=(b + t == 0), stop=(b == NB - 1 and t == 1))
                if b == NB - 1:
                    ins.then_inc(sem("vector_unit_ready"), 1)
                    pe.wait_ge(sem("vector_unit_ready"), due("vector_unit_free", 0))
                    pe.sem_inc(sem(f"slot_free{s}"), 1)
                elif b % 2:
                    ins.then_inc(sem(f"slot_free{s}"), 1)
            pe.wait_ge(sem("xo_ready"), due("xo_ready"))
            pe.wait_ge(sem("vector_unit_free"), due("vector_unit_free"))
            u = take_unit["vector"]()
            for c in range(DC):
                ins = nc.tensor.transpose(u[:, c * 32:(c + 1) * 32], XO[:, c * P:(c + 1) * P], ident[0:32, 0:32])
            ins.then_inc(sem("vector_unit_ready"), 1)
            pe.wait_ge(sem("ao_ready"), due("ao_ready"))
            project(AO, DC, DC, 4, ["vector"] * DC)

        cross(0)
        norm()
        project(H, 2 * DFF_C, DC, 4, ["scalar", "vector"] * DFF_C, wait_chunks="normed")
        pe.wait_ge(sem("hidden"), due("hidden"))
        project(HID, DC, DFF_C, 1, ["vector"] * DC)

        norm()
        project(H, 1, DC, 1, ["scalar"], cols=64, wait_chunks="normed")
        for h in range(NH):
            project(H, 8, DC, 4, ["scalar"] * 8)
            if h == 0:
                pe.wait_ge(sem("gate_rows"), due("gate_rows"))
                pe.wait_ge(sem("scalar_unit_free"), due("scalar_unit_free"))
                u = take_unit["scalar"]()
                for g in range(QB):
                    ins = nc.tensor.transpose(u[:, g * 4:g * 4 + 4], FM[0:4, 2, g * P:(g + 1) * P], ident[0:4, 0:4])
                ins.then_inc(sem("scalar_unit_ready"), 1)
            pe.wait_ge(sem("head_ready"), due("head_ready"))
            for src in (HK, HV):
                pe.wait_ge(sem("scalar_unit_free"), due("scalar_unit_free"))
                u = take_unit["scalar"]()
                for g in range(QB):
                    for c in range(2):
                        ins = nc.tensor.transpose(u[:, g * 256 + c * P:g * 256 + (c + 1) * P], src[:, c, g * P:(g + 1) * P], ident[:, :])
                ins.then_inc(sem("scalar_unit_ready"), 1)
            pe.wait_ge(sem("vector_unit_free"), due("vector_unit_free"))
            u = take_unit["vector"]()
            mm(u[:, 0:S], pick[:, h, :], FM[0:4, 3, 0:S], start=True, stop=True)
            mm(u[:, S:S + NB], pick[:, h, :], FM[0:4, 0, S:T], start=True, stop=True)
            ins = mm(u[:, S + NB:S + 2 * NB], pick[:, h, :], FM[0:4, 1, S:T], start=True, stop=True)
            ins.then_inc(sem("vector_unit_ready"), 1)
            for sb_ in range(QB):
                pe.wait_ge(sem("vector_unit_free"), due("vector_unit_free"))
                u = take_unit["vector"]()
                w = S - sb_ * P
                for c in range(2):
                    ins = mm(u[:, 0:w], HK[:, c, sb_ * P:(sb_ + 1) * P], HQ[:, c, sb_ * P:S], start=(c == 0), stop=(c == 1))
                ins.then_inc(sem("vector_unit_ready"), 1)
            pe.wait_ge(sem("st_ready"), due("st_ready"))
            for part in range(3):
                pe.wait_ge(sem("vector_unit_free"), due("vector_unit_free"))
                u = take_unit["vector"]()
                for sb_ in range(QB):
                    lhs = ones[:, :] if part == 2 else VTK[:, sb_, part * P:(part + 1) * P]
                    ins = mm(u[:, sb_ * P:S], lhs, ST[:, sb_, sb_ * P:S], start=(sb_ == 0), stop=(sb_ == QB - 1))
                ins.then_inc(sem("vector_unit_ready"), 1)
            pe.wait_ge(sem("vector_unit_free"), due("vector_unit_free"))
            u = take_unit["vector"]()
            ins = mm(u[:, 0:S], pick[:, h, :], FM[0:4, 5, 0:S], start=True, stop=True)
            ins.then_inc(sem("vector_unit_ready"), 1)
            pe.wait_ge(sem("vw_ready"), due("vw_ready"))
            pe.wait_ge(sem("scalar_unit_free"), due("scalar_unit_free"))
            u = take_unit["scalar"]()
            for vc in range(2):
                for g in range(QB):
                    mm(u[:, vc * 256:vc * 256 + 256], VW[:, g, vc * P:(vc + 1) * P], KTOK[:, g, :], start=(g == 0), stop=(g == QB - 1))
            for c in range(2):
                for g in range(QB):
                    ins = mm(u[:, 512 + c:513 + c], KTOK[:, g, c * P:(c + 1) * P], SM[:, g:g + 1], start=(g == 0), stop=(g == QB - 1))
            ins.then_inc(sem("scalar_unit_ready"), 1)
            for src in (HK, HQ):
                for half in range(2):
                    pe.wait_ge(sem("vector_unit_free"), due("vector_unit_free"))
                    u = take_unit["vector"]()
                    for b in range(4):
                        for c in range(2):
                            ins = mm(u[:, b * 256 + c * P:b * 256 + (c + 1) * P],
                                     src[:, c, S + half * 4 + b:S + half * 4 + b + 1].broadcast_to([P, P]), ident[:, :], start=True, stop=True)
                    ins.then_inc(sem("vector_unit_ready"), 1)
            pe.wait_ge(sem("nq_ready"), due("nq_ready"))
            pe.wait_ge(sem("vector_unit_free"), due("vector_unit_free"))
            u = take_unit["vector"]()
            for c in range(2):
                ins = mm(u[:, 0:NB], ones[:, :], PRD[:, c, :], start=(c == 0), stop=(c == 1))
            ins.then_inc(sem("vector_unit_ready"), 1)
            pe.wait_ge(sem("head_out"), due("head_out"))
            over_features(sq, 2, "vector")
        pe.wait_ge(sem("mix_ready"), due("mix_ready"))
        project(MIX, DC, DC, 4, ["vector"] * DC)
        cross(1)

        norm()
        pe.wait_ge(sem("normed"), due("normed", DC))
        pe.wait_ge(sem("vector_unit_free"), due("vector_unit_free"))
        u = take_unit["vector"]()
        for t in range(TBN):
            for k in range(DC):
                ins = mm(u[0:TB, t * 8:t * 8 + 8], HF[:, k, t * TB:(t + 1) * TB], router[:, k, :], start=(k == 0), stop=(k == DC - 1))
        ins.then_inc(sem("vector_unit_ready"), 1)
        pe.wait_ge(sem("comb_ready"), due("comb_ready"))
        for e in range(NE):
            pe.wait_ge(sem("scalar_unit_free"), due("scalar_unit_free"))
            u = take_unit["scalar"]()
            for t in range(TBN):
                lo = t * TB if t < 3 else 512 + (t - 3) * TB
                ins = mm(u[:, lo:lo + TB], CMB[0:TB, t, e:e + 1].broadcast_to([TB, P]), ident[0:TB, 0:TB], start=True, stop=True)
            ins.then_inc(sem("scalar_unit_ready"), 1)
        for e in range(NE):
            project(H, 2 * EXP_C, DC, 4, ["scalar", "vector"] * EXP_C)
            pe.wait_ge(sem("hidden"), due("hidden"))
            project(HIDE, DC, EXP_C, 2, ["vector"] * DC)
        norm()

    @block.scalar
    def _(act):
        due, sent = counter(), counter()
        next_unit = turns(psum_s)
        act.sem_inc(sem("scalar_unit_free"), UNITS)
        sent("scalar_unit_free", UNITS)
        A = nc.scalar.activation
        loaded = [0]

        def load_pages():
            n = shared_scalar[loaded[0]]
            loaded[0] += 1
            s = n % SLOTS
            act.wait_ge(sem(f"slot_free{s}"), n // SLOTS)
            for dst, _, (entry, lo, w) in stream[n][1][1::queues[n]]:
                number = act.value_load(pages[0:1, entry:entry + 1], min_val=0, max_val=I["pages"].shape[0] - 1)
                act.dma_start(dst(s), I["pages"][bass.ds(number, 1), :, lo:lo + w].rearrange("a p n -> p (a n)")).then_inc(sem(f"slot_ready{s}"), 16)

        def squares(src, n=T, kc=DC):
            for k in range(kc):
                if k >= 2:
                    act.wait_ge(sem("square_used"), due("square_used"))
                A(sq[:, k % 2, 0:n], src[:, k, 0:n], ACT.Square).then_inc(sem("square"), 1)
                act.wait_ge(sem("square"), sent("square"))
            act.wait_ge(sem("square_used"), due("square_used"))

        def norm(src, dst=H, n=T, tmp=None):
            squares(src, n)
            act.wait_ge(sem("mean_copied"), due("mean_copied"))
            A(inv[:, 0:n], inv[:, 0:n], ACT.Sqrt).then_inc(sem("root"), 1)
            act.wait_ge(sem("root"), sent("root"))
            if dst is not None:
                for k in range(DC):
                    act.wait_ge(sem("scaled"), due("scaled"))
                    from_ = sq[:, k % 2, 0:n] if tmp is None else tmp[:, k, 0:n]
                    A(dst[:, 0, k, 0:n], from_, ACT.Copy).then_inc(sem("high"), 1)
                    act.wait_ge(sem("high"), sent("high"))

        act.wait_ge(sem("x_in"), 16)
        act.wait_ge(sem("consts_in"), 16 * (len(const_loads) + 2))
        norm(X)
        act.wait_ge(sem("conv_in"), 16 * CONV_C)
        for c in range(CONV_C):
            act.wait_ge(sem("scalar_unit_ready"), due("scalar_unit_ready"))
            u = next_unit()
            ev = halves(u)
            tmp = split(CA[:, c, :])
            A(tmp, ev, ACT.Copy).then_inc(sem("scalar_unit_free"), 1)
            act.wait_ge(sem("scalar_unit_free"), sent("scalar_unit_free"))
            act.wait_ge(sem("scalar_unit_ready"), due("scalar_unit_ready"))
            u = next_unit()
            if c >= 2:
                act.wait_ge(sem("glu_done"), due("glu_done"))
            A(split(sq[:, c % 2, :]), halves(u), ACT.Sigmoid).then_inc(sem("scalar_unit_free"), 1)
            act.wait_ge(sem("scalar_unit_free"), sent("scalar_unit_free"))
            act.sem_inc(sem("glu_parts"), 1)
        for c in range(4):
            act.wait_ge(sem("scalar_unit_ready"), due("scalar_unit_ready"))
            u = next_unit()
            A(split(Q[:, c, :]), halves(u), ACT.Copy, scale=0.125).then_inc(sem("scalar_unit_free"), 1)
            act.wait_ge(sem("scalar_unit_free"), sent("scalar_unit_free"))
        act.wait_ge(sem("scalar_unit_ready"), due("scalar_unit_ready"))
        u = next_unit()
        A(split(GT)[0:24], halves(u)[0:24], ACT.Sigmoid).then_inc(sem("scalar_unit_free"), 1)
        act.wait_ge(sem("scalar_unit_free"), sent("scalar_unit_free"))
        act.wait_ge(sem("pages_in"), 16)
        for b in range(1, NB):
            load_pages()
        for h in range(8):
            act.wait_ge(sem("scalar_unit_ready"), due("scalar_unit_ready"))
            u = next_unit()
            if h:
                act.wait_ge(sem("toep_row_out"), due("toep_row_out"))
            A(TSP[:, 0:320], u[:, 0:320], ACT.Copy).then_inc(sem("scalar_steps"), 1)
            act.wait_ge(sem("scalar_steps"), sent("scalar_steps"))
            A(TSP[:, 320:640], u[:, 320:640], ACT.Copy).then_inc(sem("scalar_unit_free"), 1)
            act.wait_ge(sem("scalar_unit_free"), sent("scalar_unit_free"))
            act.sem_inc(sem("toep_row"), 1)
        act.wait_ge(sem("scalar_unit_ready"), due("scalar_unit_ready"))
        u = next_unit()
        A(VTOK.rearrange("p a b c -> p (a b c)"), u[:, :], ACT.Copy).then_inc(sem("scalar_unit_free"), 1)
        act.wait_ge(sem("scalar_unit_free"), sent("scalar_unit_free"))
        act.wait_ge(sem("scalar_unit_ready"), due("scalar_unit_ready"))
        u = next_unit()
        A(small[0:NB, 0:24], u[0:NB, 96:120], ACT.Copy).then_inc(sem("scalar_steps"), 1)
        act.wait_ge(sem("scalar_steps"), sent("scalar_steps"))
        act.sem_inc(sem("gates_tok"), 1)
        A(GTOK.rearrange("p a b -> p (a b)"), u[:, 0:96], ACT.Copy).then_inc(sem("scalar_steps"), 1)
        act.wait_ge(sem("scalar_steps"), sent("scalar_steps"))
        A(VC, u[0:16, 128:256], ACT.Copy).then_inc(sem("scalar_steps"), 1)
        act.wait_ge(sem("scalar_steps"), sent("scalar_steps"))
        A(NEWV.rearrange("p a b -> p (a b)"), u[0:NB, 256:512], ACT.Copy).then_inc(sem("scalar_steps"), 1)
        act.wait_ge(sem("scalar_steps"), sent("scalar_steps"))
        A(VCS.rearrange("p a b -> p (a b)"), u[:, 512:1024], ACT.Copy).then_inc(sem("scalar_unit_free"), 1)
        act.wait_ge(sem("scalar_unit_free"), sent("scalar_unit_free"))
        act.sem_inc(sem("tok_ready"), 1)
        act.sem_inc(sem("tok_ready_v"), 1)
        act.wait_ge(sem("centred_v"), due("centred_v"))
        squares(CA, kc=CONV_C)
        act.wait_ge(sem("variance"), due("variance"))
        A(inv[:, :], inv[:, :], ACT.Sqrt).then_inc(sem("root"), 1)
        act.wait_ge(sem("root"), sent("root"))
        for c in range(CONV_C):
            act.wait_ge(sem("conv_normed"), due("conv_normed"))
            A(sq[:, c % 2, :], CA[:, c, :], ACT.Sigmoid).then_inc(sem("conv_gate"), 1)
            act.wait_ge(sem("conv_gate"), sent("conv_gate"))
        def exp_compressed(qb):
            wc = 4 * (qb + 1)
            act.wait_ge(sem("cmp_shifted"), due("cmp_shifted"))
            A(CP[:, :, 0:wc], CP[:, :, 0:wc], ACT.Exp).then_inc(sem("cmp_exp"), 1)
            act.wait_ge(sem("cmp_exp"), sent("cmp_exp"))

        def read_compressed(qb):
            wc = 4 * (qb + 1)
            act.wait_ge(sem("scalar_unit_ready"), due("scalar_unit_ready"))
            u = next_unit()
            A(CPT[0:wc, :, :].rearrange("p a b -> p (a b)"), u[0:wc, :], ACT.Copy).then_inc(sem("scalar_unit_free"), 1)
            act.wait_ge(sem("scalar_unit_free"), sent("scalar_unit_free"))
            act.sem_inc(sem("cmp_probs_T"), 1)

        def exp_scores(i):
            w, m = (step(i)[0] + 1) * P, 128 + 8 * (i % 3)
            act.wait_ge(sem("shifted"), due("shifted"))
            A(SC[:, i % 3, 0, 0:w], SC[:, i % 3, 0, 0:w], ACT.Exp, bias=small[:, m:m + 1], accum_out=small[:, m + 2:m + 3]).then_inc(sem("scalar_steps"), 1)
            A(SC[:, i % 3, 1, 0:w], SC[:, i % 3, 1, 0:w], ACT.Exp, bias=small[:, m + 1:m + 2], accum_out=small[:, m + 3:m + 4]).then_inc(sem("exped"), 1)
            act.wait_ge(sem("scalar_steps"), sent("scalar_steps"))

        exp_compressed(0)
        exp_scores(0)
        read_compressed(0)
        exp_scores(1)
        for i in range(STEPS):
            qb = step(i)[0]
            act.wait_ge(sem("scalar_unit_ready"), due("scalar_unit_ready"))
            u = next_unit()
            A(PT[:, 0:qb + 1, :, :].rearrange("p a b c -> p (a b c)"), u[:, 0:2 * (qb + 1) * P], ACT.Copy).then_inc(sem("scalar_unit_free"), 1)
            act.wait_ge(sem("scalar_unit_free"), sent("scalar_unit_free"))
            act.sem_inc(sem("probs_T"), 1)
            if i + 2 < STEPS:
                if (i + 2) % 8 == 0:
                    exp_compressed(qb + 1)
                exp_scores(i + 2)
            if i % 8 == 7 and qb + 1 < QB:
                read_compressed(qb + 1)
        act.wait_ge(sem("cmp_s_shifted"), due("cmp_s_shifted"))
        A(SCM[:, 0, :], SCM[:, 0, :], ACT.Exp, accum_out=small[0:64, 80:81]).then_inc(sem("cmp_s_exp"), 1)
        act.wait_ge(sem("cmp_s_exp"), sent("cmp_s_exp"))
        act.wait_ge(sem("scalar_unit_ready"), due("scalar_unit_ready"))
        u = next_unit()
        A(SW[:, 0:S], u[0:64, 0:S], ACT.Copy).then_inc(sem("scalar_steps"), 1)
        act.wait_ge(sem("scalar_steps"), sent("scalar_steps"))
        A(SW[:, S:S + 1], u[0:64, S + 1:S + 2], ACT.Copy).then_inc(sem("scalar_steps"), 1)
        act.wait_ge(sem("scalar_steps"), sent("scalar_steps"))
        A(SS[:, PAST:PAST + 1], u[0:64, S:S + 1], ACT.Copy).then_inc(sem("scalar_unit_free"), 1)
        act.wait_ge(sem("scalar_unit_free"), sent("scalar_unit_free"))
        act.sem_inc(sem("win_scores"), 1)
        for b in range(2, NB, 2):
            load_pages()
        act.wait_ge(sem("win_shift"), due("win_shift"))
        A(SW[:, :], SW[:, :], ACT.Exp, bias=small[0:64, 82:83], accum_out=small[0:64, 83:84]).then_inc(sem("win_exp"), 1)
        act.wait_ge(sem("win_exp"), sent("win_exp"))
        load_pages()
        act.wait_ge(sem("sel_shift"), due("sel_shift"))
        A(SS[:, :], SS[:, :], ACT.Exp, bias=small[0:64, 84:85], accum_out=small[0:64, 85:86]).then_inc(sem("sel_exp"), 1)
        act.wait_ge(sem("sel_exp"), sent("sel_exp"))
        act.wait_ge(sem("scalar_unit_ready"), due("scalar_unit_ready"))
        u = next_unit()
        A(SPT.rearrange("p a b -> p (a b)"), u[:, :], ACT.Copy).then_inc(sem("scalar_unit_free"), 1)
        act.wait_ge(sem("scalar_unit_free"), sent("scalar_unit_free"))
        act.wait_ge(sem("scalar_unit_ready"), due("scalar_unit_ready"))
        u = next_unit()
        A(WPT.rearrange("p a b -> p (a b)"), u[:, 0:256], ACT.Copy).then_inc(sem("scalar_steps"), 1)
        act.wait_ge(sem("scalar_steps"), sent("scalar_steps"))
        A(CPT2, u[:, 256:320], ACT.Copy).then_inc(sem("scalar_steps"), 1)
        act.wait_ge(sem("scalar_steps"), sent("scalar_steps"))
        A(NEWT.rearrange("p a b -> p (a b)"), u[0:8, 320:448], ACT.Copy).then_inc(sem("scalar_unit_free"), 1)
        act.wait_ge(sem("scalar_unit_free"), sent("scalar_unit_free"))
        act.sem_inc(sem("sample_T"), 1)
        for b in range(2, NB, 2):
            load_pages()

        def cross(l):
            act.wait_ge(sem("mem_in"), 16 * (l + 1))
            norm(MX, MH, MEM)
            for c in range(16):
                act.wait_ge(sem("scalar_unit_ready"), due("scalar_unit_ready"))
                u = next_unit()
                A(MK[:, c, :], u[:, 0:MEM], ACT.Copy).then_inc(sem("scalar_unit_free"), 1)
                act.wait_ge(sem("scalar_unit_free"), sent("scalar_unit_free"))
            act.sem_inc(sem("mkv_done"), 1)
            act.sem_inc(sem("mkv_ready"), 1)
            norm(X)
            for c in range(DC):
                act.wait_ge(sem("scalar_unit_ready"), due("scalar_unit_ready"))
                u = next_unit()
                A(split(QX[:, c, :]), halves(u), ACT.Copy, scale=0.0625).then_inc(sem("scalar_unit_free"), 1)
                act.wait_ge(sem("scalar_unit_free"), sent("scalar_unit_free"))
            act.sem_inc(sem("qx_ready"), 1)
            for t in range(2):
                act.wait_ge(sem("scalar_unit_ready"), due("scalar_unit_ready"))
                u = next_unit()
                A(MV[:, t, :], u[:, :], ACT.Copy).then_inc(sem("scalar_unit_free"), 1)
                act.wait_ge(sem("scalar_unit_free"), sent("scalar_unit_free"))
            act.sem_inc(sem("mv_ready"), 1)
            def exp_scores(qb):
                m = 128 + 8 * (qb % 2)
                act.wait_ge(sem("xmax"), due("xmax"))
                for h in range(4):
                    ins = A(XP[:, qb % 2, h, :], XP[:, qb % 2, h, :], ACT.Exp, bias=small[:, m + h:m + h + 1], accum_out=small[:, m + 4 + h:m + 5 + h])
                    if h < 3:
                        ins.then_inc(sem("scalar_steps"), 1)
                ins.then_inc(sem("xexp"), 1)
                act.wait_ge(sem("scalar_steps"), sent("scalar_steps", 3))

            exp_scores(0)
            for qb in range(QB):
                if qb + 1 < QB:
                    exp_scores(qb + 1)
                act.wait_ge(sem("scalar_unit_ready"), due("scalar_unit_ready"))
                u = next_unit()
                A(XPT.rearrange("p a b -> p (a b)"), u[:, :], ACT.Copy).then_inc(sem("scalar_unit_free"), 1)
                act.wait_ge(sem("scalar_unit_free"), sent("scalar_unit_free"))
                act.sem_inc(sem("xprobs_T"), 1)
            act.wait_ge(sem("xs_max"), due("xs_max"))
            A(XS, XS, ACT.Exp, bias=small[0:32, 104:105], accum_out=small[0:32, 105:106]).then_inc(sem("xs_exp"), 1)
            act.wait_ge(sem("xs_exp"), sent("xs_exp"))
            act.wait_ge(sem("residual"), due("residual"))
            norm(X, tmp=HF if l else None)

        def gate(chunks):
            for c in range(chunks):
                act.wait_ge(sem("scalar_unit_ready"), due("scalar_unit_ready"))
                u = next_unit()
                if c >= 2:
                    act.wait_ge(sem("gate_used"), due("gate_used"))
                A(split(sq[:, c % 2, :]), halves(u), ACT.Silu).then_inc(sem("scalar_unit_free"), 1)
                act.wait_ge(sem("scalar_unit_free"), sent("scalar_unit_free"))
                act.sem_inc(sem("gate_parts"), 1)
            act.wait_ge(sem("gate_used"), due("gate_used", 2))

        act.wait_ge(sem("residual"), due("residual"))
        cross(0)
        gate(DFF_C)
        act.wait_ge(sem("residual"), due("residual"))
        norm(X)
        act.wait_ge(sem("scalar_unit_ready"), due("scalar_unit_ready"))
        u = next_unit()
        A(split(FM[0:4, 0, :]), halves(u)[0:4], ACT.Identity, bias=gate_b[:, 0:1]).then_inc(sem("scalar_steps"), 1)
        act.wait_ge(sem("scalar_steps"), sent("scalar_steps"))
        A(split(FM[0:4, 1, :]), halves(u)[32:36], ACT.Identity, bias=gate_b[:, 1:2]).then_inc(sem("scalar_unit_free"), 1)
        act.wait_ge(sem("scalar_unit_free"), sent("scalar_unit_free"))
        act.sem_inc(sem("gates_raw"), 1)
        act.wait_ge(sem("gate_abs"), due("gate_abs"))
        A(FM[0:4, 2, :], FM[0:4, 2, :], ACT.Exp, scale=-1.0).then_inc(sem("gate_exp"), 1)
        act.wait_ge(sem("gate_exp"), sent("gate_exp"))
        act.wait_ge(sem("gate_one"), due("gate_one"))
        A(FM[0:4, 4, :], FM[0:4, 3, :], ACT.Ln).then_inc(sem("gate_ln"), 1)
        act.wait_ge(sem("gate_ln"), sent("gate_ln"))
        act.wait_ge(sem("gate_m"), due("gate_m"))
        A(FM[0:4, 5, 0:S], FM[0:4, 4, 0:S], ACT.Exp, scale=-1.0).then_inc(sem("gate_rows_exp"), 1)
        act.wait_ge(sem("gate_rows_exp"), sent("gate_rows_exp"))
        for h in range(NH):
            if h:
                act.wait_ge(sem("head_over"), due("head_over"))
            for i, dst in enumerate((HQ, HK, HV, HO)):
                for c in range(2):
                    act.wait_ge(sem("scalar_unit_ready"), due("scalar_unit_ready"))
                    u = next_unit()
                    fn, sc_ = (ACT.Sigmoid, 1.0) if i == 3 else (ACT.Copy, 0.0625 if i == 1 else 1.0)
                    A(split(dst[:, c, :]), halves(u), fn, scale=sc_).then_inc(sem("scalar_unit_free"), 1)
                    act.wait_ge(sem("scalar_unit_free"), sent("scalar_unit_free"))
            if h == 0:
                act.wait_ge(sem("scalar_unit_ready"), due("scalar_unit_ready"))
                u = next_unit()
                A(GC.rearrange("p a b -> p (a b)"), u[:, 0:16], ACT.Copy).then_inc(sem("scalar_unit_free"), 1)
                act.wait_ge(sem("scalar_unit_free"), sent("scalar_unit_free"))
                act.sem_inc(sem("gc_ready"), 1)
            act.sem_inc(sem("head_ready"), 1)
            act.sem_inc(sem("head_ready_v"), 1)
            for dst in (KTOK, VTK):
                act.wait_ge(sem("scalar_unit_ready"), due("scalar_unit_ready"))
                u = next_unit()
                A(dst.rearrange("p a b -> p (a b)"), u[:, :], ACT.Copy).then_inc(sem("scalar_unit_free"), 1)
                act.wait_ge(sem("scalar_unit_free"), sent("scalar_unit_free"))
            act.sem_inc(sem("tok_head"), 1)
            for sb_ in range(QB):
                w = S - sb_ * P
                act.wait_ge(sem("w_arg"), due("w_arg"))
                A(WRAW[:, 0:w], WRAW[:, 0:w], ACT.Exp).then_inc(sem("w_exp"), 1)
                act.wait_ge(sem("w_exp"), sent("w_exp"))
            act.wait_ge(sem("sm_arg"), due("sm_arg"))
            A(SM[:, 0:4], SM[:, 0:4], ACT.Exp).then_inc(sem("sm_exp"), 1)
            act.wait_ge(sem("sm_exp"), sent("sm_exp"))
            act.wait_ge(sem("gs_arg"), due("gs_arg"))
            A(SM[:, 8:32], SM[:, 8:32], ACT.Exp).then_inc(sem("gs_exp"), 1)
            act.wait_ge(sem("gs_exp"), sent("gs_exp"))
            act.wait_ge(sem("c_in"), 16 * (h + 1))
            for c in range(2 * NB):
                A(CS[:, c, :], CS[:, c, :], ACT.Copy, scale=SM[:, 8 + c % NB:9 + c % NB]).then_inc(sem("c_decayed"), 1)
            act.wait_ge(sem("scalar_unit_ready"), due("scalar_unit_ready"))
            u = next_unit()
            if h:
                act.wait_ge(sem("c_prompt_out"), due("c_prompt_out"))
            A(NP_[:, h, :], u[:, 512:514], ACT.Copy).then_inc(sem("scalar_steps"), 1)
            act.wait_ge(sem("scalar_steps"), sent("scalar_steps"))
            for vc in range(2):
                ins = A(CO[:, vc, :], u[:, vc * 256:(vc + 1) * 256], ACT.Copy)
                if vc:
                    ins.then_inc(sem("scalar_unit_free"), 1)
                    act.wait_ge(sem("scalar_unit_free"), sent("scalar_unit_free"))
                else:
                    ins.then_inc(sem("scalar_steps"), 1)
                    act.wait_ge(sem("scalar_steps"), sent("scalar_steps"))
                act.sem_inc(sem("c_prompt_done"), 1)
            act.wait_ge(sem("head_h"), due("head_h"))
            A(sq[:, 0, :], HH[:, 0, :], ACT.Square).then_inc(sem("scalar_steps"), 1)
            act.wait_ge(sem("scalar_steps"), sent("scalar_steps"))
            A(sq[:, 1, :], HH[:, 1, :], ACT.Square).then_inc(sem("head_out"), 1)
            act.wait_ge(sem("head_out"), sent("head_out"))
            act.wait_ge(sem("mean_copied"), due("mean_copied"))
            A(inv[:, :], inv[:, :], ACT.Sqrt).then_inc(sem("root"), 1)
            act.wait_ge(sem("root"), sent("root"))
        act.wait_ge(sem("residual"), due("residual"))
        cross(1)
        act.wait_ge(sem("router_max"), due("router_max"))
        A(LOG[0:TB, :, :], LOG[0:TB, :, :], ACT.Exp).then_inc(sem("router_exp"), 1)
        act.wait_ge(sem("router_exp"), sent("router_exp"))
        for e in range(NE):
            act.wait_ge(sem("scalar_unit_ready"), due("scalar_unit_ready"))
            u = next_unit()
            A(COMB[:, e, 0:3 * TB], u[:, 0:3 * TB], ACT.Copy).then_inc(sem("scalar_steps"), 1)
            act.wait_ge(sem("scalar_steps"), sent("scalar_steps"))
            A(COMB[:, e, 3 * TB:T], u[:, 512:512 + 2 * TB], ACT.Copy).then_inc(sem("scalar_unit_free"), 1)
            act.wait_ge(sem("scalar_unit_free"), sent("scalar_unit_free"))
        act.sem_inc(sem("comb_bcast"), 1)
        for e in range(NE):
            gate(EXP_C)
        act.wait_ge(sem("residual"), due("residual"))
        norm(X, None)

    @block.vector
    def _(dve):
        due, sent = counter(), counter()
        next_unit = turns(psum_v)
        dve.sem_inc(sem("vector_unit_free"), UNITS)
        sent("vector_unit_free", UNITS)
        V = nc.vector
        splits = [0]

        def split_weights():
            m = splits[0]
            if m == len(parted):
                return
            splits[0] += 1
            s, n = parted[m] % SLOTS, words[m]
            high, low = parts[:, m % 2, 0, 0:n].bitcast(F16), parts[:, m % 2, 1, 0:n]
            dve.wait_ge(sem(f"slot_ready{s}"), landed[parted[m]])
            if m >= 2:
                dve.wait_ge(sem("parts_free"), m - 1)
            V.tensor_scalar(high, ring[:, s, 0:n], 65504.0, -65504.0, ALU.min, ALU.max).then_inc(sem("vector_steps"), 1)
            dve.wait_ge(sem("vector_steps"), sent("vector_steps"))
            V.tensor_tensor(low, ring[:, s, 0:n], high, ALU.subtract).then_inc(sem("parts_ready"), 1)
            dve.wait_ge(sem("parts_ready"), sent("parts_ready"))
            dve.sem_inc(sem(f"slot_free{s}"), 1)

        def split_into(high, low, value):
            V.tensor_scalar(high, value, 65504.0, -65504.0, ALU.min, ALU.max).then_inc(sem("vector_steps"), 1)
            dve.wait_ge(sem("vector_steps"), sent("vector_steps"))
            V.tensor_tensor(low, value, high, ALU.subtract).then_inc(sem("vector_steps"), 1)
            dve.wait_ge(sem("vector_steps"), sent("vector_steps"))

        def split_compression(v):
            n = [m for m in direct if stream[m][0] == "cmp_w"][v]
            s = n % SLOTS
            dve.wait_ge(sem(f"slot_ready{s}"), landed[n])
            split_into(CW[:, v, 0].bitcast(F16), CW[:, v, 1], slot_view(s, CMP, P))
            dve.sem_inc(sem(f"slot_free{s}"), 1)

        def in_parts(dst, k, value):
            V.tensor_copy(dst[:, 0, k], value).then_inc(sem("vector_steps"), 1)
            dve.wait_ge(sem("vector_steps"), sent("vector_steps"))
            V.tensor_tensor(dst[:, 1, k].bitcast(F16), value, dst[:, 0, k], ALU.subtract).then_inc(sem("vector_steps"), 1)
            dve.wait_ge(sem("vector_steps"), sent("vector_steps"))

        def post(name):
            dve.sem_inc(sem(name), 1)

        def norm(src, dst, gain, n=T, bias=1e-6, tmp=None):
            dve.wait_ge(sem("vector_unit_ready"), due("vector_unit_ready"))
            u = next_unit()
            w = n // 2
            V.tensor_scalar(inv[:, 0:n].rearrange("p (a b) -> p a b", a=2),
                                    u[:, :].rearrange("p (a b) -> p a b", a=2)[:, :, 0:w], 1.0 / D, bias, ALU.mult, ALU.add).then_inc(sem("vector_unit_free"), 1)
            dve.wait_ge(sem("vector_unit_free"), sent("vector_unit_free"))
            dve.sem_inc(sem("mean_copied"), 1)
            dve.wait_ge(sem("root"), due("root"))
            V.reciprocal(inv[:, 0:n], inv[:, 0:n]).then_inc(sem("vector_steps"), 1)
            dve.wait_ge(sem("vector_steps"), sent("vector_steps"))
            def scaled(k):
                return sq[:, k % 2, 0:n] if tmp is None else tmp[:, k, 0:n]

            for k in range(DC + 1):
                if k < DC:
                    V.scalar_tensor_tensor(scaled(k), src[:, k, 0:n], col(gain, k), inv[:, 0:n], ALU.mult, ALU.mult).then_inc(sem("vector_steps"), 1)
                    dve.wait_ge(sem("vector_steps"), sent("vector_steps"))
                    dve.sem_inc(sem("scaled"), 1)
                if k:
                    dve.wait_ge(sem("high"), due("high"))
                    V.tensor_tensor(dst[:, 1, k - 1, 0:n].bitcast(F16), scaled(k - 1), dst[:, 0, k - 1, 0:n], ALU.subtract).then_inc(sem("normed"), 1)
                    dve.wait_ge(sem("normed"), sent("normed"))

        def add_residual(per=4):
            for c in range(DC):
                if c % per == 0:
                    split_weights()
                dve.wait_ge(sem("vector_unit_ready"), due("vector_unit_ready"))
                u = next_unit()
                V.tensor_tensor(split(X[:, c, :]), split(X[:, c, :]), halves(u), ALU.add).then_inc(sem("vector_unit_free"), 1)
                dve.wait_ge(sem("vector_unit_free"), sent("vector_unit_free"))
            dve.sem_inc(sem("residual"), 1)

        def convolve(c, first, end):
            for j in range(first, end):
                wj, dst, src = col("conv_w", c * CONV_W + j), CA[:, c, 0:S], GL[:, c, j:j + S]
                if j == 0:
                    V.tensor_scalar(dst, src, wj, col("conv_b", c), ALU.mult, ALU.add).then_inc(sem("vector_steps"), 1)
                    dve.wait_ge(sem("vector_steps"), sent("vector_steps"))
                else:
                    V.scalar_tensor_tensor(dst, src, wj, dst, ALU.mult, ALU.add).then_inc(sem("vector_steps"), 1)
                    dve.wait_ge(sem("vector_steps"), sent("vector_steps"))

        def convolve_samples(c):
            ext = GL[:, c, GLP:GLW].rearrange("p (b w) -> p b w", b=NB)
            product = sq[:, 0, 0:NB * CONV_W].rearrange("p (b w) -> p b w", b=NB)
            taps = vec[:, VEC["conv_w"] + c * CONV_W:VEC["conv_w"] + (c + 1) * CONV_W].rearrange("p (a w) -> p a w", a=1)
            V.tensor_tensor(product, ext, taps.broadcast_to([P, NB, CONV_W]), ALU.mult).then_inc(sem("vector_steps"), 1)
            dve.wait_ge(sem("vector_steps"), sent("vector_steps"))
            V.tensor_reduce(CA[:, c, S:T], product, AX, ALU.add).then_inc(sem("vector_steps"), 1)
            dve.wait_ge(sem("vector_steps"), sent("vector_steps"))
            V.tensor_scalar(CA[:, c, S:T], CA[:, c, S:T], col("conv_b", c), None, ALU.add).then_inc(sem("vector_steps"), 1)
            dve.wait_ge(sem("vector_steps"), sent("vector_steps"))

        V.memset(ones[:, :], 1.0).then_inc(sem("vector_steps"), 1)
        dve.wait_ge(sem("vector_steps"), sent("vector_steps"))
        dve.sem_inc(sem("ones_set"), 1)
        dve.wait_ge(sem("x_in"), 16)
        dve.wait_ge(sem("consts_in"), 16 * (len(const_loads) + 2))
        split_weights()
        norm(X, H, "mix0")
        dve.wait_ge(sem("conv_in"), 16 * CONV_C)
        V.memset(GL[:, :, 0:CONV_W - 1], 0.0).then_inc(sem("vector_steps"), 1)
        dve.wait_ge(sem("vector_steps"), sent("vector_steps"))
        split_weights()
        for c in range(CONV_C):
            if c == 2:
                split_weights()
            dve.wait_ge(sem("glu_parts"), due("glu_parts"))
            V.tensor_tensor(GL[:, c, CONV_W - 1:GLP], CA[:, c, 0:S], sq[:, c % 2, 0:S], ALU.mult).then_inc(sem("vector_steps"), 1)
            dve.wait_ge(sem("vector_steps"), sent("vector_steps"))
            ext = GL[:, c, GLP:GLW].rearrange("p (b w) -> p b w", b=NB)
            V.tensor_tensor(ext[:, :, CONV_W - 1], CA[:, c, S:T], sq[:, c % 2, S:T], ALU.mult).then_inc(sem("glu_done"), 1)
            dve.wait_ge(sem("glu_done"), sent("glu_done"))
        split_weights()
        for v in range(2):
            split_compression(v)
        split_weights()
        for c in range(6):
            dve.wait_ge(sem("vector_unit_ready"), due("vector_unit_ready"))
            u = next_unit()
            V.tensor_copy(split(KV[:, c, :]), halves(u)).then_inc(sem("vector_unit_free"), 1)
            dve.wait_ge(sem("vector_unit_free"), sent("vector_unit_free"))
        dve.wait_ge(sem("cmp_pe_in"), 16)
        split_into(PEP[:, 0].bitcast(F16), PEP[:, 1], PE_T)
        dve.sem_inc(sem("cmp_w_ready"), 1)
        split_into(KVP[:, 0].bitcast(F16), KVP[:, 1], KV[:, 0:2, 0:S])
        dve.sem_inc(sem("kv_done"), 1)
        dve.sem_inc(sem("kv_ready"), 1)
        split_weights()
        dve.wait_ge(sem("vector_unit_ready"), due("vector_unit_ready"))
        u = next_unit()
        V.tensor_copy(PEB, u[:, 0:2]).then_inc(sem("vector_unit_free"), 1)
        dve.wait_ge(sem("vector_unit_free"), sent("vector_unit_free"))
        dve.wait_ge(sem("vector_unit_ready"), due("vector_unit_ready"))
        u = next_unit()
        for v in range(2):
            ins = V.tensor_scalar(KC[:, v, S:S + 16], u[:, v * 16:v * 16 + 16], PEB[:, v:v + 1], None, ALU.add)
            if v == 0:
                ins.then_inc(sem("vector_steps"), 1)
                dve.wait_ge(sem("vector_steps"), sent("vector_steps"))
            else:
                ins.then_inc(sem("vector_unit_free"), 1)
                dve.wait_ge(sem("vector_unit_free"), sent("vector_unit_free"))
        for b in range(NB):
            split_weights()
            convolve(b // 2, (b % 2) * 16, CONV_W if b % 2 else 16)
            if b % 2:
                convolve_samples(b // 2)
            dve.wait_ge(sem("vector_unit_ready"), due("vector_unit_ready"))
            u = next_unit()
            for v in range(2):
                ins = V.tensor_scalar(KC[:, v, b * 64:(b + 1) * 64], u[:, v * 64:v * 64 + 64], PEB[:, v:v + 1], None, ALU.add)
                if v == 0:
                    ins.then_inc(sem("vector_steps"), 1)
                    dve.wait_ge(sem("vector_steps"), sent("vector_steps"))
                else:
                    ins.then_inc(sem("vector_unit_free"), 1)
                    dve.wait_ge(sem("vector_unit_free"), sent("vector_unit_free"))
        dve.sem_inc(sem("kc_ready"), 1)
        dve.sem_inc(sem("conv_done"), 1)
        dve.wait_ge(sem("vector_unit_ready"), due("vector_unit_ready"))
        u = next_unit()
        V.tensor_scalar(split(inv[:, :]), halves(u), 1.0 / 512, None, ALU.mult).then_inc(sem("vector_unit_free"), 1)
        dve.wait_ge(sem("vector_unit_free"), sent("vector_unit_free"))
        for c in range(CONV_C):
            V.tensor_tensor(CA[:, c, :], CA[:, c, :], inv[:, :], ALU.subtract).then_inc(sem("vector_steps"), 1)
            dve.wait_ge(sem("vector_steps"), sent("vector_steps"))
        dve.sem_inc(sem("centred_v"), 1)
        dve.wait_ge(sem("vector_unit_ready"), due("vector_unit_ready"))
        u = next_unit()
        V.tensor_scalar(split(inv[:, :]), halves(u), 1.0 / 512, 1e-5, ALU.mult, ALU.add).then_inc(sem("vector_unit_free"), 1)
        dve.wait_ge(sem("vector_unit_free"), sent("vector_unit_free"))
        dve.sem_inc(sem("variance"), 1)
        dve.wait_ge(sem("root"), due("root"))
        V.reciprocal(inv[:, :], inv[:, :]).then_inc(sem("vector_steps"), 1)
        dve.wait_ge(sem("vector_steps"), sent("vector_steps"))
        for c in range(CONV_C):
            V.scalar_tensor_tensor(CA[:, c, :], CA[:, c, :], col("ln_g", c), inv[:, :], ALU.mult, ALU.mult).then_inc(sem("vector_steps"), 1)
            dve.wait_ge(sem("vector_steps"), sent("vector_steps"))
            V.tensor_scalar(CA[:, c, :], CA[:, c, :], col("ln_b", c), None, ALU.add).then_inc(sem("vector_steps"), 1)
            dve.wait_ge(sem("vector_steps"), sent("vector_steps"))
            dve.sem_inc(sem("conv_normed"), 1)
            dve.wait_ge(sem("conv_gate"), due("conv_gate"))
            V.tensor_tensor(CA[:, c, :], CA[:, c, :], sq[:, c % 2, :], ALU.mult).then_inc(sem("vector_steps"), 1)
            dve.wait_ge(sem("vector_steps"), sent("vector_steps"))
        in_parts(H, slice(0, 4), CA)
        dve.wait_ge(sem("toep_back"), 16 * 8)
        dve.wait_ge(sem("tok_ready_v"), due("tok_ready_v"))
        def shift_compressed(qb):
            off, wc = 384 - P * qb, 4 * (qb + 1)
            dve.wait_ge(sem("vector_unit_ready"), due("vector_unit_ready"))
            u = next_unit()
            for k in range(2):
                got = u[:, 512 * k:512 * k + 64].rearrange("p (a b) -> p a b", a=4)[:, :, 0:wc]
                ins = V.tensor_tensor(CP[:, 4 * k:4 * k + 4, 0:wc], got, E[:, 4 * k:4 * k + 4, off + CMP - 1:off + CMP * wc:CMP], ALU.add)
                if k == 0:
                    ins.then_inc(sem("vector_steps"), 1)
                    dve.wait_ge(sem("vector_steps"), sent("vector_steps"))
                else:
                    ins.then_inc(sem("vector_unit_free"), 1)
                    dve.wait_ge(sem("vector_unit_free"), sent("vector_unit_free"))
            V.tensor_reduce(small[:, 32:40], CP[:, :, 0:wc], AX, ALU.max).then_inc(sem("vector_steps"), 1)
            dve.wait_ge(sem("vector_steps"), sent("vector_steps"))
            V.tensor_tensor(CP[:, :, 0:wc], CP[:, :, 0:wc], small[:, 32:40].rearrange("p (a b) -> p a b", b=1).broadcast_to([P, 8, wc]), ALU.subtract).then_inc(sem("cmp_shifted"), 1)
            dve.wait_ge(sem("cmp_shifted"), sent("cmp_shifted"))

        def norm_compressed(qb):
            wc = 4 * (qb + 1)
            dve.wait_ge(sem("cmp_exp"), due("cmp_exp"))
            V.tensor_reduce(small[:, 40:48], CP[:, :, 0:wc], AX, ALU.add).then_inc(sem("vector_steps"), 1)
            dve.wait_ge(sem("vector_steps"), sent("vector_steps"))
            V.reciprocal(small[:, 40:48], small[:, 40:48]).then_inc(sem("vector_steps"), 1)
            dve.wait_ge(sem("vector_steps"), sent("vector_steps"))
            if qb == 0:
                V.tensor_scalar(small[:, 40:48], small[:, 40:48], rowok[:, 0:1], None, ALU.mult).then_inc(sem("vector_steps"), 1)
                dve.wait_ge(sem("vector_steps"), sent("vector_steps"))
            gates = GTOK[:, qb, :].rearrange("p (h c) -> p h c", c=3)
            V.tensor_tensor(small[:, 40:48], small[:, 40:48], gates[:, :, 0], ALU.mult).then_inc(sem("vector_steps"), 1)
            dve.wait_ge(sem("vector_steps"), sent("vector_steps"))
            V.tensor_tensor(CP[:, :, 0:wc], CP[:, :, 0:wc], small[:, 40:48].rearrange("p (a b) -> p a b", b=1).broadcast_to([P, 8, wc]), ALU.mult).then_inc(sem("cmp_probs"), 1)
            dve.wait_ge(sem("cmp_probs"), sent("cmp_probs"))

        def shift_scores(i):
            qb, k, gp, br = step(i)
            off, w, h, m = 384 - P * qb, P * (qb + 1), 4 * k + 2 * gp, 128 + 8 * (i % 3)
            dve.wait_ge(sem("vector_unit_ready"), due("vector_unit_ready"))
            u = next_unit()
            s3 = u[:, :].rearrange("p (a b) -> p a b", a=2)[:, :, 0:w]
            V.tensor_tensor(SC[:, i % 3, :, 0:w], s3, E[:, h:h + 2, off:off + w], ALU.add).then_inc(sem("vector_unit_free"), 1)
            dve.wait_ge(sem("vector_unit_free"), sent("vector_unit_free"))
            V.tensor_reduce(small[:, m:m + 2], SC[:, i % 3, :, 0:w], AX, ALU.max, negate=True).then_inc(sem("shifted"), 1)
            dve.wait_ge(sem("shifted"), sent("shifted"))

        def norm_scores(i):
            qb, k, gp, br = step(i)
            w, h, m = P * (qb + 1), 4 * k + 2 * gp, 128 + 8 * (i % 3)
            gates = GTOK[:, qb, :].rearrange("p (h c) -> p h c", c=3)
            dve.wait_ge(sem("exped"), due("exped"))
            V.reciprocal(small[:, m + 4:m + 6], small[:, m + 2:m + 4]).then_inc(sem("vector_steps"), 1)
            dve.wait_ge(sem("vector_steps"), sent("vector_steps"))
            V.tensor_tensor(small[:, m + 4:m + 6], small[:, m + 4:m + 6], gates[:, h:h + 2, 1 + br], ALU.mult).then_inc(sem("vector_steps"), 1)
            dve.wait_ge(sem("vector_steps"), sent("vector_steps"))
            V.tensor_scalar(SC[:, i % 3, 0, 0:w], SC[:, i % 3, 0, 0:w], small[:, m + 4:m + 5], None, ALU.mult).then_inc(sem("vector_steps"), 1)
            V.tensor_scalar(SC[:, i % 3, 1, 0:w], SC[:, i % 3, 1, 0:w], small[:, m + 5:m + 6], None, ALU.mult).then_inc(sem("probs"), 1)
            dve.wait_ge(sem("vector_steps"), sent("vector_steps"))

        shift_compressed(0)
        shift_scores(0)
        norm_compressed(0)
        shift_scores(1)
        for i in range(STEPS):
            qb, k, gp, br = step(i)
            norm_scores(i)
            if i + 2 < STEPS:
                if (i + 2) % 8 == 0:
                    shift_compressed(qb + 1)
                shift_scores(i + 2)
                if (i + 2) % 8 == 0:
                    norm_compressed(qb + 1)
            dve.wait_ge(sem("vector_unit_ready"), due("vector_unit_ready"))
            u = next_unit()
            dst = CA[64 * k:64 * k + 64, 2 * gp:2 * gp + 2, qb * P:(qb + 1) * P]
            got = u[64 * k:64 * k + 64, 0:256].rearrange("p (a b) -> p a b", a=2)
            if br == 0:
                V.tensor_copy(dst, got).then_inc(sem("vector_unit_free"), 1)
                dve.wait_ge(sem("vector_unit_free"), sent("vector_unit_free"))
            else:
                V.tensor_tensor(dst, dst, got, ALU.add).then_inc(sem("vector_unit_free"), 1)
                dve.wait_ge(sem("vector_unit_free"), sent("vector_unit_free"))
        V.memset(QP[:, :, :], 0.0).then_inc(sem("vector_steps"), 1)
        dve.wait_ge(sem("vector_steps"), sent("vector_steps"))
        for k in range(2):
            for b in range(NB):
                V.tensor_copy(QP[64 * k:64 * k + 64, b, b * 8 + 4 * k:b * 8 + 4 * k + 4], Q[64 * k:64 * k + 64, :, S + b]).then_inc(sem("vector_steps"), 1)
                dve.wait_ge(sem("vector_steps"), sent("vector_steps"))
        dve.sem_inc(sem("qp_ready"), 1)
        dve.sem_inc(sem("attention_over"), 1)
        dve.wait_ge(sem("vector_unit_ready"), due("vector_unit_ready"))
        u = next_unit()
        V.tensor_reduce(small[0:64, 78:79], u[0:64, 0:64], AX, ALU.max).then_inc(sem("vector_steps"), 1)
        dve.wait_ge(sem("vector_steps"), sent("vector_steps"))
        V.tensor_scalar(SCM[:, 0, :], u[0:64, 0:64], small[0:64, 78:79], None, ALU.subtract).then_inc(sem("vector_unit_free"), 1)
        dve.wait_ge(sem("vector_unit_free"), sent("vector_unit_free"))
        dve.sem_inc(sem("cmp_s_shifted"), 1)
        dve.wait_ge(sem("cmp_s_exp"), due("cmp_s_exp"))
        dve.wait_ge(sem("gates_rows"), 16)
        V.reciprocal(small[0:64, 81:82], small[0:64, 80:81]).then_inc(sem("vector_steps"), 1)
        dve.wait_ge(sem("vector_steps"), sent("vector_steps"))
        V.tensor_scalar(SCM[:, 1, :], SCM[:, 0, :], small[0:64, 81:82], None, ALU.mult).then_inc(sem("vector_steps"), 1)
        dve.wait_ge(sem("vector_steps"), sent("vector_steps"))
        dve.sem_inc(sem("cmp_s"), 1)
        dve.wait_ge(sem("vector_unit_ready"), due("vector_unit_ready"))
        u = next_unit()
        V.memset(SCORE, 0.0).then_inc(sem("vector_steps"), 1)
        dve.wait_ge(sem("vector_steps"), sent("vector_steps"))
        V.tensor_copy(SCORE[:, 2, 0:32], u[0:16, 0:64:2]).then_inc(sem("vector_steps"), 1)
        dve.wait_ge(sem("vector_steps"), sent("vector_steps"))
        V.tensor_tensor(SCORE[:, 0, 0:32], SCORE[:, 2, 0:32], u[0:16, 1:64:2], ALU.add).then_inc(sem("vector_unit_free"), 1)
        dve.wait_ge(sem("vector_unit_free"), sent("vector_unit_free"))
        V.memset(SCORE[:, 0, 0:1], 1e4).then_inc(sem("vector_steps"), 1)
        dve.wait_ge(sem("vector_steps"), sent("vector_steps"))
        V.memset(SCORE[:, 0, 31:33], 1e4).then_inc(sem("vector_steps"), 1)
        dve.wait_ge(sem("vector_steps"), sent("vector_steps"))
        for r in range(2):
            V.max(TOP, SCORE[:, r, 0:33]).then_inc(sem("vector_steps"), 1)
            dve.wait_ge(sem("vector_steps"), sent("vector_steps"))
            V.match_replace(SCORE[:, r + 1, 0:33], TOP, SCORE[:, r, 0:33], -2.0).then_inc(sem("vector_steps"), 1)
            dve.wait_ge(sem("vector_steps"), sent("vector_steps"))
        V.tensor_scalar(SELN[:, 0:33], SCORE[:, 2, 0:33], -1.5, NEG, ALU.is_gt, ALU.mult).then_inc(sem("vector_steps"), 1)
        dve.wait_ge(sem("vector_steps"), sent("vector_steps"))
        dve.sem_inc(sem("sel_mask"), 1)
        for i in range(2):
            V.tensor_scalar(SCM[:, i, :], SCM[:, 1, :], SG[:, 0:1], rowok[0:64, 1 + i:2 + i], ALU.mult, ALU.mult).then_inc(sem("vector_steps"), 1)
            dve.wait_ge(sem("vector_steps"), sent("vector_steps"))
        dve.wait_ge(sem("win_scores"), due("win_scores"))
        V.memset(SW[:, 0:1], NEG).then_inc(sem("vector_steps"), 1)
        dve.wait_ge(sem("vector_steps"), sent("vector_steps"))
        V.tensor_reduce(small[0:64, 82:83], SW, AX, ALU.max, negate=True).then_inc(sem("vector_steps"), 1)
        dve.wait_ge(sem("vector_steps"), sent("vector_steps"))
        dve.sem_inc(sem("win_shift"), 1)
        dve.wait_ge(sem("win_exp"), due("win_exp"))
        V.reciprocal(small[0:64, 86:87], small[0:64, 83:84]).then_inc(sem("vector_steps"), 1)
        dve.wait_ge(sem("vector_steps"), sent("vector_steps"))
        V.tensor_scalar(SW, SW, small[0:64, 86:87], SG[:, 2:3], ALU.mult, ALU.mult).then_inc(sem("vector_steps"), 1)
        dve.wait_ge(sem("vector_steps"), sent("vector_steps"))
        V.tensor_scalar(NEWP[:, 1, :], own[:, :], SW[:, S:S + 1], None, ALU.mult).then_inc(sem("vector_steps"), 1)
        dve.wait_ge(sem("vector_steps"), sent("vector_steps"))
        for i in range(2):
            dve.wait_ge(sem("vector_unit_ready"), due("vector_unit_ready"))
            u = next_unit()
            V.tensor_copy(SS[:, i * 1024:(i + 1) * 1024], u[0:64, :]).then_inc(sem("vector_unit_free"), 1)
            dve.wait_ge(sem("vector_unit_free"), sent("vector_unit_free"))
        V.tensor_reduce(small[0:64, 84:85], SS, AX, ALU.max, negate=True).then_inc(sem("vector_steps"), 1)
        dve.wait_ge(sem("vector_steps"), sent("vector_steps"))
        dve.sem_inc(sem("sel_shift"), 1)
        dve.wait_ge(sem("sel_exp"), due("sel_exp"))
        V.reciprocal(small[0:64, 87:88], small[0:64, 85:86]).then_inc(sem("vector_steps"), 1)
        dve.wait_ge(sem("vector_steps"), sent("vector_steps"))
        V.tensor_scalar(SS, SS, small[0:64, 87:88], SG[:, 1:2], ALU.mult, ALU.mult).then_inc(sem("vector_steps"), 1)
        dve.wait_ge(sem("vector_steps"), sent("vector_steps"))
        V.tensor_scalar(NEWP[:, 0, :], own[:, :], SS[:, PAST:PAST + 1], None, ALU.mult).then_inc(sem("vector_steps"), 1)
        dve.wait_ge(sem("vector_steps"), sent("vector_steps"))
        dve.sem_inc(sem("sel_probs"), 1)
        dve.sem_inc(sem("win_probs"), 1)
        dve.wait_ge(sem("vector_unit_ready"), due("vector_unit_ready"))
        u = next_unit()
        for k in range(2):
            dst = CA[64 * k:64 * k + 64, :, S:T].rearrange("p g b -> p b g")
            got = [u[64 * k:64 * k + 64, lo:lo + 64].rearrange("p (b k g) -> p b k g", k=2, g=4)[:, :, k, :] for lo in (0, 512)]
            V.tensor_copy(dst, got[0]).then_inc(sem("vector_steps"), 1)
            dve.wait_ge(sem("vector_steps"), sent("vector_steps"))
            ins = V.tensor_tensor(dst, dst, got[1], ALU.add)
            if k == 0:
                ins.then_inc(sem("vector_steps"), 1)
                dve.wait_ge(sem("vector_steps"), sent("vector_steps"))
            else:
                ins.then_inc(sem("vector_unit_free"), 1)
                dve.wait_ge(sem("vector_unit_free"), sent("vector_unit_free"))
        in_parts(H, slice(4, 8), CA)
        dve.sem_inc(sem("mix_ready"), 1)
        add_residual()
        dve.sem_inc(sem("mixer_over"), 1)

        def cross(l):
            dve.wait_ge(sem("mem_in"), 16 * (l + 1))
            norm(MX, MH, f"mem{l}", MEM)
            for c in range(4):
                split_weights()
            norm(X, H, f"x{l}")
            split_weights()
            split_weights()
            def shift_scores(qb):
                dve.wait_ge(sem("vector_unit_ready"), due("vector_unit_ready"))
                u = next_unit()
                V.tensor_copy(XP[:, qb % 2].rearrange("p a b -> p (a b)"), u[:, :]).then_inc(sem("vector_unit_free"), 1)
                dve.wait_ge(sem("vector_unit_free"), sent("vector_unit_free"))
                m = 128 + 8 * (qb % 2)
                V.tensor_reduce(small[:, m:m + 4], XP[:, qb % 2], AX, ALU.max, negate=True).then_inc(sem("xmax"), 1)
                dve.wait_ge(sem("xmax"), sent("xmax"))

            shift_scores(0)
            for qb in range(QB):
                if qb + 1 < QB:
                    shift_scores(qb + 1)
                m = 132 + 8 * (qb % 2)
                dve.wait_ge(sem("xexp"), due("xexp"))
                V.reciprocal(small[:, m:m + 4], small[:, m:m + 4]).then_inc(sem("vector_steps"), 1)
                dve.wait_ge(sem("vector_steps"), sent("vector_steps"))
                V.tensor_tensor(XP[:, qb % 2], XP[:, qb % 2], small[:, m:m + 4].rearrange("p (a b) -> p a b", b=1).broadcast_to([P, 4, MEM]), ALU.mult).then_inc(sem("xprobs"), 1)
                dve.wait_ge(sem("xprobs"), sent("xprobs"))
                dve.wait_ge(sem("vector_unit_ready"), due("vector_unit_ready"))
                u = next_unit()
                got = u[:, :].rearrange("p (a b) -> p a b", a=8)
                V.tensor_copy(AO[:, 0, :, qb * P:(qb + 1) * P], got).then_inc(sem("vector_steps"), 1)
                dve.wait_ge(sem("vector_steps"), sent("vector_steps"))
                V.tensor_tensor(AO[:, 1, :, qb * P:(qb + 1) * P].bitcast(F16), got, AO[:, 0, :, qb * P:(qb + 1) * P], ALU.subtract).then_inc(sem("vector_unit_free"), 1)
                dve.wait_ge(sem("vector_unit_free"), sent("vector_unit_free"))
            V.memset(QXP[:, :, :], 0.0).then_inc(sem("vector_steps"), 1)
            dve.wait_ge(sem("vector_steps"), sent("vector_steps"))
            dve.wait_ge(sem("qx_ready"), due("qx_ready"))
            for b in range(NB):
                for h in range(4):
                    ins = V.tensor_copy(QXP[:, b * DC + 2 * h:b * DC + 2 * h + 2, 4 * b + h], QX[:, 2 * h:2 * h + 2, S + b])
                    ins.then_inc(sem("vector_steps"), 1)
                    dve.wait_ge(sem("vector_steps"), sent("vector_steps"))
            dve.sem_inc(sem("qxp_ready"), 1)
            dve.wait_ge(sem("vector_unit_ready"), due("vector_unit_ready"))
            u = next_unit()
            V.tensor_copy(XS, u[0:32, 0:MEM]).then_inc(sem("vector_unit_free"), 1)
            dve.wait_ge(sem("vector_unit_free"), sent("vector_unit_free"))
            V.tensor_reduce(small[0:32, 104:105], XS, AX, ALU.max, negate=True).then_inc(sem("vector_steps"), 1)
            dve.wait_ge(sem("vector_steps"), sent("vector_steps"))
            dve.sem_inc(sem("xs_max"), 1)
            dve.wait_ge(sem("xs_exp"), due("xs_exp"))
            V.reciprocal(small[0:32, 105:106], small[0:32, 105:106]).then_inc(sem("vector_steps"), 1)
            dve.wait_ge(sem("vector_steps"), sent("vector_steps"))
            V.tensor_scalar(XS, XS, small[0:32, 105:106], None, ALU.mult).then_inc(sem("vector_steps"), 1)
            dve.wait_ge(sem("vector_steps"), sent("vector_steps"))
            dve.sem_inc(sem("xs_probs"), 1)
            dve.wait_ge(sem("vector_unit_ready"), due("vector_unit_ready"))
            u = next_unit()
            V.memset(XST[:, :, :], 0.0).then_inc(sem("vector_steps"), 1)
            dve.wait_ge(sem("vector_steps"), sent("vector_steps"))
            for b in range(NB):
                ins = V.tensor_copy(XST[:, 2 * b:2 * b + 2, 4 * b:4 * b + 4], u[:, 0:64].rearrange("p (t r) -> p t r", t=2)[:, :, 4 * b:4 * b + 4])
                if b < NB - 1:
                    ins.then_inc(sem("vector_steps"), 1)
                    dve.wait_ge(sem("vector_steps"), sent("vector_steps"))
            ins.then_inc(sem("vector_unit_free"), 1)
            dve.wait_ge(sem("vector_unit_free"), sent("vector_unit_free"))
            dve.sem_inc(sem("xs_T"), 1)
            dve.wait_ge(sem("vector_unit_ready"), due("vector_unit_ready"))
            u = next_unit()
            V.tensor_copy(XO, u[0:32, :]).then_inc(sem("vector_unit_free"), 1)
            dve.wait_ge(sem("vector_unit_free"), sent("vector_unit_free"))
            dve.sem_inc(sem("xo_ready"), 1)
            dve.wait_ge(sem("vector_unit_ready"), due("vector_unit_ready"))
            u = next_unit()
            for h in range(4):
                got = u[:, 64 * h:64 * h + 64].rearrange("p (c b k) -> p c b k", c=2, b=NB)[:, :, :, h]
                V.tensor_copy(AO[:, 0, 2 * h:2 * h + 2, S:T], got).then_inc(sem("vector_steps"), 1)
                dve.wait_ge(sem("vector_steps"), sent("vector_steps"))
                ins = V.tensor_tensor(AO[:, 1, 2 * h:2 * h + 2, S:T].bitcast(F16), got, AO[:, 0, 2 * h:2 * h + 2, S:T], ALU.subtract)
                if h < 3:
                    ins.then_inc(sem("vector_steps"), 1)
                    dve.wait_ge(sem("vector_steps"), sent("vector_steps"))
            ins.then_inc(sem("vector_unit_free"), 1)
            dve.wait_ge(sem("vector_unit_free"), sent("vector_unit_free"))
            dve.wait_ge(sem("mkv_out"), due("mkv_out"))
            dve.sem_inc(sem("ao_ready"), 1)
            add_residual()
            norm(X, H, f"ffn{l}", tmp=HF if l else None)

        def up(chunks, dst):
            for c in range(chunks):
                if c % 2 == 0:
                    split_weights()
                dve.wait_ge(sem("gate_parts"), due("gate_parts"))
                dve.wait_ge(sem("vector_unit_ready"), due("vector_unit_ready"))
                u = next_unit()
                V.tensor_tensor(split(sq[:, c % 2, :]), split(sq[:, c % 2, :]), halves(u), ALU.mult).then_inc(sem("vector_unit_free"), 1)
                dve.wait_ge(sem("vector_unit_free"), sent("vector_unit_free"))
                in_parts(dst, c, sq[:, c % 2, :])
                dve.sem_inc(sem("gate_used"), 1)
            dve.sem_inc(sem("hidden"), 1)

        cross(0)
        up(DFF_C, HID)
        add_residual(1)
        dve.sem_inc(sem("ffn_over"), 1)

        norm(X, H, "mix1")
        split_weights()
        dve.wait_ge(sem("gates_raw"), due("gates_raw"))
        ig, lf, e_, u_, l_, x_ = (FM[0:4, i, :] for i in range(6))
        V.tensor_scalar(u_, lf, -1.0, None, ALU.mult).then_inc(sem("vector_steps"), 1)
        dve.wait_ge(sem("vector_steps"), sent("vector_steps"))
        V.tensor_tensor(e_, lf, u_, ALU.max).then_inc(sem("vector_steps"), 1)
        dve.wait_ge(sem("vector_steps"), sent("vector_steps"))
        dve.sem_inc(sem("gate_abs"), 1)
        dve.wait_ge(sem("gate_exp"), due("gate_exp"))
        V.tensor_scalar(u_, e_, 1.0, None, ALU.add).then_inc(sem("vector_steps"), 1)
        dve.wait_ge(sem("vector_steps"), sent("vector_steps"))
        dve.sem_inc(sem("gate_one"), 1)
        V.tensor_scalar(x_, u_, -1.0, None, ALU.add).then_inc(sem("vector_steps"), 1)
        dve.wait_ge(sem("vector_steps"), sent("vector_steps"))
        V.tensor_tensor(e_, e_, x_, ALU.subtract).then_inc(sem("vector_steps"), 1)
        dve.wait_ge(sem("vector_steps"), sent("vector_steps"))
        dve.wait_ge(sem("gate_ln"), due("gate_ln"))
        V.reciprocal(x_, u_).then_inc(sem("vector_steps"), 1)
        dve.wait_ge(sem("vector_steps"), sent("vector_steps"))
        V.tensor_tensor(e_, e_, x_, ALU.mult).then_inc(sem("vector_steps"), 1)
        dve.wait_ge(sem("vector_steps"), sent("vector_steps"))
        V.tensor_tensor(l_, l_, e_, ALU.add).then_inc(sem("vector_steps"), 1)
        dve.wait_ge(sem("vector_steps"), sent("vector_steps"))
        V.tensor_scalar(lf, lf, 0.0, None, ALU.min).then_inc(sem("vector_steps"), 1)
        dve.wait_ge(sem("vector_steps"), sent("vector_steps"))
        V.tensor_tensor(lf, lf, l_, ALU.subtract).then_inc(sem("vector_steps"), 1)
        dve.wait_ge(sem("vector_steps"), sent("vector_steps"))
        V.memset(x_[:, 0:S], 0.0).then_inc(sem("vector_steps"), 1)
        dve.wait_ge(sem("vector_steps"), sent("vector_steps"))
        V.tensor_tensor_scan(l_[:, 0:S], lf[:, 0:S], x_[:, 0:S], 0.0, ALU.add, ALU.add).then_inc(sem("vector_steps"), 1)
        dve.wait_ge(sem("vector_steps"), sent("vector_steps"))
        V.tensor_tensor(e_[:, 0:S], ig[:, 0:S], l_[:, 0:S], ALU.subtract).then_inc(sem("vector_steps"), 1)
        dve.wait_ge(sem("vector_steps"), sent("vector_steps"))
        V.tensor_tensor_scan(u_[:, 0:S], e_[:, 0:S], x_[:, 0:S], NEG, ALU.max, ALU.add).then_inc(sem("vector_steps"), 1)
        dve.wait_ge(sem("vector_steps"), sent("vector_steps"))
        V.tensor_tensor(l_[:, 0:S], l_[:, 0:S], u_[:, 0:S], ALU.add).then_inc(sem("vector_steps"), 1)
        dve.wait_ge(sem("vector_steps"), sent("vector_steps"))
        V.tensor_copy(MMP[0:4, 0:1], l_[:, S - 1:S]).then_inc(sem("vector_steps"), 1)
        dve.wait_ge(sem("vector_steps"), sent("vector_steps"))
        dve.sem_inc(sem("gate_m"), 1)
        dve.wait_ge(sem("gate_rows_exp"), due("gate_rows_exp"))
        dve.wait_ge(sem("state_in"), 32)
        dve.sem_inc(sem("gate_rows"), 1)
        for h in range(NH):
            split_weights()
            split_weights()
            if h == 0:
                dve.wait_ge(sem("gc_ready"), due("gc_ready"))
            dve.wait_ge(sem("head_ready_v"), due("head_ready_v"))
            dve.wait_ge(sem("tok_head"), due("tok_head"))
            dve.wait_ge(sem("vector_unit_ready"), due("vector_unit_ready"))
            u = next_unit()
            V.tensor_copy(MB, u[:, 0:S]).then_inc(sem("vector_steps"), 1)
            dve.wait_ge(sem("vector_steps"), sent("vector_steps"))
            V.tensor_copy(GS[:, 0:2, :].rearrange("p a b -> p (a b)"), u[:, S:S + 16]).then_inc(sem("vector_unit_free"), 1)
            dve.wait_ge(sem("vector_unit_free"), sent("vector_unit_free"))
            for sb_ in range(QB):
                w = S - sb_ * P
                V.tensor_scalar(WRAW[:, 0:w], MB[:, sb_ * P:S], GC[:, sb_, h:h + 1], -1.0, ALU.subtract, ALU.mult).then_inc(sem("vector_steps"), 1)
                dve.wait_ge(sem("vector_steps"), sent("vector_steps"))
                V.tensor_scalar(WRAW[:, 0:w], WRAW[:, 0:w], 0.0, None, ALU.min).then_inc(sem("vector_steps"), 1)
                dve.wait_ge(sem("vector_steps"), sent("vector_steps"))
                dve.sem_inc(sem("w_arg"), 1)
                dve.wait_ge(sem("w_exp"), due("w_exp"))
                V.tensor_tensor(WRAW[:, 0:P], WRAW[:, 0:P], tri[:, :], ALU.mult).then_inc(sem("vector_steps"), 1)
                dve.wait_ge(sem("vector_steps"), sent("vector_steps"))
                dve.wait_ge(sem("vector_unit_ready"), due("vector_unit_ready"))
                u = next_unit()
                V.tensor_tensor(ST[:, sb_, sb_ * P:S], WRAW[:, 0:w], u[:, 0:w], ALU.mult).then_inc(sem("vector_unit_free"), 1)
                dve.wait_ge(sem("vector_unit_free"), sent("vector_unit_free"))
            dve.sem_inc(sem("st_ready"), 1)
            V.tensor_scalar(SM[:, 0:4], GC[:, :, h], MB[:, S - 1:S], None, ALU.subtract).then_inc(sem("vector_steps"), 1)
            dve.wait_ge(sem("vector_steps"), sent("vector_steps"))
            dve.sem_inc(sem("sm_arg"), 1)
            dve.wait_ge(sem("sm_exp"), due("sm_exp"))
            for g in range(QB):
                V.tensor_scalar(VW[:, g, :], VTK[:, g, :], SM[:, g:g + 1], None, ALU.mult).then_inc(sem("vector_steps"), 1)
                dve.wait_ge(sem("vector_steps"), sent("vector_steps"))
            dve.sem_inc(sem("vw_ready"), 1)
            gi, gf, inter, mt = (GS[:, i, :] for i in range(4))
            V.tensor_tensor(inter, gf, ML[:, :].rearrange("p (b h) -> p b h", h=NH)[:, :, h], ALU.add).then_inc(sem("vector_steps"), 1)
            dve.wait_ge(sem("vector_steps"), sent("vector_steps"))
            V.tensor_tensor(mt, inter, gi, ALU.max).then_inc(sem("vector_steps"), 1)
            dve.wait_ge(sem("vector_steps"), sent("vector_steps"))
            V.tensor_copy(SMO[:, h * NB:(h + 1) * NB], mt).then_inc(sem("vector_steps"), 1)
            dve.wait_ge(sem("vector_steps"), sent("vector_steps"))
            V.tensor_tensor(SM[:, 8:16], inter, mt, ALU.subtract).then_inc(sem("vector_steps"), 1)
            dve.wait_ge(sem("vector_steps"), sent("vector_steps"))
            V.tensor_tensor(SM[:, 16:24], gi, mt, ALU.subtract).then_inc(sem("vector_steps"), 1)
            dve.wait_ge(sem("vector_steps"), sent("vector_steps"))
            V.tensor_scalar(SM[:, 24:32], mt, -1.0, None, ALU.mult).then_inc(sem("vector_steps"), 1)
            dve.wait_ge(sem("vector_steps"), sent("vector_steps"))
            dve.sem_inc(sem("gs_arg"), 1)
            dve.wait_ge(sem("gs_exp"), due("gs_exp"))
            for part in range(2):
                dve.wait_ge(sem("vector_unit_ready"), due("vector_unit_ready"))
                u = next_unit()
                V.tensor_copy(HH[:, part, 0:S], u[:, 0:S]).then_inc(sem("vector_unit_free"), 1)
                dve.wait_ge(sem("vector_unit_free"), sent("vector_unit_free"))
            dve.wait_ge(sem("vector_unit_ready"), due("vector_unit_ready"))
            u = next_unit()
            V.tensor_scalar(DEN[:, 0:S], u[:, 0:S], -1.0, None, ALU.mult).then_inc(sem("vector_steps"), 1)
            dve.wait_ge(sem("vector_steps"), sent("vector_steps"))
            V.tensor_tensor(DEN[:, 0:S], DEN[:, 0:S], u[:, 0:S], ALU.max).then_inc(sem("vector_unit_free"), 1)
            dve.wait_ge(sem("vector_unit_free"), sent("vector_unit_free"))
            dve.wait_ge(sem("vector_unit_ready"), due("vector_unit_ready"))
            u = next_unit()
            V.tensor_tensor(DEN[:, 0:S], DEN[:, 0:S], u[:, 0:S], ALU.max).then_inc(sem("vector_unit_free"), 1)
            dve.wait_ge(sem("vector_unit_free"), sent("vector_unit_free"))
            V.reciprocal(DEN[:, 0:S], DEN[:, 0:S]).then_inc(sem("vector_steps"), 1)
            dve.wait_ge(sem("vector_steps"), sent("vector_steps"))
            decay, inp = SM[:, 8:16], SM[:, 16:24]
            for c in range(2):
                V.tensor_tensor(SN[:, h, c, :], SN[:, h, c, :], decay, ALU.mult).then_inc(sem("vector_steps"), 1)
                dve.wait_ge(sem("vector_steps"), sent("vector_steps"))
                V.tensor_tensor(PRD[:, c, :], HK[:, c, S:T], inp, ALU.mult).then_inc(sem("vector_steps"), 1)
                dve.wait_ge(sem("vector_steps"), sent("vector_steps"))
                V.tensor_tensor(SN[:, h, c, :], SN[:, h, c, :], PRD[:, c, :], ALU.add).then_inc(sem("vector_steps"), 1)
                dve.wait_ge(sem("vector_steps"), sent("vector_steps"))
                V.tensor_tensor(HH[:, c, S:T], HV[:, c, S:T], inp, ALU.mult).then_inc(sem("vector_steps"), 1)
                dve.wait_ge(sem("vector_steps"), sent("vector_steps"))
            for half in range(2):
                dve.wait_ge(sem("vector_unit_ready"), due("vector_unit_ready"))
                u = next_unit()
                if half == 0:
                    dve.wait_ge(sem("c_decayed"), due("c_decayed", 2 * NB))
                for b in range(4):
                    for vc in range(2):
                        bb = half * 4 + b
                        cs = CS[:, vc * NB + bb, :]
                        ins = V.scalar_tensor_tensor(cs, u[:, b * 256:(b + 1) * 256], HH[:, vc, S + bb:S + bb + 1], cs, ALU.mult, ALU.add)
                        if (b, vc) != (3, 1):
                            ins.then_inc(sem("vector_steps"), 1)
                            sent("vector_steps")
                        else:
                            dve.wait_ge(sem("vector_steps"), sent("vector_steps", 0))
                            ins.then_inc(sem("vector_unit_free"), 1)
                            dve.wait_ge(sem("vector_unit_free"), sent("vector_unit_free"))
            for half in range(2):
                dve.wait_ge(sem("vector_unit_ready"), due("vector_unit_ready"))
                u = next_unit()
                product = sq[:, :, :].rearrange("p a b -> p (a b)")[:, 0:1024].rearrange("p (a b) -> p a b", a=4)
                for vc in range(2):
                    lo = half * 4
                    ins = V.tensor_tensor(product, CS[:, vc * NB + lo:vc * NB + lo + 4, :], u[:, :].rearrange("p (a b) -> p a b", a=4), ALU.mult)
                    if vc == 0:
                        ins.then_inc(sem("vector_steps"), 1)
                        dve.wait_ge(sem("vector_steps"), sent("vector_steps"))
                    else:
                        ins.then_inc(sem("vector_unit_free"), 1)
                        dve.wait_ge(sem("vector_unit_free"), sent("vector_unit_free"))
                    V.tensor_reduce(HH[:, vc, S + lo:S + lo + 4], product, AX, ALU.add).then_inc(sem("vector_steps"), 1)
                    dve.wait_ge(sem("vector_steps"), sent("vector_steps"))
            dve.sem_inc(sem("c_sample_done"), 1)
            for c in range(2):
                V.tensor_tensor(PRD[:, c, :], SN[:, h, c, :], HQ[:, c, S:T], ALU.mult).then_inc(sem("vector_steps"), 1)
                dve.wait_ge(sem("vector_steps"), sent("vector_steps"))
            dve.sem_inc(sem("nq_ready"), 1)
            dve.wait_ge(sem("vector_unit_ready"), due("vector_unit_ready"))
            u = next_unit()
            V.tensor_scalar(DEN[:, S:T], u[:, 0:NB], -1.0, None, ALU.mult).then_inc(sem("vector_steps"), 1)
            dve.wait_ge(sem("vector_steps"), sent("vector_steps"))
            V.tensor_tensor(DEN[:, S:T], DEN[:, S:T], u[:, 0:NB], ALU.max).then_inc(sem("vector_unit_free"), 1)
            dve.wait_ge(sem("vector_unit_free"), sent("vector_unit_free"))
            V.tensor_tensor(DEN[:, S:T], DEN[:, S:T], SM[:, 24:32], ALU.max).then_inc(sem("vector_steps"), 1)
            dve.wait_ge(sem("vector_steps"), sent("vector_steps"))
            V.reciprocal(DEN[:, S:T], DEN[:, S:T]).then_inc(sem("vector_steps"), 1)
            dve.wait_ge(sem("vector_steps"), sent("vector_steps"))
            for c in range(2):
                V.tensor_tensor(HH[:, c, :], HH[:, c, :], DEN[:, :], ALU.mult).then_inc(sem("vector_steps"), 1)
                dve.wait_ge(sem("vector_steps"), sent("vector_steps"))
            dve.sem_inc(sem("head_h"), 1)
            dve.wait_ge(sem("vector_unit_ready"), due("vector_unit_ready"))
            u = next_unit()
            V.tensor_scalar(split(inv[:, :]), halves(u), 1.0 / 256, 1e-6, ALU.mult, ALU.add).then_inc(sem("vector_unit_free"), 1)
            dve.wait_ge(sem("vector_unit_free"), sent("vector_unit_free"))
            dve.sem_inc(sem("mean_copied"), 1)
            dve.wait_ge(sem("root"), due("root"))
            V.reciprocal(inv[:, :], inv[:, :]).then_inc(sem("vector_steps"), 1)
            dve.wait_ge(sem("vector_steps"), sent("vector_steps"))
            for c in range(2):
                V.scalar_tensor_tensor(HH[:, c, :], HH[:, c, :], col("mnorm", 2 * h + c), inv[:, :], ALU.mult, ALU.mult).then_inc(sem("vector_steps"), 1)
                dve.wait_ge(sem("vector_steps"), sent("vector_steps"))
                V.tensor_tensor(HH[:, c, :], HH[:, c, :], HO[:, c, :], ALU.mult).then_inc(sem("vector_steps"), 1)
                dve.wait_ge(sem("vector_steps"), sent("vector_steps"))
                in_parts(MIX, 2 * h + c, HH[:, c, :])
            dve.sem_inc(sem("head_over"), 1)
        dve.sem_inc(sem("mix_ready"), 1)
        add_residual()
        dve.wait_ge(sem("states_out"), due("states_out"))
        dve.sem_inc(sem("mixer_over"), 1)
        cross(1)

        dve.wait_ge(sem("vector_unit_ready"), due("vector_unit_ready"))
        u = next_unit()
        for t in range(TBN):
            ins = V.tensor_tensor(LOG[0:TB, t, :], u[0:TB, t * 8:t * 8 + 8], rb[0:TB, :], ALU.add)
            if t < TBN - 1:
                ins.then_inc(sem("vector_steps"), 1)
                dve.wait_ge(sem("vector_steps"), sent("vector_steps"))
            else:
                ins.then_inc(sem("vector_unit_free"), 1)
                dve.wait_ge(sem("vector_unit_free"), sent("vector_unit_free"))
        for t in range(TBN):
            V.max(TOP8[0:TB, t, :], LOG[0:TB, t, :]).then_inc(sem("vector_steps"), 1)
            dve.wait_ge(sem("vector_steps"), sent("vector_steps"))
            V.max_index(IDX[0:TB, t, :].bitcast(U32), TOP8[0:TB, t, :], LOG[0:TB, t, :]).then_inc(sem("vector_steps"), 1)
            dve.wait_ge(sem("vector_steps"), sent("vector_steps"))
        V.tensor_copy(IDXF[0:TB, :, :], IDX[0:TB, :, :].bitcast(U32)).then_inc(sem("vector_steps"), 1)
        dve.wait_ge(sem("vector_steps"), sent("vector_steps"))
        V.tensor_tensor(LOG[0:TB, :, 0], TOP8[0:TB, :, 1], TOP8[0:TB, :, 0], ALU.subtract).then_inc(sem("vector_steps"), 1)
        dve.wait_ge(sem("vector_steps"), sent("vector_steps"))
        dve.sem_inc(sem("router_max"), 1)
        dve.wait_ge(sem("router_exp"), due("router_exp"))
        V.tensor_scalar(LOG[0:TB, :, 1], LOG[0:TB, :, 0], 1.0, None, ALU.add).then_inc(sem("vector_steps"), 1)
        dve.wait_ge(sem("vector_steps"), sent("vector_steps"))
        V.reciprocal(LOG[0:TB, :, 1], LOG[0:TB, :, 1]).then_inc(sem("vector_steps"), 1)
        dve.wait_ge(sem("vector_steps"), sent("vector_steps"))
        V.tensor_tensor(LOG[0:TB, :, 2], LOG[0:TB, :, 0], LOG[0:TB, :, 1], ALU.mult).then_inc(sem("vector_steps"), 1)
        dve.wait_ge(sem("vector_steps"), sent("vector_steps"))
        for t in range(TBN):
            for i in range(2):
                dst = CMB[0:TB, t, :] if i == 0 else TOP8[0:TB, t, :]
                V.tensor_scalar(dst, experts_iota[0:TB, :], IDXF[0:TB, t, i:i + 1], LOG[0:TB, t, 1 + i:2 + i], ALU.is_equal, ALU.mult).then_inc(sem("vector_steps"), 1)
                dve.wait_ge(sem("vector_steps"), sent("vector_steps"))
            V.tensor_tensor(CMB[0:TB, t, :], CMB[0:TB, t, :], TOP8[0:TB, t, :], ALU.add).then_inc(sem("vector_steps"), 1)
            dve.wait_ge(sem("vector_steps"), sent("vector_steps"))
        dve.sem_inc(sem("comb_ready"), 1)
        dve.wait_ge(sem("comb_bcast"), due("comb_bcast"))
        for e in range(NE):
            up(EXP_C, HIDE)
            for c in range(DC):
                if c % 2 == 0:
                    split_weights()
                dve.wait_ge(sem("vector_unit_ready"), due("vector_unit_ready"))
                u = next_unit()
                V.tensor_tensor(split(YT), split(COMB[:, e, :]), halves(u), ALU.mult).then_inc(sem("vector_unit_free"), 1)
                dve.wait_ge(sem("vector_unit_free"), sent("vector_unit_free"))
                V.tensor_tensor(X[:, c, :], X[:, c, :], YT, ALU.add).then_inc(sem("vector_steps"), 1)
                dve.wait_ge(sem("vector_steps"), sent("vector_steps"))
        dve.sem_inc(sem("residual"), 1)
        dve.wait_ge(sem("vector_unit_ready"), due("vector_unit_ready"))
        u = next_unit()
        V.tensor_scalar(split(inv[:, :]), halves(u), 1.0 / D, 1e-6, ALU.mult, ALU.add).then_inc(sem("vector_unit_free"), 1)
        dve.wait_ge(sem("vector_unit_free"), sent("vector_unit_free"))
        dve.sem_inc(sem("mean_copied"), 1)
        dve.wait_ge(sem("root"), due("root"))
        V.reciprocal(inv[:, :], inv[:, :]).then_inc(sem("vector_steps"), 1)
        dve.wait_ge(sem("vector_steps"), sent("vector_steps"))
        for k in range(DC):
            V.scalar_tensor_tensor(X[:, k, :], X[:, k, :], col("final", k), inv[:, :], ALU.mult, ALU.mult).then_inc(sem("vector_steps"), 1)
            dve.wait_ge(sem("vector_steps"), sent("vector_steps"))
        dve.sem_inc(sem("y_done"), 1)


OUTS = {
    "y": (P, DC, T), "conv_p": (P, CONV_C, CONV_W - 1), "conv_s": (P, CONV_C, NB, CONV_W - 1), "kv": (P, 6, T),
    "win_k_s": (NB, P, S), "win_v_s": (NB, S, P), "c_p": (NH, 2, P, 256), "c_s": (NH, P, 2 * NB, 256),
    "n_p": (P, NH, 2), "n_s": (P, NH, 2, NB), "m_p": (4, 1), "m_s": (1, NH * NB), "mem_kv": (2, P, 16, MEM),
}


def kernel(**inputs):
    import concourse.bacc as _bacc
    from concourse.bass_utils import run_bass_kernel_spmd as _run

    a = {n: np.asarray(v) for n, v in inputs.items()}
    A = np.ascontiguousarray

    def feats(v):
        return A(v.T.reshape(-1, P, v.shape[0]).transpose(1, 0, 2))

    def cols(v):
        return v.reshape(-1, P).T

    def tiles(w):
        k, n = w.shape
        return A(w.reshape(k // P, P, n // P, P).transpose(2, 1, 0, 3).reshape(n // P, P, k))

    g = {}
    g["xT"] = feats(np.concatenate([a["x_prompt"][0], a["x_sample"][:, 0]], 0))
    g["memT"] = feats(a["mem_prompt"][0])
    vec = np.zeros((P, VECW), np.float32)
    for name, v in [("mix0", a["norm_mix"][0]), ("mix1", a["norm_mix"][1]), ("x0", a["norm_xattn"][0]),
                    ("x1", a["norm_xattn"][1]), ("mem0", a["norm_mem"][0]), ("mem1", a["norm_mem"][1]),
                    ("ffn0", a["norm_ffn"][0]), ("ffn1", a["norm_ffn"][1]), ("final", a["norm_final"]),
                    ("conv_b", a["conv_b"][0]), ("ln_g", a["conv_ln_g"][0]), ("ln_b", a["conv_ln_b"][0]),
                    ("mnorm", a["mlstm_norm"][0])]:
        c = cols(v)
        vec[:, VEC[name]:VEC[name] + c.shape[1]] = c
    vec[:, VEC["conv_w"]:] = a["conv_w"][0].reshape(CONV_W, CONV_C, P).transpose(2, 1, 0).reshape(P, -1)
    g["vectors"] = vec
    w = a["w_in_even"][0]
    order = []
    for c in range(4):
        order += list(range(c * P, (c + 1) * P)) + list(range(512 + c * P, 512 + (c + 1) * P))
    for c in range(4):
        order += list(range(1024 + c * 64, 1088 + c * 64)) + list(range(1280 + c * 64, 1344 + c * 64))
    order += list(range(1536, 1536 + 768))
    w2 = np.zeros((D, 19 * P), np.float32)
    w2[:, :18 * P] = w[:, order]
    w2[:, 18 * P:18 * P + 24] = w[:, 2304:2328]
    g["w_in_even"] = tiles(w2)
    w = a["w_out_even"][0]
    b = w[512:].reshape(2, 4, 64, D).transpose(1, 0, 2, 3).reshape(512, D)
    g["w_out_even"] = tiles(np.concatenate([w[:512], b], 0))
    w = a["w_in_odd"][0]
    order = []
    for h in range(4):
        for part in range(4):
            order += list(range(part * D + h * 256, part * D + (h + 1) * 256))
    gt = np.zeros((D, P), np.float32)
    gt[:, 0:4] = w[:, 4096:4100]
    gt[:, 32:36] = w[:, 4100:4104]
    g["w_in_odd"] = tiles(np.concatenate([gt, w[:, order]], 1))
    g["w_out_odd"] = tiles(a["w_out_odd"][0])
    for n in ("xattn_wkv", "xattn_wq", "xattn_wo"):
        g[n] = np.stack([tiles(v) for v in a[n]])

    def pairs(w):
        f = w.shape[1] // 2
        v = w.reshape(w.shape[0], 2, f // P, P).transpose(0, 2, 1, 3).reshape(w.shape[0], 2 * f)
        return tiles(v)

    g["ffn_w_gu"] = pairs(a["ffn_w_gu"][0])
    g["ffn_w_dn"] = tiles(a["ffn_w_dn"][0])
    g["expert_w_gu"] = np.stack([pairs(v) for v in a["expert_w_gu"][0]])
    g["expert_w_dn"] = np.stack([tiles(v) for v in a["expert_w_dn"][0]])
    g["router_w"] = A(a["router_w"][0].reshape(DC, P, NE).transpose(1, 0, 2))
    g["router_b"] = A(np.broadcast_to(a["router_b"][0], (P, NE)))
    g["gate_b"] = A(np.stack([a["mlstm_b_i"][0], a["mlstm_b_f"][0]], 1))
    g["relx"] = np.tile(np.concatenate([a["rel_bias"], np.ones((1, 8), np.float32)], 0), (1, NB))
    pg = a["cache_nsa_pages"][0].reshape(-1, PAGE, 4, P)
    g["pages"] = A(np.concatenate([pg[:, :, 0].transpose(0, 2, 1), pg[:, :, 1].transpose(0, 2, 1),
                                   pg[:, :, 2].transpose(0, 2, 1), pg[:, :, 3]], 2))
    g["page_table"] = A(a["page_table"].reshape(1, -1)).astype(np.int32)
    wn = a["cache_nsa_window"][0].reshape(NB, S, 2, P)
    g["win_k"] = A(wn[:, :, 0].transpose(0, 2, 1))
    g["win_v"] = A(wn[:, :, 1])
    cw = np.zeros((P, 2, CMP, P), np.float32)
    for k in range(2):
        cw[64 * k:64 * k + 64, :, :, 64 * k:64 * k + 64] = a["nsa_cmp_w"][0].transpose(2, 0, 1, 3)
    g["cmp_w"] = cw
    pe = a["nsa_cmp_pe"][0].transpose(2, 0, 1)
    g["cmp_pe"] = A(np.concatenate([pe, pe], 0))
    g["cache_conv"] = A(a["cache_conv"][0].reshape(NB, CONV_W - 1, CONV_C, P).transpose(3, 2, 0, 1))
    g["state_c"] = A(a["state_mlstm_c"][0].reshape(NB, NH, 2, P, 256).transpose(1, 3, 2, 0, 4).reshape(NH, P, 2 * NB, 256))
    g["state_n"] = A(a["state_mlstm_n"][0].reshape(NB, NH, 2, P).transpose(3, 1, 2, 0))
    g["state_m"] = A(np.broadcast_to(a["state_mlstm_m"][0].reshape(1, -1), (P, NB * NH)))
    mk = a["cache_mem_kv"]
    kk = mk[:, :, :, 0].reshape(2, NB, MEM, 4, 2, P).transpose(0, 1, 5, 3, 4, 2).reshape(2, NB, P, 2048)
    vv = mk[:, :, :, 1].reshape(2, NB, 2, P, D).transpose(0, 1, 3, 2, 4).reshape(2, NB, P, 2048)
    g["mem_kv"] = np.stack([kk, vv], 1)
    g.update(constants())

    nc = _bacc.Bacc("TRN2", target_bir_lowering=False, num_devices=1)
    arrays, ins, outs = {}, {}, {}
    for name, v in g.items():
        arrays["in_" + name] = v
        ins[name] = nc.dram_tensor("in_" + name, v.shape, mybir.dt.from_np(v.dtype), kind="ExternalInput").ap()
    for name, shape in OUTS.items():
        outs[name] = nc.dram_tensor("out_" + name, shape, F32, kind="ExternalOutput").ap()
    program(nc, ins, outs)
    r = _run(nc, [arrays], core_ids=[0]).results[0]
    o = {name: np.asarray(r["out_" + name]) for name in OUTS}

    y = o["y"].transpose(2, 1, 0).reshape(T, D)
    kv = o["kv"].transpose(2, 1, 0)
    conv_p = o["conv_p"].transpose(2, 1, 0).reshape(1, 1, CONV_W - 1, 512)
    conv_s = o["conv_s"].transpose(2, 3, 1, 0).reshape(1, NB, CONV_W - 1, 512)
    nsa_p = kv[:S, :4].reshape(1, 1, S, 4, 2, 64)
    nsa_s = kv[S:, :4].reshape(1, NB, 1, 4, 2, 64)
    win_p = kv[:S, 4:].reshape(1, 1, S, 2, 2, 64)
    win_s = np.stack([o["win_k_s"].transpose(0, 2, 1), o["win_v_s"]], 2).reshape(1, NB, S, 2, 2, 64)
    c_p = o["c_p"].reshape(1, 1, NH, 256, 256)
    c_s = o["c_s"].reshape(NH, P, 2, NB, 256).transpose(3, 0, 2, 1, 4).reshape(1, NB, NH, 256, 256)
    n_p = o["n_p"].transpose(1, 2, 0).reshape(1, 1, NH, 256)
    n_s = o["n_s"].transpose(3, 1, 2, 0).reshape(1, NB, NH, 256)
    m_p = o["m_p"].reshape(1, 1, NH)
    m_s = o["m_s"].reshape(NH, NB).T.reshape(1, NB, NH)
    mkv = o["mem_kv"].transpose(0, 3, 2, 1).reshape(2, 1, MEM, 2, 4, 256)
    return tuple(A(v) for v in (y[:S].reshape(1, S, D), y[S:].reshape(NB, 1, D), conv_p, conv_s, nsa_p, nsa_s,
                                win_p, win_s, c_p, c_s, n_p, n_s, m_p, m_s, mkv))
```
